# Optimizing a Trainium2 kernel written in Bass

```python
import jax, jax.numpy as jnp
from jax import lax
import numpy as np

D_MODEL = 1024
BATCH = 1
SEQ = 1024
DEPTH = 1
DEC_BATCH = 8
DEC_SEQ = 4
PAST_LEN = 512
PAGE_SIZE = 128

N_HEADS_ATT = 8
HEAD_DIM = 64
D_ATT = N_HEADS_ATT * HEAD_DIM
D_CONV = D_MODEL - D_ATT
CONV_WIDTH = 31
Q_BLOCK = 128
D_IN = 3 * D_ATT + N_HEADS_ATT + 2 * D_CONV
PEER_HEADS = 8
PEER_N_KEYS = 128
PEER_N_EXPERTS = PEER_N_KEYS * PEER_N_KEYS
PEER_QUERY_DIM = 256
PEER_HALF = PEER_QUERY_DIM // 2
PEER_TOPK = 16
PEER_TOKEN_BLOCK = 128
EPS = 1e-6
FORGET_BIAS_INIT = 3.0

kernel_name = 'hymba_fox_conformer_peer_adaln_step'

def _rms(x, g):
    xf = x.astype(jnp.float32)
    y = xf * lax.rsqrt(jnp.mean(xf * xf, axis=-1, keepdims=True) + EPS)
    return (y * g.astype(jnp.float32)).astype(x.dtype)

def _adaln(c, w_ada, b_ada):
    mod = (c @ w_ada + b_ada)[:, None, :]
    return jnp.split(mod, 6, axis=-1)

def _modulate(h, shift, scale):
    return h * (1 + scale) + shift

def _in_proj(h, w_in, b_f, b_glu, q_norm_g, k_norm_g):
    n, t, _ = h.shape
    z = h @ w_in
    q, k, v, fg, glu = jnp.split(
        z, [D_ATT, 2 * D_ATT, 3 * D_ATT, 3 * D_ATT + N_HEADS_ATT], axis=-1)
    q = _rms(q.reshape(n, t, N_HEADS_ATT, HEAD_DIM), q_norm_g)
    k = _rms(k.reshape(n, t, N_HEADS_ATT, HEAD_DIM), k_norm_g)
    v = v.reshape(n, t, N_HEADS_ATT, HEAD_DIM)
    logf = jax.nn.log_sigmoid((fg + b_f).astype(jnp.float32))
    a, b = jnp.split(glu + b_glu, 2, axis=-1)
    u = a * jax.nn.sigmoid(b)
    return q, k, v, logf, u

def _attend(q, k, v, fq, fk, q_pos, k_pos):
    s = jnp.einsum('nqhd,nkhd->nhqk', q, k).astype(jnp.float32) * (HEAD_DIM ** -0.5)
    s = s + jnp.swapaxes(fq, 1, 2)[..., :, None] - jnp.swapaxes(fk, 1, 2)[..., None, :]
    mask = k_pos[None, :] <= q_pos[:, None]
    s = jnp.where(mask, s, -jnp.inf)
    p = jax.nn.softmax(s, axis=-1)
    return jnp.einsum('nhqk,nkhd->nqhd', p.astype(v.dtype), v)

def _prompt_attention(q, k, v, logf):
    n, t, h, d = q.shape
    nb = t // Q_BLOCK
    f_cum = jnp.cumsum(logf, axis=1)
    pos = jnp.arange(t)
    qb = jnp.moveaxis(q.reshape(n, nb, Q_BLOCK, h, d), 1, 0)
    fb = jnp.moveaxis(f_cum.reshape(n, nb, Q_BLOCK, h), 1, 0)
    pb = pos.reshape(nb, Q_BLOCK)
    out = lax.map(lambda a: _attend(a[0], k, v, a[1], f_cum, a[2], pos), (qb, fb, pb))
    return jnp.moveaxis(out, 0, 1).reshape(n, t, h * d)

def _sample_attention(q, k, v, logf, cache_k, cache_v, cache_logf, page_table):
    n, s = q.shape[:2]
    past = page_table.shape[1] * PAGE_SIZE
    kp = cache_k[page_table].reshape(n, past, N_HEADS_ATT, HEAD_DIM).astype(k.dtype)
    vp = cache_v[page_table].reshape(n, past, N_HEADS_ATT, HEAD_DIM).astype(v.dtype)
    lp = cache_logf[page_table].reshape(n, past, N_HEADS_ATT).astype(jnp.float32)
    k_all = jnp.concatenate([kp, k], axis=1)
    v_all = jnp.concatenate([vp, v], axis=1)
    f_cum = jnp.cumsum(jnp.concatenate([lp, logf], axis=1), axis=1)
    k_pos = jnp.arange(past + s)
    q_pos = past + jnp.arange(s)
    out = _attend(q, k_all, v_all, f_cum[:, past:], f_cum, q_pos, k_pos)
    return out.reshape(n, s, D_ATT)

def _conv_branch(u_ext, conv_w, conv_b, ln_g, ln_b):
    y = lax.conv_general_dilated(
        u_ext, conv_w[:, None, :].astype(u_ext.dtype), (1,), 'VALID',
        dimension_numbers=('NWC', 'WIO', 'NWC'), feature_group_count=D_CONV) + conv_b
    yf = y.astype(jnp.float32)
    mu = jnp.mean(yf, axis=-1, keepdims=True)
    var = jnp.mean(jnp.square(yf - mu), axis=-1, keepdims=True)
    yn = (yf - mu) * lax.rsqrt(var + EPS) * ln_g + ln_b
    return jax.nn.silu(yn).astype(u_ext.dtype)

def _peer(h, w_query, sub_keys, expert_u, expert_v):
    shape = h.shape
    hf = h.reshape(-1, D_MODEL)
    n = hf.shape[0]
    nb = -(-n // PEER_TOKEN_BLOCK)
    hf = jnp.pad(hf, ((0, nb * PEER_TOKEN_BLOCK - n), (0, 0))).reshape(nb, PEER_TOKEN_BLOCK, D_MODEL)

    def block(hb):
        q = (hb @ w_query).reshape(PEER_TOKEN_BLOCK, PEER_HEADS, 2, PEER_HALF)
        s = jnp.einsum('nhpd,hpkd->nhpk', q, sub_keys).astype(jnp.float32)
        s1, i1 = lax.top_k(s[:, :, 0], PEER_TOPK)
        s2, i2 = lax.top_k(s[:, :, 1], PEER_TOPK)
        cand = (s1[..., :, None] + s2[..., None, :]).reshape(PEER_TOKEN_BLOCK, PEER_HEADS, PEER_TOPK * PEER_TOPK)
        cidx = (i1[..., :, None] * PEER_N_KEYS + i2[..., None, :]).reshape(PEER_TOKEN_BLOCK, PEER_HEADS, PEER_TOPK * PEER_TOPK)
        top, sel = lax.top_k(cand, PEER_TOPK)
        eidx = jnp.take_along_axis(cidx, sel, axis=-1)
        g = jax.nn.softmax(top, axis=-1)
        act = jax.nn.gelu(jnp.einsum('nd,nhkd->nhk', hb, expert_u[eidx]).astype(jnp.float32), approximate=False)
        return jnp.einsum('nhk,nhkd->nd', (g * act).astype(hb.dtype), expert_v[eidx])

    out = lax.map(block, hf).reshape(nb * PEER_TOKEN_BLOCK, D_MODEL)[:n]
    return out.reshape(shape)

def _tail(x, attn_out, conv_out, gate1, shift2, scale2, gate2, w_o, norm2_g,
          w_query, sub_keys, expert_u, expert_v):
    x1 = x + gate1 * (jnp.concatenate([attn_out, conv_out], axis=-1) @ w_o)
    h2 = _modulate(_rms(x1, norm2_g), shift2, scale2)
    return x1 + gate2 * _peer(h2, w_query, sub_keys, expert_u, expert_v)

def setup_inputs(seed: int = 0) -> dict:
    key = jax.random.key(seed)
    ks = jax.random.split(key, 32)
    f32 = jnp.float32
    n_pages = PAST_LEN // PAGE_SIZE
    n_phys = (DEC_BATCH * n_pages * 5) // 4

    def nrm(k, shape, s):
        return s * jax.random.normal(k, shape, f32)

    page_table = jax.random.permutation(ks[0], n_phys)[: DEC_BATCH * n_pages]
    page_table = page_table.reshape(DEC_BATCH, n_pages).astype(jnp.int32)
    return {
        'x_prompt': nrm(ks[1], (BATCH, SEQ, D_MODEL), 1.0),
        'x_sample': nrm(ks[2], (DEC_BATCH, DEC_SEQ, D_MODEL), 1.0),
        'c_prompt': nrm(ks[3], (BATCH, D_MODEL), 1.0),
        'c_sample': nrm(ks[4], (DEC_BATCH, D_MODEL), 1.0),
        'cache_k': nrm(ks[5], (DEPTH, n_phys, PAGE_SIZE, N_HEADS_ATT, HEAD_DIM), 1.0),
        'cache_v': nrm(ks[6], (DEPTH, n_phys, PAGE_SIZE, N_HEADS_ATT, HEAD_DIM), 1.0),
        'cache_logf': jax.nn.log_sigmoid(FORGET_BIAS_INIT + nrm(ks[7], (DEPTH, n_phys, PAGE_SIZE, N_HEADS_ATT), 0.5)),
        'state_conv': nrm(ks[8], (DEPTH, DEC_BATCH, CONV_WIDTH - 1, D_CONV), 0.5),
        'page_table': page_table,
        'norm1_g': 1.0 + nrm(ks[9], (DEPTH, D_MODEL), 0.05),
        'norm2_g': 1.0 + nrm(ks[10], (DEPTH, D_MODEL), 0.05),
        'w_ada': nrm(ks[11], (DEPTH, D_MODEL, 6 * D_MODEL), 0.5 * D_MODEL ** -0.5),
        'b_ada': nrm(ks[12], (DEPTH, 6 * D_MODEL), 0.02),
        'w_in': nrm(ks[13], (DEPTH, D_MODEL, D_IN), D_MODEL ** -0.5),
        'b_f': FORGET_BIAS_INIT + nrm(ks[14], (DEPTH, N_HEADS_ATT), 0.5),
        'b_glu': nrm(ks[15], (DEPTH, 2 * D_CONV), 0.02),
        'q_norm_g': 1.0 + nrm(ks[16], (DEPTH, HEAD_DIM), 0.05),
        'k_norm_g': 1.0 + nrm(ks[17], (DEPTH, HEAD_DIM), 0.05),
        'conv_w': nrm(ks[18], (DEPTH, CONV_WIDTH, D_CONV), CONV_WIDTH ** -0.5),
        'conv_b': nrm(ks[19], (DEPTH, D_CONV), 0.02),
        'conv_ln_g': 1.0 + nrm(ks[20], (DEPTH, D_CONV), 0.05),
        'conv_ln_b': nrm(ks[21], (DEPTH, D_CONV), 0.02),
        'w_o': nrm(ks[22], (DEPTH, D_MODEL, D_MODEL), D_MODEL ** -0.5),
        'peer_w_query': nrm(ks[23], (DEPTH, D_MODEL, PEER_HEADS * PEER_QUERY_DIM), D_MODEL ** -0.5),
        'peer_sub_keys': nrm(ks[24], (DEPTH, PEER_HEADS, 2, PEER_N_KEYS, PEER_HALF), PEER_HALF ** -0.5),
        'peer_u': nrm(ks[25], (DEPTH, PEER_N_EXPERTS, D_MODEL), D_MODEL ** -0.5),
        'peer_v': nrm(ks[26], (DEPTH, PEER_N_EXPERTS, D_MODEL), PEER_HEADS ** -0.5),
    }

def reference(x_prompt, x_sample, c_prompt, c_sample, cache_k, cache_v, cache_logf,
              state_conv, page_table, norm1_g, norm2_g, w_ada, b_ada, w_in, b_f, b_glu,
              q_norm_g, k_norm_g, conv_w, conv_b, conv_ln_g, conv_ln_b, w_o,
              peer_w_query, peer_sub_keys, peer_u, peer_v):
    xp, xs = x_prompt, x_sample
    kps, vps, lps, cps = [], [], [], []
    kss, vss, lss, css = [], [], [], []
    for l in range(DEPTH):
        sh1, sc1, g1, sh2, sc2, g2 = _adaln(c_prompt, w_ada[l], b_ada[l])
        h = _modulate(_rms(xp, norm1_g[l]), sh1, sc1)
        q, k, v, logf, u = _in_proj(h, w_in[l], b_f[l], b_glu[l], q_norm_g[l], k_norm_g[l])
        a_out = _prompt_attention(q, k, v, logf)
        u_ext = jnp.concatenate([jnp.zeros((u.shape[0], CONV_WIDTH - 1, D_CONV), u.dtype), u], axis=1)
        c_out = _conv_branch(u_ext, conv_w[l], conv_b[l], conv_ln_g[l], conv_ln_b[l])
        xp = _tail(xp, a_out, c_out, g1, sh2, sc2, g2, w_o[l], norm2_g[l],
                   peer_w_query[l], peer_sub_keys[l], peer_u[l], peer_v[l])
        kps.append(k)
        vps.append(v)
        lps.append(logf)
        cps.append(u_ext[:, -(CONV_WIDTH - 1):])
        sh1, sc1, g1, sh2, sc2, g2 = _adaln(c_sample, w_ada[l], b_ada[l])
        h = _modulate(_rms(xs, norm1_g[l]), sh1, sc1)
        q, k, v, logf, u = _in_proj(h, w_in[l], b_f[l], b_glu[l], q_norm_g[l], k_norm_g[l])
        a_out = _sample_attention(q, k, v, logf, cache_k[l], cache_v[l], cache_logf[l], page_table)
        u_ext = jnp.concatenate([state_conv[l].astype(u.dtype), u], axis=1)
        c_out = _conv_branch(u_ext, conv_w[l], conv_b[l], conv_ln_g[l], conv_ln_b[l])
        xs = _tail(xs, a_out, c_out, g1, sh2, sc2, g2, w_o[l], norm2_g[l],
                   peer_w_query[l], peer_sub_keys[l], peer_u[l], peer_v[l])
        kss.append(k)
        vss.append(v)
        lss.append(logf)
        css.append(u_ext[:, -(CONV_WIDTH - 1):])
    return (xp, xs, jnp.stack(kps), jnp.stack(vps), jnp.stack(lps), jnp.stack(cps),
            jnp.stack(kss), jnp.stack(vss), jnp.stack(lss), jnp.stack(css))


_drawn_inputs = setup_inputs


def setup_inputs(seed=0):
    import zlib

    import numpy as np

    out = dict(_drawn_inputs(seed))
    spreads = {}
    factors = {'cache_logf': 5.876,
     'b_glu': 3.16,
     'q_norm_g': 6.06,
     'conv_b': 3.844,
     'conv_ln_g': 3.512,
     'conv_ln_b': 7.568,
     'norm2_g': 3.116}
    for name, (base, spread) in spreads.items():
        noise = np.random.default_rng([zlib.crc32(name.encode()), seed]).standard_normal(out[name].shape)
        drawn = base * np.exp(spread * noise) if base else spread * noise
        out[name] = __import__('jax').numpy.asarray(drawn.astype(out[name].dtype))
    for name, factor in factors.items():
        out[name] = (out[name] * factor).astype(out[name].dtype)
    return out
```

```python
from contextlib import ExitStack

import concourse.bass as bass
from concourse import mybir

F32 = mybir.dt.float32
BF16 = mybir.dt.bfloat16
I32 = mybir.dt.int32
U32 = mybir.dt.uint32
ALU = mybir.AluOpType
ACT = mybir.ActivationFunctionType
X = mybir.AxisListType.X

P = 128
D = 1024
DC = D // P
SEQ = 1024
NB = SEQ // P
NS = 8
QS = 4
TS = NS * QS
H = 8
HD = 64
DA = H * HD
CC = 4
W = 31
ZQ, ZK, ZV, ZF, ZG = 0, DA, 2 * DA, 3 * DA, 3 * DA + H
DIN = 3 * DA + H + 2 * CC * P
M = 1 + NS
EPS = 1e-6
AUG = HD + 2


def rows(t):
    return TS if isinstance(t, int) and t == 0 else P


class Own:

    def __init__(self, eng, sem):
        self.eng, self.sem, self.base, self.n = eng, sem, 0, 0

    def start(self, base):
        self.base, self.n = base, 0

    def step(self, ins):
        ins.then_inc(self.sem, 1)
        self.n += 1

    def settle(self):
        self.eng.wait_ge(self.sem, self.base + self.n)

    def carry(self):
        self.eng.sem_inc(self.carrier, 1)

    def do(self, ins):
        self.step(ins)
        self.settle()


def condition(nc, I, S, K):
    with ExitStack() as ctx:
        sb = lambda n, s, d=F32: ctx.enter_context(nc.sbuf_tensor(n, s, d))
        sem = lambda n: ctx.enter_context(nc.semaphore(n))
        wa = [sb(f"wa{i}", [P, DC, 512]) for i in range(3)]
        cT = sb("cT", [P, DC, M])
        bT = sb("bT", [P, 48])
        ng = sb("ng", [P, 2, DC])
        gS, gate, gate_s = sb("gS", [P, 2, DC, TS]), sb("gate", [P, 2, D]), sb("gate_s", [TS, 2, D])
        wide = sb("wide", [P, 2 * SEQ - P], BF16)
        mod_bank = ctx.enter_context(nc.psum_tensor("mod_bank", [P, 512], F32))
        mod_ps = mod_bank[:, 0:48 * M].rearrange("p (n m) -> p n m", m=M)
        gate_ps = [ctx.enter_context(nc.psum_tensor(f"gate_ps{i}", [P, 512], F32)) for i in range(4)]
        w_in = [sem(f"c_w{i}") for i in range(3)]
        small_in, w_used, id_step = sem("c_small"), sem("c_used"), sem("c_id")
        own_v, gates, gates_out = sem("c_own"), sem("c_gates"), sem("c_gout")
        stored = sem("c_stored")
        wv = I["w_ada"].rearrange("(k p) n -> p k n", p=P)
        modT, sgT, ident = K["modT"], K["sgT"], K["ident"]
        NCH = 12
        block = ctx.enter_context(nc.Block())

        @block.sync
        def _(sp):
            sp.dma_start(cT[:, :, :], I["cT"]).then_inc(small_in, 16)
            sp.dma_start(bT[:, :], I["b_adaT"]).then_inc(small_in, 16)
            sp.dma_start(ng[:, :, :], I["norm_gT"]).then_inc(small_in, 16)
            for n in range(NCH):
                if n >= 3:
                    sp.wait_ge(w_used, n - 2)
                sp.dma_start(wa[n % 3][:, :, :], wv[:, :, n * 512:(n + 1) * 512]).then_inc(w_in[n % 3], 16)
            sp.wait_ge(id_step, 7)
            sp.dma_start(S["mask"], wide[:, :]).then_inc(stored, 16)
            sp.wait_ge(gates_out, 2)
            for g in range(2):
                sp.dma_start(S["gate"][g], gate[:, g, :]).then_inc(stored, 16)
                sp.dma_start(S["gate_s"][g], gate_s[:, g, :]).then_inc(stored, 16)
            sp.wait_ge(stored, 16 * 5)

        @block.gpsimd
        def _(pool):
            pool.memset(ident[:, :], 0.0).then_inc(id_step, 1)
            pool.memset(K["tri"][:, :], 1.0).then_inc(id_step, 1)
            pool.memset(K["ones"][:, :], 1.0).then_inc(id_step, 1)
            pool.memset(wide[:, :], 0.0).then_inc(id_step, 1)
            pool.wait_ge(id_step, 4)
            pool.affine_select(out=ident[:, :], in_=ident[:, :], compare_op=ALU.not_equal, fill=1.0, base=0,
                               pattern=[[-1, P]], channel_multiplier=1).then_inc(id_step, 1)
            pool.affine_select(out=K["tri"][:, :], in_=K["tri"][:, :], compare_op=ALU.is_ge, fill=0.0, base=0,
                               pattern=[[1, P]], channel_multiplier=-1).then_inc(id_step, 1)
            pool.affine_select(out=wide[:, :], in_=wide[:, :], compare_op=ALU.is_ge, fill=-1e30, base=SEQ - P,
                               pattern=[[-1, 2 * SEQ - P]], channel_multiplier=1).then_inc(id_step, 1)

        @block.tensor
        def _(pe):
            pe.wait_ge(small_in, 48)
            for n in range(NCH):
                pe.wait_ge(w_in[n % 3], 16 * (n // 3 + 1))
                for j in range(4):
                    for k in range(DC):
                        mm = pe.matmul(mod_ps[:, 4 * n + j, :], wa[n % 3][:, k, j * P:(j + 1) * P], cT[:, k, :],
                                       start=(k == 0), stop=(k == DC - 1))
                mm.then_inc(w_used, 1)

            pe.wait_ge(own_v, 1)
            pe.wait_ge(id_step, 6)
            for g, first in ((0, 16), (1, 40)):
                for half in range(2):
                    for c in range(4):
                        mm = pe.matmul(gate_ps[2 * g + half][:, c * P:(c + 1) * P],
                                       modT[:, first + 4 * half + c, 0:1].to_broadcast([P, P]),
                                       ident[:, :], start=True, stop=True)
            mm.then_inc(gates, 1)
            pe.wait_ge(gates_out, 1)
            for g, first in ((0, 16), (1, 40)):
                for half in range(2):
                    for c in range(4):
                        mm = pe.matmul(gate_ps[2 * g + half][0:TS, c * P:(c + 1) * P],
                                       gS[:, g, 4 * half + c, :],
                                       ident[:, :], start=True, stop=True)
            mm.then_inc(gates, 1)

        @block.vector
        def _(v):
            own = Own(v, own_v)
            v.wait_ge(w_used, NCH)
            own.do(v.tensor_tensor(modT[:, :, :], mod_ps[:, :, :],
                                   bT[:, :].unsqueeze(2).to_broadcast([P, 48, M]), ALU.add))
            for i, first in ((0, 8), (1, 32)):
                own.do(v.tensor_scalar(sgT[:, i, :, :], modT[:, first:first + DC, :], 1.0, None, ALU.add))
                own.do(v.tensor_tensor(sgT[:, i, :, :], sgT[:, i, :, :],
                                       ng[:, i, :].unsqueeze(2).to_broadcast([P, DC, M]), ALU.mult))
                for c in range(DC):
                    fr = modT[:, (16, 40)[i] + c, 1:M].unsqueeze(2).to_broadcast([P, NS, QS])
                    own.do(v.tensor_copy(gS[:, i, c, :].rearrange("p (n q) -> p n q", n=NS), fr))
            v.wait_ge(gates, 1)
            for g in range(2):
                for half in range(2):
                    own.do(v.tensor_copy(gate[:, g, half * 512:(half + 1) * 512], gate_ps[2 * g + half][:, :]))
            v.sem_inc(gates_out, 1)
            v.wait_ge(gates, 2)
            for g in range(2):
                for half in range(2):
                    own.do(v.tensor_copy(gate_s[0:TS, g, half * 512:(half + 1) * 512],
                                         gate_ps[2 * g + half][0:TS, :]))
            v.sem_inc(gates_out, 1)


def project(nc, I, O, S, K):
    with ExitStack() as ctx:
        sb = lambda n, s, d=F32: ctx.enter_context(nc.sbuf_tensor(n, s, d))
        sem = lambda n: ctx.enter_context(nc.semaphore(n))
        w_in = sb("w_in", [P, DC, DIN])
        xb = sb("xb", [P, D])
        xs = sb("xs", [P, D])
        sqx = sb("sqx", [P, D])
        sqq = sb("sqq", [P, 2 * DA])
        hT = sb("hT", [P, DC, P])
        st = sb("st", [P, 8])
        sh = sb("sh", [P, 8, 2 * H])
        lf = sb("lf", [P, 8, H])
        lacc = sb("lacc", [P, H])
        qa = sb("qa", [P, H, AUG])
        ka = sb("ka", [P, H, AUG])
        vb = sb("vb", [P, DA])
        qTb = sb("qTb", [P, H, P])
        kTb = sb("kTb", [P, H, P])
        eg = sb("eg", [P, CC, P])
        uT = sb("uT", [P, CC, P])
        ub = sb("ub", [P, DA])
        gq = sb("gq", [P, HD])
        gk = sb("gk", [P, HD])
        bf = sb("bf", [P, H])
        bg = sb("bg", [P, 2, CC])
        nbg = sb("nbg", [P, CC])
        zero = sb("zero", [P, CC, W - 1])
        A = [ctx.enter_context(nc.psum_tensor(f"A{i}", [P, 512], F32)) for i in range(8)]

        w_sem, small_in, x_in = sem("p_w"), sem("p_small"), sem("p_x")
        ss_ready, ms_ready, r0_ready, xs_ready = sem("p_ss"), sem("p_ms"), sem("p_r0"), sem("p_xs")
        xT_done, hT_ready, qkv_done, fg_done, glu_done = sem("p_xT"), sem("p_hT"), sem("p_qkv"), sem("p_fg"), sem("p_glu")
        sqq_ready, hms_ready, hr0_ready, qk_ready = sem("p_sqq"), sem("p_hms"), sem("p_hr0"), sem("p_qk")
        v_ready, la_ready, lln_ready, logf_ready = sem("p_v"), sem("p_la"), sem("p_lln"), sem("p_logf")
        F_done, Fq_ready, qkT_done, qkT_ready = sem("p_F"), sem("p_Fq"), sem("p_qkT"), sem("p_qkTr")
        eg_ready, u_ready, uTT_done, ub_ready = sem("p_eg"), sem("p_u"), sem("p_uTT"), sem("p_ub")
        stored_k, stored_v, stored_l, stored_qk, stored_u = sem("p_ok"), sem("p_ov"), sem("p_ol"), sem("p_oqk"), sem("p_ou")
        once_out = sem("p_once")
        ubs_ready, ubs_out, cst2 = sem("p_ubs"), sem("p_ubso"), sem("p_cst2")
        own_v, own_a, own_p, cst = sem("p_ownv"), sem("p_owna"), sem("p_ownp"), sem("p_cst")
        OV, OA = 17, 1
        OVN, OAN = 4, 1
        ident = K["ident"]
        block = ctx.enter_context(nc.Block())

        @block.sync
        def _(sp):
            sp.dma_start(xb[0:TS, :], I["x_sample"]).then_inc(x_in, 16)
            sp.dma_start(w_in[:, :, :], I["w_in"].rearrange("(k p) n -> p k n", p=P)).then_inc(w_sem, 16)
            for dst, src in ((gq[:, :], I["q_g"].to_broadcast([P, HD])), (gk[:, :], I["k_g"].to_broadcast([P, HD])),
                             (bf[:, :], I["b_f"].to_broadcast([P, H])), (bg[:, :, :], I["b_gluT"])):
                sp.dma_start(dst, src).then_inc(small_in, 16)
            sp.dma_start(O["conv_sample"][:, 0:W - 1 - QS, :], I["state_conv"][:, QS:W - 1, :]).then_inc(once_out, 16)
            sp.wait_ge(cst, 1)
            sp.dma_start(S["uT"][:, :, 0:W - 1], zero[:, :, :]).then_inc(once_out, 16)

            def load_x(t, at):
                sp.wait_ge(xs_ready, t)
                sp.dma_start(xb[:, :], I["x_prompt"][bass.ds(at, P), :]).then_inc(x_in, 16)

            def store(t, n, at, u_at):
                r = rows(t)
                sp.wait_ge(v_ready, n)
                if r == TS:
                    sp.dma_start(O["v_sample"], vb[0:r, :]).then_inc(stored_v, 16)
                else:
                    sp.dma_start(O["v_prompt"][bass.ds(at, P), :], vb[:, :]).then_inc(stored_v, 16)
                sp.wait_ge(logf_ready, n)
                if r == TS:
                    sp.dma_start(O["logf_sample"], lf[0:r, 5, :]).then_inc(stored_l, 16)
                else:
                    sp.dma_start(O["logf_prompt"][bass.ds(at, P), :], lf[:, 5, :]).then_inc(stored_l, 16)
                sp.wait_ge(qk_ready, n)
                if r == TS:
                    sp.dma_start(O["k_sample"].rearrange("t (h d) -> t h d", h=H), ka[0:r, :, 0:HD]).then_inc(stored_k, 16)
                else:
                    sp.dma_start(O["k_prompt"][bass.ds(at, P), :].rearrange("t (h d) -> t h d", h=H),
                                 ka[:, :, 0:HD]).then_inc(stored_k, 16)
                sp.wait_ge(u_ready, n)
                if r == TS:
                    sp.dma_start(S["uTs"], uT[:, :, 0:TS]).then_inc(stored_u, 16)
                else:
                    sp.dma_start(S["uT"][:, :, bass.ds(u_at, P)], uT[:, :, :]).then_inc(stored_u, 16)
                sp.wait_ge(qkT_ready, n)
                if r == TS:
                    sp.dma_start(S["qTs"], qTb[:, 0:CC, 0:TS]).then_inc(stored_qk, 16)
                    sp.dma_start(S["kTs"], kTb[:, 0:CC, 0:TS]).then_inc(stored_qk, 16)
                else:
                    sp.dma_start(S["qT"][:, :, bass.ds(at, P)], qTb[0:AUG, :, :]).then_inc(stored_qk, 16)
                    sp.dma_start(S["kT"][:, :, bass.ds(at, P)], kTb[0:AUG, :, :]).then_inc(stored_qk, 16)

            load_x(1, 0)
            store(0, 1, None, None)
            sp.wait_ge(ubs_ready, 1)
            sp.dma_start(O["conv_sample"][:, W - 1 - QS:W - 1, :], ub[0:TS, :]).then_inc(ubs_out, 16)
            for t in range(1, NB):
                load_x(t + 1, t * P)
                store(t, t + 1, (t - 1) * P, (t - 1) * P + W - 1)
            store(NB, NB + 1, (NB - 1) * P, (NB - 1) * P + W - 1)
            sp.wait_ge(ub_ready, 1)
            sp.dma_start(O["conv_prompt"], ub[P - (W - 1):P, :]).then_inc(once_out, 16)
            sp.wait_ge(once_out, 16 * 3)
            for s, n in ((stored_k, 1), (stored_v, 1), (stored_l, 1), (stored_u, 1), (stored_qk, 2)):
                sp.wait_ge(s, 16 * n * (NB + 1))

        @block.gpsimd
        def _(pool):
            pool.memset(zero[:, :, :], 0.0).then_inc(cst, 1)
            pool.memset(lacc[:, :], 0.0).then_inc(own_p, 1)
            pool.memset(qa[:, :, HD + 1:AUG], 1.0).then_inc(own_p, 1)
            pool.memset(ka[:, :, HD:HD + 1], 1.0).then_inc(own_p, 1)
            pool.wait_ge(small_in, 64)
            pool.wait_ge(own_p, 3)
            pool.tensor_scalar(nbg[:, :], bg[:, 1, :], -1.0, None, ALU.mult).then_inc(own_p, 1)
            pool.tensor_scalar(gq[:, :], gq[:, :], HD ** -0.5, None, ALU.mult).then_inc(own_p, 1)

        @block.scalar
        def _(act):
            own = Own(act, own_a)

            def norm_x(t):
                r = rows(t)
                act.wait_ge(x_in, 16 * t + 16)
                act.activation(sqx[0:r, :], xb[0:r, :], ACT.Square, accum_out=st[0:r, 0:1]).then_inc(ss_ready, 1)
                act.wait_ge(ms_ready, t + 1)
                own.start(t)
                own.do(act.activation(st[0:r, 2:3], st[0:r, 1:2], ACT.Ln))
                act.activation(st[0:r, 3:4], st[0:r, 2:3], ACT.Exp, scale=-0.5).then_inc(r0_ready, 1)

            def body(t, more=True):
                r = rows(t)
                if r == P:
                    act.wait_ge(xT_done, t + 1)
                    for c in range(DC):
                        a = act.activation(hT[:, c, :], A[c // 4][:, (c % 4) * P:(c % 4 + 1) * P], ACT.Identity,
                                           scale=K["sgT"][:, 0, c, 0:1], bias=K["modT"][:, c, 0:1])
                    a.then_inc(hT_ready, 1)
                if more:
                    norm_x(t + 1)
                act.wait_ge(qkv_done, 3 * t + 3)
                act.activation(sqq[0:r, 0:DA], A[2][0:r, :], ACT.Square)
                act.activation(sqq[0:r, DA:2 * DA], A[3][0:r, :], ACT.Square).then_inc(sqq_ready, 1)
                if not isinstance(t, int) or t > 0:
                    act.wait_ge(stored_v, 16 * t)
                act.activation(vb[0:r, :], A[4][0:r, :], ACT.Copy).then_inc(v_ready, 1)
                act.wait_ge(hms_ready, t + 1)
                act.activation(sh[0:r, 2, :], sh[0:r, 1, :], ACT.Ln).then_inc(hr0_ready, 1)
                act.wait_ge(hr0_ready, 2 * t + 1)
                act.activation(sh[0:r, 3, :], sh[0:r, 2, :], ACT.Exp, scale=-0.5).then_inc(hr0_ready, 1)
                act.wait_ge(la_ready, t + 1)
                act.activation(lf[0:r, 2, :], lf[0:r, 1, :], ACT.Exp, scale=-1.0).then_inc(lln_ready, 1)
                act.wait_ge(lln_ready, 2 * t + 1)
                act.activation(lf[0:r, 3, :], lf[0:r, 2, :], ACT.Ln, bias=1.0).then_inc(lln_ready, 1)
                act.wait_ge(glu_done, t + 1)
                for c in range(CC):
                    a = act.activation(eg[:, c, 0:r], A[1][:, c * P:c * P + r], ACT.Exp, scale=-1.0,
                                       bias=nbg[:, c:c + 1])
                a.then_inc(eg_ready, 1)
                act.wait_ge(qkT_done, t + 1)
                if not isinstance(t, int) or t > 0:
                    act.wait_ge(stored_qk, 32 * t)
                if r == P:
                    for i, dst in enumerate((qTb, kTb)):
                        for g in range(2):
                            a = act.activation(dst[0:AUG, 4 * g:4 * g + 4, :].rearrange("p h t -> p (h t)"),
                                               A[2 + 2 * i + g][0:AUG, :], ACT.Copy)
                else:
                    for i, dst in enumerate((qTb, kTb)):
                        a = act.activation(dst[:, 0:CC, 0:TS],
                                           A[2 + 2 * i][:, 0:CC * TS].rearrange("p (c t) -> p c t", c=CC), ACT.Copy)
                a.then_inc(qkT_ready, 1)

            act.wait_ge(own_p, 5)
            norm_x(0)
            body(0)
            with act.Fori(1, NB) as t:
                body(t)
            body(NB, False)

        @block.vector
        def _(v):
            own = Own(v, own_v)

            def newton(m, r0, a, b, r):
                own.do(v.tensor_tensor(a, r0, r0, ALU.mult))
                own.do(v.tensor_tensor(b, a, m, ALU.mult))
                own.do(v.tensor_scalar(a, b, -0.5, 1.5, ALU.mult, ALU.add))
                return v.tensor_tensor(r, a, r0, ALU.mult)

            def norm_x(t):
                r = rows(t)
                v.wait_ge(ss_ready, t + 1)
                v.tensor_scalar(st[0:r, 1:2], st[0:r, 0:1], 1.0 / D, EPS, ALU.mult, ALU.add).then_inc(ms_ready, 1)
                v.wait_ge(r0_ready, t + 1)
                own.start(OVN * t + (0 if isinstance(t, int) and t == 0 else OV * (t - 1)))
                own.do(newton(st[0:r, 1:2], st[0:r, 3:4], st[0:r, 4:5], st[0:r, 5:6], st[0:r, 7:8]))
                if not isinstance(t, int) or t > 0:
                    v.wait_ge(xT_done, t)
                v.tensor_scalar(xs[0:r, :], xb[0:r, :], st[0:r, 7:8], None, ALU.mult).then_inc(xs_ready, 1)
                assert own.n == OVN

            def body(t, more=True):
                r = rows(t)
                if r == TS:
                    own.start(OVN)
                    v.wait_ge(xT_done, 1)
                    for g in range(2):
                        ps = A[g][:, :].rearrange("p (c n) -> p c n", c=4)
                        for c in range(4):
                            o = hT[:, 4 * g + c, 0:TS].rearrange("p (n q) -> p n q", n=NS)
                            i = ps[:, c, 0:TS].rearrange("p (n q) -> p n q", n=NS)
                            cc = 4 * g + c
                            v.tensor_tensor(o, i, K["sgT"][:, 0, cc, 1:M].unsqueeze(2).to_broadcast([P, NS, QS]),
                                            ALU.mult).then_inc(cst2, 1)
                            v.wait_ge(cst2, 2 * cc + 1)
                            v.tensor_tensor(o, o, K["modT"][:, cc, 1:M].unsqueeze(2).to_broadcast([P, NS, QS]),
                                            ALU.add).then_inc(cst2, 1)
                    v.wait_ge(cst2, 2 * DC)
                    v.sem_inc(hT_ready, 1)
                if more:
                    norm_x(t + 1)
                own.start(OVN * (t + 2) + OV * t if more else OVN * (t + 1) + OV * t)
                v.wait_ge(fg_done, t + 1)
                if not isinstance(t, int) or t > 0:
                    v.wait_ge(stored_l, 16 * t)
                own.do(v.tensor_tensor(lf[0:r, 0, :], A[5][0:r, 0:H], bf[0:r, :], ALU.add))
                own.do(v.tensor_scalar(lf[0:r, 4, :], lf[0:r, 0, :], -1.0, None, ALU.mult))
                v.tensor_tensor(lf[0:r, 1, :], lf[0:r, 0, :], lf[0:r, 4, :], ALU.max).then_inc(la_ready, 1)
                own.do(v.tensor_scalar(lf[0:r, 6, :], lf[0:r, 0, :], 0.0, None, ALU.min))
                v.wait_ge(sqq_ready, t + 1)
                own.do(v.tensor_reduce(sh[0:r, 0, :], sqq[0:r, :].rearrange("p (h d) -> p h d", d=HD), X, ALU.add))
                v.tensor_scalar(sh[0:r, 1, :], sh[0:r, 0, :], 1.0 / HD, EPS, ALU.mult, ALU.add).then_inc(hms_ready, 1)
                v.wait_ge(lln_ready, 2 * t + 2)
                own.settle()
                v.tensor_tensor(lf[0:r, 5, :], lf[0:r, 6, :], lf[0:r, 3, :], ALU.subtract).then_inc(logf_ready, 1)
                v.wait_ge(hr0_ready, 2 * t + 2)
                own.do(newton(sh[0:r, 1, :], sh[0:r, 3, :], sh[0:r, 4, :], sh[0:r, 5, :], sh[0:r, 7, :]))
                if not isinstance(t, int) or t > 0:
                    v.wait_ge(stored_k, 16 * t)
                    v.wait_ge(qkT_done, t)
                for i, (dst, g) in enumerate(((qa, gq), (ka, gk))):
                    o = dst[0:r, :, 0:HD]
                    own.do(v.tensor_tensor(o, A[2 + i][0:r, :].rearrange("p (h d) -> p h d", h=H),
                                           sh[0:r, 7, i * H:(i + 1) * H].unsqueeze(2).to_broadcast([r, H, HD]), ALU.mult))
                    own.step(v.tensor_tensor(o, o, g[0:r, :].unsqueeze(1).to_broadcast([r, H, HD]), ALU.mult))
                own.settle()
                if r == TS:
                    for i, src in enumerate((qa, ka)):
                        v.tensor_copy(sqq[0:r, i * DA:(i + 1) * DA].rearrange("p (h d) -> p h d", h=H),
                                      src[0:r, :, 0:HD]).then_inc(cst2, 1)
                    v.wait_ge(cst2, 2 * DC + 2)
                v.sem_inc(qk_ready, 1)
                v.wait_ge(F_done, t + 1)
                if r == P:
                    own.step(v.tensor_copy(qa[:, :, HD], A[5][:, 16:16 + H]))
                    own.step(v.tensor_scalar(ka[:, :, HD + 1], A[5][:, 16:16 + H], -1.0, None, ALU.mult))
                    own.step(v.tensor_tensor(lacc[:, :], lacc[:, :], lf[:, 5, :], ALU.add))
                    own.settle()
                else:
                    for _ in range(3):
                        own.step(v.nop())
                    own.settle()
                v.sem_inc(Fq_ready, 1)
                v.wait_ge(eg_ready, t + 1)
                own.do(v.tensor_scalar(eg[:, :, 0:r], eg[:, :, 0:r], 1.0, None, ALU.add))
                own.do(v.reciprocal(eg[:, :, 0:r], eg[:, :, 0:r]))
                if not isinstance(t, int) or t > 0:
                    v.wait_ge(stored_u, 16 * t)
                for c in range(CC):
                    a = v.scalar_tensor_tensor(uT[:, c, 0:r], A[0][:, c * P:c * P + r], bg[:, 0, c:c + 1],
                                               eg[:, c, 0:r], ALU.add, ALU.mult)
                a.then_inc(u_ready, 1)
                assert own.n == OV, own.n

            v.wait_ge(own_p, 5)
            norm_x(0)
            body(0)
            v.wait_ge(uTT_done, 1)
            v.tensor_copy(ub[0:TS, :], A[6][0:TS, :]).then_inc(ubs_ready, 1)
            with v.Fori(1, NB) as t:
                body(t)
            body(NB, False)
            v.wait_ge(uTT_done, 2)
            v.wait_ge(ubs_out, 16)
            v.tensor_copy(ub[:, :], A[6][:, :]).then_inc(ub_ready, 1)

        @block.tensor
        def _(pe):
            def body(t):
                r = rows(t)
                pe.wait_ge(xs_ready, t + 1)
                if not isinstance(t, int) or t > 0:
                    pe.wait_ge(u_ready, t)
                    pe.wait_ge(qkT_ready, t)
                for c in range(DC):
                    mm = pe.transpose(A[c // 4][:, (c % 4) * P:(c % 4) * P + r], xs[0:r, c * P:(c + 1) * P],
                                      ident[0:r, 0:r])
                mm.then_inc(xT_done, 1)
                pe.wait_ge(hT_ready, t + 1)
                for k in range(DC):
                    mm = pe.matmul(A[5][0:r, 0:H], hT[:, k, 0:r], w_in[:, k, ZF:ZF + H], start=(k == 0), stop=(k == DC - 1))
                mm.then_inc(fg_done, 1)
                for j in range(3):
                    for k in range(DC):
                        mm = pe.matmul(A[2 + j][0:r, :], hT[:, k, 0:r], w_in[:, k, j * DA:(j + 1) * DA],
                                       start=(k == 0), stop=(k == DC - 1))
                    mm.then_inc(qkv_done, 1)
                for j in range(2 * CC):
                    for k in range(DC):
                        mm = pe.matmul(A[j // CC][:, (j % CC) * P:(j % CC) * P + r],
                                       w_in[:, k, ZG + j * P:ZG + (j + 1) * P], hT[:, k, 0:r],
                                       start=(k == 0), stop=(k == DC - 1))
                mm.then_inc(glu_done, 1)
                pe.wait_ge(logf_ready, t + 1)
                if r == P:
                    pe.matmul(A[5][:, 16:16 + H], K["tri"][:, :], lf[:, 5, :], start=True, stop=False)
                    pe.matmul(A[5][:, 16:16 + H], K["ones"][:, :], lacc[:, :], start=False, stop=True).then_inc(F_done, 1)
                else:
                    pe.nop().then_inc(F_done, 1)
                pe.wait_ge(qk_ready, t + 1)
                pe.wait_ge(Fq_ready, t + 1)
                pe.wait_ge(v_ready, t + 1)
                if r == P:
                    for i, src in enumerate((qa, ka)):
                        for h in range(H):
                            mm = pe.transpose(A[2 + 2 * i + h // 4][0:AUG, (h % 4) * P:(h % 4 + 1) * P],
                                              src[:, h, :], ident[:, :])
                else:
                    for i, src in enumerate((qa, ka)):
                        for c in range(CC):
                            mm = pe.transpose(A[2 + 2 * i][:, c * TS:(c + 1) * TS],
                                              sqq[0:r, i * DA + c * P:i * DA + (c + 1) * P], ident[0:r, 0:r])
                mm.then_inc(qkT_done, 1)

            def u_rows(r):
                for c in range(CC):
                    mm = pe.transpose(A[6][0:r, c * P:(c + 1) * P], uT[:, c, 0:r], ident[:, :])
                mm.then_inc(uTT_done, 1)

            pe.wait_ge(w_sem, 16)
            body(0)
            pe.wait_ge(u_ready, 1)
            u_rows(TS)
            with pe.Fori(1, NB) as t:
                body(t)
            body(NB)
            pe.wait_ge(u_ready, NB + 1)
            pe.wait_ge(ubs_ready, 1)
            u_rows(P)


def sampled(nc, I, O, S, K):
    NP = 4
    with ExitStack() as ctx:
        sb = lambda n, s, d=F32: ctx.enter_context(nc.sbuf_tensor(n, s, d))
        sem = lambda n: ctx.enter_context(nc.semaphore(n))
        psum = lambda n: ctx.enter_context(nc.psum_tensor(n, [P, 512], F32))
        Kp = sb("Kp", [P, 2, NP, DA])
        Vp = sb("Vp", [P, NS, NP, DA])
        Lp = sb("Lp", [P, NS * NP, H])
        KT = sb("KT", [P, 2, CC, NP * P])
        idx = sb("idx", [P, NS * NP], I32)
        pt = sb("pt", [P, NS * NP], I32)
        lane = sb("lane", [P, 1], I32)
        lanef = sb("lanef", [P, 1])
        qT = sb("s_qT", [P, CC, TS])
        kT = sb("s_kT", [P, CC, TS])
        vs = sb("s_v", [TS, DA])
        ls = sb("s_l", [TS, H])
        Qbd = sb("Qbd", [P, CC, NS, H, QS])
        later = sb("later", [P, 896])
        later32 = sb("later32", [TS, TS])
        upto = sb("upto", [TS, NS, QS])
        uptoh = sb("uptoh", [TS, NS, H, QS])
        eqh = sb("eqh", [TS, NS, H, QS])
        L = sb("L", [TS, NS, H, QS])
        Lb = sb("Lb", [P, NS * NP, H, QS])
        hrow = sb("hrow", [H, P])
        hcol = sb("hcol", [H, DA])
        ones5 = sb("ones5", [TS, 512])
        hm = sb("hm", [P, DA])
        selS = sb("selS", [P, 2, TS])
        mown = sb("mown", [P, 2, TS])
        So = sb("So", [P, 2, TS])
        Pm = sb("Pm", [P, 2, 512 + TS])
        PT = sb("PT", [P, 2, NP, P])
        PTo = sb("PTo", [TS, 2, P])
        Om = sb("Om", [P, 2, DA])
        sm = sb("sm", [P, 2, 8])
        aT = sb("aT", [P, CC, TS])
        T = [psum(f"T{i}") for i in range(2)]
        SG = [psum(f"SG{i}") for i in range(2)]
        SO, MI, OG, AT = psum("SO"), psum("MI"), psum("OG"), psum("AT")
        OWN = [SO, MI]
        small_in, idx_ready, cst, own_v = sem("s_small"), sem("s_idx"), sem("s_cst"), sem("s_own")
        k_in = [sem(f"s_k{i}") for i in range(2)]
        v_in, l_in = [sem(f"s_v{i}") for i in range(2)], [sem(f"s_l{i}") for i in range(2)]
        pt_in = sem("s_pt")
        kt_done, kt_act, kt_dve = sem("s_ktd"), sem("s_kta"), sem("s_ktv")
        q_ready, s_done, masks_done, m_ready, e_done = sem("s_q"), sem("s_s"), sem("s_mk"), sem("s_m"), sem("s_e")
        pt_done, pt_ready, o_done, om_ready, at_done, at_ready = (sem("s_ptd"), sem("s_ptr"), sem("s_od"), sem("s_om"),
                                                                  sem("s_atd"), sem("s_atr"))
        stored, masks_ready = sem("s_st"), sem("s_mkr")
        ident = K["ident"]
        i32 = ident[0:TS, 0:TS]
        cache = {"k": I["cache_k"], "v": I["cache_v"], "l": I["cache_logf"]}
        block = ctx.enter_context(nc.Block())

        @block.sync
        def _(sp):
            sp.dma_start(pt[:, :], I["page_table"].to_broadcast([P, NS * NP])).then_inc(pt_in, 16)
            for dst, src in ((qT, S["qTs"]), (kT, S["kTs"]), (vs, O["v_sample"]), (ls, O["logf_sample"])):
                sp.dma_start(dst[:], src).then_inc(small_in, 16)
            sp.wait_ge(at_ready, 1)
            sp.dma_start(S["attTs"], aT[:, :, :]).then_inc(stored, 16)
            sp.wait_ge(stored, 16)

        @block.gpsimd
        def _(pool):
            pool.iota(lane[:, :], [[0, 1]], base=0, channel_multiplier=1).then_inc(cst, 1)
            pool.memset(later[:, :], 1.0).then_inc(cst, 1)
            pool.memset(later32[:, :], 1.0).then_inc(cst, 1)
            pool.memset(upto[:, :, :], 1.0).then_inc(cst, 1)
            pool.memset(hrow[:, :], 1.0).then_inc(cst, 1)
            pool.memset(hcol[:, :], 1.0).then_inc(cst, 1)
            pool.memset(ones5[:, :], 1.0).then_inc(cst, 1)
            pool.memset(Qbd[:, :, :, :, :], 0.0).then_inc(cst, 1)
            pool.wait_ge(cst, 8)
            pool.affine_select(out=later[:, :], in_=later[:, :], compare_op=ALU.is_gt, fill=0.0, base=384,
                               pattern=[[-1, 896]], channel_multiplier=1).then_inc(cst, 1)
            pool.affine_select(out=later32[:, :], in_=later32[:, :], compare_op=ALU.is_gt, fill=0.0, base=0,
                               pattern=[[-1, TS]], channel_multiplier=1).then_inc(cst, 1)
            pool.affine_select(out=upto[:, :, :], in_=upto[:, :, :], compare_op=ALU.is_ge, fill=0.0, base=0,
                               pattern=[[-QS, NS], [0, QS]], channel_multiplier=1).then_inc(cst, 1)
            pool.affine_select(out=hrow[:, :], in_=hrow[:, :], compare_op=ALU.is_equal, fill=0.0, base=0,
                               pattern=[[0, 4], [-1, H], [0, QS]], channel_multiplier=1).then_inc(cst, 1)
            pool.affine_select(out=hcol[:, :], in_=hcol[:, :], compare_op=ALU.is_equal, fill=0.0, base=0,
                               pattern=[[-1, H], [0, HD]], channel_multiplier=1).then_inc(cst, 1)
            pool.wait_ge(cst, 13)
            pool.affine_select(out=upto[:, :, :], in_=upto[:, :, :], compare_op=ALU.is_ge, fill=0.0, base=0,
                               pattern=[[QS, NS], [1, QS]], channel_multiplier=-1).then_inc(cst, 1)
            pool.wait_ge(idx_ready, 1)
            at = lambda n: bass.IndirectOffsetOnAxis(idx[:, n:n + 1], 0)
            for n in range(NS):
                if n >= 2:
                    pool.wait_ge(s_done, n - 1)
                for j in range(NP):
                    pool.indirect_dma_start(Kp[:, n % 2, j, :], None, cache["k"], at(NP * n + j)).then_inc(k_in[n % 2], 16)
                    pool.indirect_dma_start(Lp[:, NP * n + j, :], None, cache["l"], at(NP * n + j)).then_inc(l_in[n % 2], 16)
                for j in range(NP):
                    pool.indirect_dma_start(Vp[:, n, j, :], None, cache["v"], at(NP * n + j)).then_inc(v_in[n // 4], 16)

        @block.scalar
        def _(act):
            def keys(n):
                for c in range(1, CC, 2):
                    act.wait_ge(kt_done, CC * n + c + 1)
                    if n >= 2:
                        act.wait_ge(s_done, n - 1)
                    act.activation(KT[:, n % 2, c, :], T[c % 2][:, :], ACT.Copy).then_inc(kt_act, 1)

            def soft(g):
                act.wait_ge(m_ready, g + 1)
                act.activation(Pm[:, g, 0:512], SG[g][:, :], ACT.Exp, bias=sm[:, g, 2:3], accum_out=sm[:, g, 3:4])
                act.activation(Pm[:, g, 512:], So[:, g, :], ACT.Exp, bias=sm[:, g, 2:3],
                               accum_out=sm[:, g, 4:5]).then_inc(e_done, 1)

            for n in range(NS):
                keys(n)
                if n == 4:
                    soft(0)
            soft(1)

        @block.vector
        def _(v):
            own = Own(v, own_v)
            v.wait_ge(pt_in, 16)
            v.wait_ge(cst, 8)
            own.do(v.tensor_copy(lanef[:, :], lane[:, :]))
            v.tensor_scalar(idx[:, :], pt[:, :], float(P), lanef[:, 0:1], ALU.mult, ALU.add).then_inc(idx_ready, 1)
            v.wait_ge(small_in, 64)
            for c in range(CC):
                for half in range(2):
                    r = slice(half * HD, (half + 1) * HD)
                    own.step(v.tensor_copy(Qbd[r, c, :, 2 * c + half, :],
                                           qT[r, c, :].rearrange("p (n q) -> p n q", n=NS)))
            v.wait_ge(cst, 14)
            own.step(v.tensor_copy(uptoh[:, :, :, :], upto[:, :, :].unsqueeze(2).to_broadcast([TS, NS, H, QS])))
            own.step(v.tensor_copy(eqh[:, :, :, :], i32.rearrange("p (n q) -> p n q", n=NS).unsqueeze(2)
                                   .to_broadcast([TS, NS, H, QS])))
            own.settle()
            own.do(v.tensor_tensor(L[:, :, :, :].rearrange("p n h q -> p n (h q)").rearrange("p n (h q) -> p n h q", h=H),
                                   uptoh[:, :, :, :],
                                   ls[:, :].unsqueeze(1).unsqueeze(3).to_broadcast([TS, NS, H, QS]), ALU.mult))
            v.sem_inc(q_ready, 1)

            def keys(n):
                v.wait_ge(l_in[n % 2], 16 * NP * (n // 2 + 1))
                for j in range(NP):
                    own.step(v.tensor_copy(Lb[:, NP * n + j, :, :],
                                           Lp[:, NP * n + j, :].unsqueeze(2).to_broadcast([P, H, QS])))
                own.settle()
                for c in range(0, CC, 2):
                    v.wait_ge(kt_done, CC * n + c + 1)
                    if n >= 2:
                        v.wait_ge(s_done, n - 1)
                    v.tensor_copy(KT[:, n % 2, c, :], T[c % 2][:, :]).then_inc(kt_dve, 1)

            def soft(g):
                v.wait_ge(s_done, 4 * g + 4)
                own.do(v.tensor_tensor(So[:, g, :], OWN[g][:, 0:TS], mown[:, g, :], ALU.add))
                own.step(v.tensor_reduce(sm[:, g, 0:1], SG[g][:, :], X, ALU.max))
                own.step(v.tensor_reduce(sm[:, g, 1:2], So[:, g, :], X, ALU.max))
                own.settle()
                own.do(v.tensor_tensor(sm[:, g, 5:6], sm[:, g, 0:1], sm[:, g, 1:2], ALU.max))
                v.tensor_scalar(sm[:, g, 2:3], sm[:, g, 5:6], -1.0, None, ALU.mult).then_inc(m_ready, 1)
                v.wait_ge(e_done, g + 1)
                own.do(v.tensor_tensor(sm[:, g, 6:7], sm[:, g, 3:4], sm[:, g, 4:5], ALU.add))
                own.do(v.reciprocal(sm[:, g, 7:8], sm[:, g, 6:7]))

            def weigh(g):
                v.wait_ge(pt_done, g + 1)
                own.step(v.tensor_copy(PT[:, g, :, :].rearrange("p j r -> p (j r)"), AT[:, :]))
                own.step(v.tensor_copy(PTo[:, g, :], SO[0:TS, 0:P]))
                own.settle()
                v.sem_inc(pt_ready, 1)
                v.wait_ge(o_done, g + 1)
                v.scalar_tensor_tensor(Om[:, g, :], OG[:, :], sm[:, g, 7:8], hm[:, :], ALU.mult, ALU.mult)\
                    .then_inc(om_ready, 1)

            v.wait_ge(masks_done, 1)
            own.step(v.tensor_scalar(mown[:, :, :].rearrange("p g t -> p (g t)"), MI[:, 0:2 * TS], -1.0, 1e30,
                                     ALU.add, ALU.mult))
            own.step(v.tensor_copy(selS[:, :, :].rearrange("p g t -> p (g t)"), MI[:, 2 * TS:4 * TS]))
            own.step(v.tensor_copy(hm[:, :], OG[:, :]))
            own.settle()
            v.sem_inc(masks_ready, 1)
            for n in range(NS):
                keys(n)
                if n == 4:
                    soft(0)
                if n == 5:
                    weigh(0)
            soft(1)
            weigh(1)
            v.wait_ge(at_done, 1)
            v.tensor_copy(aT[:, :, :].rearrange("p c t -> p (c t)"), AT[:, 0:CC * TS]).then_inc(at_ready, 1)

        @block.tensor
        def _(pe):
            pe.wait_ge(q_ready, 1)
            for n in range(NS):
                o = slice(32 * (n % 4), 32 * (n % 4) + 32)
                hq = lambda a: a[:, n, :, :].rearrange("p h q -> p (h q)")
                pe.matmul(MI[o, (n // 4) * TS:(n // 4 + 1) * TS], hq(uptoh), i32, start=True, stop=True)
            for n in range(NS):
                o = slice(32 * (n % 4), 32 * (n % 4) + 32)
                hq = lambda a: a[:, n, :, :].rearrange("p h q -> p (h q)")
                pe.matmul(MI[o, (2 + n // 4) * TS:(3 + n // 4) * TS], hq(eqh), i32, start=True, stop=True)
            pe.matmul(OG[:, :], hrow[:, :], hcol[:, :], start=True, stop=True).then_inc(masks_done, 1)

            def score(n):
                g, o = n // 4, slice(32 * (n % 4), 32 * (n % 4) + 32)
                hq = lambda a, m: a[:, m, :, :].rearrange("p h q -> p (h q)")
                pe.wait_ge(k_in[n % 2], 16 * NP * (n // 2 + 1))
                for c in range(CC):
                    if c >= 2 or n >= 1:
                        last = 2 * n + c // 2
                        pe.wait_ge(kt_dve if c % 2 == 0 else kt_act, last)
                    for j in range(NP):
                        mm = pe.transpose(T[c % 2][:, j * P:(j + 1) * P], Kp[:, n % 2, j, c * P:(c + 1) * P], ident[:, :])
                    mm.then_inc(kt_done, 1)
                pe.wait_ge(kt_dve, 2 * n + 2)
                pe.wait_ge(kt_act, 2 * n + 2)
                for c in range(CC):
                    pe.matmul(SG[g][o, :], hq(Qbd[:, c], n), KT[:, n % 2, c, :], start=(c == 0), stop=False)
                for j in range(NP):
                    pe.matmul(SG[g][o, :], hq(Lb, NP * n + j), later[:, 384 - P * j:896 - P * j], start=False, stop=False)
                pe.matmul(SG[g][o, :], hq(L, n), ones5[:, :], start=False, stop=True)
                so = OWN[g][o, 0:TS]
                for c in range(CC):
                    pe.matmul(so, hq(Qbd[:, c], n), kT[:, c, :], start=(c == 0), stop=False)
                pe.matmul(so, hq(L, n), later32[:, :], start=False, stop=True).then_inc(s_done, 1)

            def values(g):
                pe.wait_ge(e_done, g + 1)
                for j in range(NP):
                    pe.transpose(AT[:, j * P:(j + 1) * P], Pm[:, g, j * P:(j + 1) * P], ident[:, :])
                pe.transpose(SO[0:TS, 0:P], Pm[:, g, 512:], ident[:, :]).then_inc(pt_done, 1)
                pe.wait_ge(pt_ready, g + 1)
                pe.wait_ge(v_in[g], 16 * NP * 4)
                if g:
                    pe.wait_ge(om_ready, 1)
                for n in range(4 * g, 4 * g + 4):
                    o = slice(32 * (n % 4), 32 * (n % 4) + 32)
                    for j in range(NP):
                        pe.matmul(OG[o, :], PT[:, g, j, o], Vp[:, n, j, :], start=(j == 0), stop=False)
                    mm = pe.matmul(OG[o, :], PTo[:, g, o], vs[:, :], start=False, stop=True)
                mm.then_inc(o_done, 1)

            pe.wait_ge(masks_ready, 1)
            for n in range(NS):
                score(n)
                if n == 5:
                    values(0)
            values(1)
            pe.wait_ge(om_ready, 2)
            for c in range(CC):
                for g in range(2):
                    mm = pe.matmul(AT[:, c * TS:(c + 1) * TS], Om[:, g, c * P:(c + 1) * P], selS[:, g, :],
                                   start=(g == 0), stop=(g == 1))
            mm.then_inc(at_done, 1)


NK = 128
TOP = 16
SLOTS = H * TOP
RING = 8
GRP = 1
DG = 4
NG = SLOTS // GRP
STEPS = 32
PLAN = [4] * 16 + [3, 3, 2, 2, 2, 2, 2] + [6] * 8 + [0]
LOWEST = -3.0e38
ONCE = 16 * 11
OA = 6
OV0, OVT = 357, 341


def tail(nc, I, O, S, K):
    with ExitStack() as ctx:
        sb = lambda n, s, d=F32: ctx.enter_context(nc.sbuf_tensor(n, s, d))
        sem = lambda n: ctx.enter_context(nc.semaphore("t_" + n))
        psum = lambda n, w: ctx.enter_context(nc.psum_tensor(n, [P, w], F32))
        ring = sb("ring", [P, RING, 2 * D])
        w_o = sb("w_o", [P, DC, D])
        wq = [sb(f"wq{i}", [P, DC, 2 * NK]) for i in range(2)]
        subk = sb("subk", [P, H, 2, NK])
        V = sb("V", [P, NB, DA])
        kh = [sb(f"kh{i}", [AUG, SEQ]) for i in range(2)]
        qTb = sb("t_qT", [AUG, H, P])
        gate = [sb(f"gate{i}", [P, D]) for i in range(2)]
        h2n = sb("h2n", [P, D])
        h2c = sb("h2c", [P, D])
        xb = sb("t_xb", [P, D])
        Pm = sb("t_Pm", [P, SEQ])
        PTs = sb("t_PT", [P, SEQ])
        fT = sb("fT", [P, DC, P])
        win = sb("win", [P, CC, P + W - 1])
        yac = sb("yac", [P, CC, P])
        mask = sb("mask", [P, SEQ], BF16)
        cw = sb("cw", [P, CC, W])
        cv = sb("cv", [P, 3, CC])
        ez = sb("ez", [P, CC, P])
        stt = sb("stt", [P, 2, 8])
        mx = sb("mx", [P, 3, H])
        rl = sb("rl", [P, H])
        act8 = sb("act8", [P, RING])
        ga = sb("ga", [P, RING])
        dg = sb("dg", [P, DG, P])
        idxn = sb("idxn", [P, SLOTS], I32)
        idxc = sb("idxc", [P, SLOTS], I32)
        gn = sb("gn", [P, H, TOP])
        gc = sb("gc", [P, SLOTS])
        gs = sb("gs", [P, 2, H])
        qh = sb("qh", [P, 2, P])
        sc = sb("sc", [P, 2, NK])
        sc2 = sb("sc2", [P, 2, NK])
        best = sb("best", [P, 2, TOP])
        bix = sb("bix", [P, 2, TOP], U32)
        cand = sb("cand", [P, 2, TOP, TOP])
        px = sb("px", [P, 3, TOP], U32)
        eq = sb("eq", [P, 2, TOP, TOP])
        ss = sb("sel2", [P, 2, TOP])
        io16 = sb("io16", [P, TOP])
        io16i = sb("io16i", [P, TOP], I32)
        top = sb("top", [P, H, TOP])
        SS, TT, YY = psum("SS", SEQ), psum("TT", SEQ), psum("YY", D)
        V0, M0 = psum("V0", 512), psum("M0", 512)

        once_in, cst, own_v, own_a = sem("once"), sem("cst"), sem("own_v"), sem("own_a")
        g_in = [sem(f"g{i}") for i in range(RING)]
        idx_copied, dot_done, gelu_done, diag_done, v_done = (sem("idxc"), sem("dot"), sem("gelu"), sem("diag"), sem("v"))
        carrier_v, carrier, ue_free, yg_done = sem("carrier_v"), sem("carrier"), sem("ue_free"), sem("yg")
        q_in, win_in, mask_in, x_in = sem("q_in"), sem("win_in"), sem("mask_in"), sem("x_in")
        k_in = [sem(f"k{i}") for i in range(2)]
        wq_in = [sem(f"wq{i}") for i in range(2)]
        gate_in = [sem(f"gate{i}") for i in range(2)]
        x1_out, x1_in, y_out, m_out = sem("x1_out"), sem("x1_in"), sem("y_out"), sem("m_out")
        s_done, m_ready, e_done, pt_done, pts_ready, pv_done = (sem("s"), sem("m"), sem("e"), sem("pt"), sem("pts"), sem("pv"))
        conv_done, yT_done, y_sum, nmu_ready, ssq_ready = sem("conv"), sem("yT"), sem("ysum"), sem("nmu"), sem("ssq")
        ms_ready, r0_ready, att_ready, yn_ready = sem("ms"), sem("r0"), sem("att"), sem("yn")
        attT_done, ynT_done, attT_ready, z_ready, catc_ready = sem("attT"), sem("ynT"), sem("attTr"), sem("z"), sem("catc")
        wo_done, x1_ready, ss_ready, xs_ready, x1T_done = sem("wo"), sem("x1"), sem("ss"), sem("xs"), sem("x1T")
        fT_ready, h2_done, h2_ready = sem("fTr"), sem("h2d"), sem("h2")
        qd_done, qh_ready, sc_done, sc_ready = sem("qd"), sem("qh"), sem("scd"), sem("scr")
        idx_ready, sh_ready, eg_ready, route_ready, cur_ready = sem("idx"), sem("shr"), sem("eg"), sem("route"), sem("cur")
        sc_free, y_ready, st_in, stT_done, ue_ready = sem("scf"), sem("y"), sem("st_in"), sem("stT"), sem("ue")
        ident = K["ident"]
        state = ring[0:120, 0, 0:2 * DA].rearrange("p (g c) -> p g c", g=2)
        ue = ring[:, 1, 0:CC * NS * (W - 1 + QS)].rearrange("p (c n w) -> p c n w", c=CC, n=NS)
        modT, sgT = K["modT"], K["sgT"]
        block = ctx.enter_context(nc.Block())

        @block.sync
        def _(sp):
            loads = ((w_o[:, :, :], I["w_o"].rearrange("(k p) n -> p k n", p=P)),
                     (subk[:, :, :, :], I["subkT"]), (cw[:, :, :], I["conv_wT"]), (cv[:, :, :], I["conv_v"]),
                     (fT[:, 0:CC, 0:TS], S["attTs"]), (ue[:, :, :, W - 1:], S["uTs"].rearrange("p c (n q) -> p c n q", n=NS)),
                     (state, I["state_conv"].rearrange("n w c -> (n w) c").rearrange("(g p) c -> p g c", g=2)),
                     (xb[0:TS, :], I["x_sample"]), (gate[0][0:TS, :], S["gate_s"][0]), (gate[1][0:TS, :], S["gate_s"][1]),
                     (V[:, :, :], O["v_prompt"].rearrange("(b p) n -> p b n", p=P)))
            for dst, src in loads[4:] + loads[:4]:
                sp.dma_start(dst, src).then_inc(once_in, 16)
            wqv = I["w_query"].rearrange("(k p) n -> p k n", p=P)

            def load_wq(t, h):
                n = H * t + h
                if n >= 2:
                    sp.wait_ge(qd_done, n - 1)
                sp.dma_start(wq[n % 2][:, :, :], wqv[:, :, h * 2 * NK:(h + 1) * 2 * NK]).then_inc(wq_in[n % 2], 16)

            def load_k(t, h):
                n, nk = H * (t - 1) + h, keys_of(t)
                if n >= 2:
                    sp.wait_ge(s_done, n - 1)
                sp.dma_start(kh[n % 2][:, 0:nk], S["kT"][:, h, 0:nk]).then_inc(k_in[n % 2], 16)

            def prefetch(t):
                b, nk = t - 1, keys_of(t)
                if t >= 2:
                    sp.wait_ge(s_done, H * (t - 1))
                    sp.wait_ge(m_ready, H * (t - 1))
                    sp.wait_ge(conv_done, t)
                sp.dma_start(qTb[:, :, :], S["qT"][:, :, b * P:(b + 1) * P]).then_inc(q_in, 16)
                sp.dma_start(mask[:, 0:nk], S["mask"][:, SEQ - P - b * P:SEQ - P - b * P + nk]).then_inc(mask_in, 16)
                sp.dma_start(win[:, :, :], S["uT"][:, :, b * P:b * P + P + W - 1]).then_inc(win_in, 16)
                load_k(t, 0)
                load_k(t, 1)

            def tail_io(t):
                r = rows(t)
                for h in range(2, H if t else 0):
                    load_k(t, h)
                if t:
                    sp.wait_ge(xs_ready, t)
                    sp.wait_ge(x1_out, 16 * t)
                    sp.dma_start(xb[:, :], I["x_prompt"][(t - 1) * P:t * P, :]).then_inc(x_in, 16)
                if t == 1:
                    sp.dma_start(gate[0][:, :], S["gate"][0]).then_inc(gate_in[0], 16)
                load_wq(t, 0)
                load_wq(t, 1)
                sp.wait_ge(x1_ready, t + 1)
                sp.dma_start(S["x1"][t, 0:r, :], xb[0:r, :]).then_inc(x1_out, 16)
                if t:
                    e = t - 1
                    sp.wait_ge(x1_out, 16 * (t + 1))
                    sp.dma_start(PTs[0:rows(e), :], S["x1"][e, 0:rows(e), :]).then_inc(x1_in, 16)
                for h in range(2, H):
                    load_wq(t, h)
                if t < NB:
                    prefetch(t + 1)

            def store_y(e):
                sp.wait_ge(y_ready, e + 1)
                dst = O["y_sample"] if e == 0 else O["y_prompt"][(e - 1) * P:e * P, :]
                sp.dma_start(dst, Pm[0:rows(e), :]).then_inc(y_out, 16)

            tail_io(0)
            for i in range(1, NB + 1):
                tail_io(i)
                store_y(i - 1)
                if i == 1:
                    sp.dma_start(gate[1][:, :], S["gate"][1]).then_inc(gate_in[1], 16)
            sp.dma_start(PTs[:, :], S["x1"][NB, :, :]).then_inc(x1_in, 16)
            store_y(NB)
            sp.wait_ge(y_out, 16 * (NB + 1))

        @block.gpsimd
        def _(pool):
            pool.iota(io16i[:, :], [[1, TOP]], base=0, channel_multiplier=0).then_inc(cst, 1)

            def experts(e, r):
                pool.wait_ge(idx_ready, 8 * e + 8)
                pool.sem_inc(carrier, 1)
                half = SLOTS // 2
                for k in range(NG):
                    if k in (0, NG // 2):
                        o = slice(0, half) if k == 0 else slice(half, SLOTS)
                        pool.tensor_copy(idxc[0:r, o], idxn[0:r, o]).then_inc(idx_copied, 1)
                        pool.wait_ge(idx_copied, 2 * e + (1 if k == 0 else 2))
                    n = NG * e + k
                    if not isinstance(e, int) or n >= RING // GRP:
                        pool.wait_ge(v_done, n - RING // GRP + 1)
                    elif e == 0 and k == 0:
                        pool.wait_ge(ue_free, 1)
                    if k in (0, NG // 2) or not isinstance(e, int) or n >= RING // GRP:
                        pool.sem_inc(carrier, 1)
                    for j in range(GRP):
                        s = GRP * k + j
                        pool.indirect_dma_start(ring[0:r, s % RING, :], None, I["experts"],
                                                bass.IndirectOffsetOnAxis(idxc[0:r, s:s + 1], 0)).then_inc(g_in[s % RING], 16)

            experts(0, TS)
            with pool.Fori(1, NB + 1) as e:
                experts(e, P)

        @block.scalar
        def _(act):
            own = Own(act, own_a)

            def rsqrt(count, r, src, ln, out):
                act.wait_ge(ms_ready, count)
                own.do(act.activation(ln, src, ACT.Ln))
                act.activation(out, ln, ACT.Exp, scale=-0.5).then_inc(r0_ready, 1)

            def step(s, t, nk):
                r = rows(t)
                first = isinstance(t, int) and t == 0
                if s == 0:
                    own.start(OA * t)
                if s < 2 * H and not first:
                    n = H * (t - 1) + s // 2 + 1
                    if s % 2 == 0:
                        act.wait_ge(m_ready, n)
                        act.activation(Pm[:, 0:nk], Pm[:, 0:nk], ACT.Exp, bias=mx[:, 1, s // 2:s // 2 + 1],
                                       accum_out=mx[:, 2, s // 2:s // 2 + 1]).then_inc(e_done, 1)
                    else:
                        act.wait_ge(pt_done, n)
                        act.activation(PTs[:, 0:nk], TT[:, 0:nk], ACT.Copy).then_inc(pts_ready, 1)
                if s == 16:
                    yl = PTs[0:r, 512:1024]
                    act.wait_ge(yT_done, t + 1)
                    act.activation(yl, M0[0:r, :], ACT.Identity, accum_out=stt[0:r, 0, 0:1]).then_inc(y_sum, 1)
                    act.wait_ge(nmu_ready, t + 1)
                    act.activation(PTs[0:r, 0:512], yl, ACT.Square, bias=stt[0:r, 0, 1:2],
                                   accum_out=stt[0:r, 0, 2:3]).then_inc(ssq_ready, 1)
                    rsqrt(2 * t + 1, r, stt[0:r, 0, 3:4], stt[0:r, 0, 4:5], stt[0:r, 0, 5:6])
                if s == 17:
                    if not first:
                        act.wait_ge(attT_done, t)
                        act.activation(fT[:, 0:CC, :], SS[:, 0:512].rearrange("p (c t) -> p c t", c=CC),
                                       ACT.Copy).then_inc(attT_ready, 1)
                    act.wait_ge(ynT_done, t + 1)
                    for c in range(CC):
                        own.step(act.activation(ez[:, c, 0:r], M0[:, c * P:c * P + r], ACT.Identity,
                                                scale=cv[:, 1, c:c + 1], bias=cv[:, 2, c:c + 1]))
                    own.settle()
                    act.activation(yac[:, :, 0:r], ez[:, :, 0:r], ACT.Exp, scale=-1.0).then_inc(z_ready, 1)
                if s == 18:
                    act.wait_ge(x1_ready, t + 1)
                    act.activation(Pm[0:r, :], xb[0:r, :], ACT.Square, accum_out=stt[0:r, 1, 2:3]).then_inc(ss_ready, 1)
                    rsqrt(2 * t + 2, r, stt[0:r, 1, 3:4], stt[0:r, 1, 4:5], stt[0:r, 1, 5:6])
                if s == 19 and not first:
                    act.wait_ge(x1T_done, t + 1)
                    for c in range(DC):
                        a = act.activation(fT[:, c, :], SS[:, c * P:(c + 1) * P], ACT.Identity,
                                           scale=sgT[:, 1, c, 0:1], bias=modT[:, 24 + c, 0:1])
                    a.then_inc(fT_ready, 1)
                if s == 20:
                    act.wait_ge(h2_done, t + 1)
                    if not first:
                        act.wait_ge(cur_ready, t)
                    act.activation(h2n[0:r, :], TT[0:r, :], ACT.Copy).then_inc(h2_ready, 1)
                if 21 <= s < 29:
                    act.wait_ge(qd_done, H * t + s - 20)
                    act.activation(qh[:, :, 0:r], M0[:, 0:2 * P].rearrange("p (g t) -> p g t", g=2)[:, :, 0:r],
                                   ACT.Copy).then_inc(qh_ready, 1)
                if 22 <= s < 30:
                    act.wait_ge(sc_done, H * t + s - 21)
                    if not first or s > 22:
                        act.wait_ge(sc_free, H * t + s - 22)
                    act.activation(sc[0:r, :, :].rearrange("p g k -> p (g k)"), V0[0:r, 0:2 * NK],
                                   ACT.Copy).then_inc(sc_ready, 1)
                if s == 31:
                    act.wait_ge(sh_ready, t + 1)
                    act.activation(gn[0:r, :, :], top[0:r, :, :], ACT.Exp).then_inc(eg_ready, 1)
                    assert own.n == OA, own.n

            def gelu(e, k, r):
                act.wait_ge(dot_done, SLOTS * e + GRP * (k + 1))
                a = GRP * k % RING
                act.activation(ga[0:r, a:a + GRP], act8[0:r, a:a + GRP], ACT.Gelu).then_inc(gelu_done, 1)

            iterate(act, step, gelu, lambda e, r: None, lambda e, r: None, prologue=lambda: act.wait_ge(once_in, ONCE))

        @block.vector
        def _(v):
            own = Own(v, own_v)
            own.carrier = carrier_v

            def newton(m, r0, a, b, out):
                own.do(v.tensor_tensor(a, r0, r0, ALU.mult))
                own.do(v.tensor_tensor(b, a, m, ALU.mult))
                own.do(v.tensor_scalar(a, b, -0.5, 1.5, ALU.mult, ALU.add))
                own.do(v.tensor_tensor(out, a, r0, ALU.mult))

            def taps(ks, r, rows_of, out_of):
                for k in ks:
                    for c in range(CC):
                        if k:
                            v.wait_ge(own.sem, own.base + own.n - CC + 1)
                            own.step(v.scalar_tensor_tensor(out_of(c), rows_of(c, k), cw[:, c, k:k + 1], out_of(c),
                                                            ALU.mult, ALU.add))
                        else:
                            own.step(v.tensor_scalar(out_of(c), rows_of(c, k), cw[:, c, 0:1], cv[:, 0, c:c + 1],
                                                     ALU.mult, ALU.add))

            def modulate(r):
                v.wait_ge(x1T_done, 1)
                for c in range(DC):
                    o = fT[:, c, 0:r].rearrange("p (n q) -> p n q", n=NS)
                    i = SS[:, c * P:c * P + r].rearrange("p (n q) -> p n q", n=NS)
                    own.do(v.tensor_tensor(o, i, sgT[:, 1, c, 1:M].unsqueeze(2).to_broadcast([P, NS, QS]), ALU.mult))
                    own.do(v.tensor_tensor(o, o, modT[:, 24 + c, 1:M].unsqueeze(2).to_broadcast([P, NS, QS]), ALU.add))
                v.sem_inc(fT_ready, 1)

            def choose(t, h, r):
                v.wait_ge(sc_ready, H * t + h + 1)
                own.carry()
                for g in range(2):
                    own.step(v.max(best[0:r, g, 0:8], sc[0:r, g, :]))
                own.settle()
                own.carry()
                for g in range(2):
                    own.step(v.max_index(bix[0:r, g, 0:8], best[0:r, g, 0:8], sc[0:r, g, :]))
                    own.step(v.match_replace(sc2[0:r, g, :], best[0:r, g, 0:8], sc[0:r, g, :], LOWEST))
                own.settle()
                v.sem_inc(sc_free, 1)
                for g in range(2):
                    own.step(v.max(best[0:r, g, 8:16], sc2[0:r, g, :]))
                own.settle()
                own.carry()
                for g in range(2):
                    own.step(v.max_index(bix[0:r, g, 8:16], best[0:r, g, 8:16], sc2[0:r, g, :]))
                own.do(v.tensor_tensor(cand[0:r, 0, :, :], best[0:r, 0, :].unsqueeze(2).to_broadcast([r, TOP, TOP]),
                                       best[0:r, 1, :].unsqueeze(1).to_broadcast([r, TOP, TOP]), ALU.add))
                c0 = cand[0:r, 0, :, :].rearrange("p i j -> p (i j)")
                c1 = cand[0:r, 1, :, :].rearrange("p i j -> p (i j)")
                own.carry()
                own.do(v.max(top[0:r, h, 0:8], c0))
                own.carry()
                own.step(v.max_index(px[0:r, 0, 0:8], top[0:r, h, 0:8], c0))
                own.do(v.match_replace(c1, top[0:r, h, 0:8], c0, LOWEST))
                own.carry()
                own.do(v.max(top[0:r, h, 8:16], c1))
                own.carry()
                own.do(v.max_index(px[0:r, 0, 8:16], top[0:r, h, 8:16], c1))
                own.step(v.tensor_scalar(px[0:r, 1, :], px[0:r, 0, :], 4, None, ALU.logical_shift_right))
                own.do(v.tensor_scalar(px[0:r, 2, :], px[0:r, 0, :], 15, None, ALU.bitwise_and))
                for g in range(2):
                    own.step(v.tensor_tensor(eq[0:r, g, :, :], px[0:r, 1 + g, :].unsqueeze(2).to_broadcast([r, TOP, TOP]),
                                             io16[0:r, :].unsqueeze(1).to_broadcast([r, TOP, TOP]), ALU.is_equal))
                own.settle()
                for g in range(2):
                    own.step(v.tensor_tensor(eq[0:r, g, :, :], eq[0:r, g, :, :],
                                             bix[0:r, g, :].unsqueeze(1).to_broadcast([r, TOP, TOP]), ALU.mult))
                own.settle()
                for g in range(2):
                    own.step(v.tensor_reduce(ss[0:r, g, :], eq[0:r, g, :, :], X, ALU.add))
                own.settle()
                if h == 0 and not (isinstance(t, int) and t == 0):
                    v.wait_ge(idx_copied, 2 * t)
                v.scalar_tensor_tensor(idxn[0:r, h * TOP:(h + 1) * TOP], ss[0:r, 0, :], float(NK), ss[0:r, 1, :],
                                       ALU.mult, ALU.add).then_inc(idx_ready, 1)

            def step(s, t, nk):
                r = rows(t)
                first = isinstance(t, int) and t == 0
                if s == 0:
                    own.start(0 if first else OV0 + OVT * (t - 1))
                    if first:
                        v.wait_ge(cst, 1)
                        own.do(v.tensor_copy(io16[:, :], io16i[:, :]))
                        v.wait_ge(stT_done, 1)
                        for g in range(2):
                            src = (SS, TT)[g][:, 0:CC * 120].rearrange("p (c n w) -> p c n w", c=CC, n=4)
                            for c in range(CC):
                                own.step(v.tensor_copy(ue[:, c, 4 * g:4 * g + 4, 0:W - 1], src[:, c, :, :]))
                        own.settle()
                        taps(range(W), r, lambda c, k: ue[:, c, :, k:k + QS],
                             lambda c: yac[:, c, 0:TS].rearrange("p (n q) -> p n q", n=NS))
                        own.settle()
                        v.sem_inc(conv_done, 1)
                        v.sem_inc(ue_free, 1)
                if s < 2 * H and not first:
                    h = s // 2
                    if s == 0:
                        v.wait_ge(win_in, 16 * t)
                    if s % 2 == 0:
                        n = H * (t - 1) + h + 1
                        if s == 0:
                            v.wait_ge(mask_in, 16 * t)
                            if not isinstance(t, int) or t > 1:
                                v.wait_ge(y_out, 16 * (t - 1))
                        else:
                            v.wait_ge(pt_done, n - 1)
                        v.wait_ge(s_done, n)
                        own.carry()
                        own.do(v.tensor_tensor_reduce(out=Pm[:, 0:nk], in0=SS[:, 0:nk], in1=mask[:, 0:nk], scale=1.0,
                                                      scalar=LOWEST, op0=ALU.add, op1=ALU.max,
                                                      accum_out=mx[:, 0, h:h + 1]))
                        v.tensor_scalar(mx[:, 1, h:h + 1], mx[:, 0, h:h + 1], -1.0, None, ALU.mult).then_inc(m_ready, 1)
                    if s == 0:
                        v.wait_ge(z_ready, t)
                    taps([k for k in (2 * s, 2 * s + 1) if k < W], r, lambda c, k: win[:, c, k:k + P],
                         lambda c: yac[:, c, :])
                    if s == 2 * H - 1:
                        own.settle()
                        v.sem_inc(conv_done, 1)
                if s == 16:
                    a = stt[0:r, 0, :]
                    v.wait_ge(y_sum, t + 1)
                    v.tensor_scalar(a[:, 1:2], a[:, 0:1], -1.0 / DA, None, ALU.mult).then_inc(nmu_ready, 1)
                    if not first:
                        v.wait_ge(e_done, H * t)
                        own.do(v.reciprocal(rl[:, :], mx[:, 2, :]))
                        v.wait_ge(pv_done, H * t)
                        v.tensor_tensor(Pm[:, 0:DA].rearrange("p (h d) -> p h d", h=H),
                                        V0[:, :].rearrange("p (h d) -> p h d", h=H),
                                        rl[:, :].unsqueeze(2).to_broadcast([P, H, HD]), ALU.mult).then_inc(att_ready, 1)
                    v.wait_ge(ssq_ready, t + 1)
                    v.tensor_scalar(a[:, 3:4], a[:, 2:3], 1.0 / DA, EPS, ALU.mult, ALU.add).then_inc(ms_ready, 1)
                    v.wait_ge(r0_ready, 2 * t + 1)
                    newton(a[:, 3:4], a[:, 5:6], a[:, 6:7], a[:, 7:8], a[:, 4:5])
                    v.tensor_scalar(Pm[0:r, 512:1024], PTs[0:r, 512:1024], a[:, 1:2], a[:, 4:5], ALU.add, ALU.mult)\
                        .then_inc(yn_ready, 1)
                if s == 17:
                    v.wait_ge(z_ready, t + 1)
                    own.do(v.tensor_scalar(yac[:, :, 0:r], yac[:, :, 0:r], 1.0, None, ALU.add))
                    own.do(v.reciprocal(yac[:, :, 0:r], yac[:, :, 0:r]))
                    v.tensor_tensor(fT[:, CC:DC, 0:r], ez[:, :, 0:r], yac[:, :, 0:r], ALU.mult).then_inc(catc_ready, 1)
                if s == 18:
                    a = stt[0:r, 1, :]
                    v.wait_ge(wo_done, t + 1)
                    if not first:
                        v.wait_ge(x_in, 16 * t)
                        v.wait_ge(gate_in[0], 16)
                    own.do(v.tensor_tensor(PTs[0:r, :], TT[0:r, :], gate[0][0:r, :], ALU.mult))
                    v.tensor_tensor(xb[0:r, :], xb[0:r, :], PTs[0:r, :], ALU.add).then_inc(x1_ready, 1)
                    v.wait_ge(ss_ready, t + 1)
                    v.tensor_scalar(a[:, 3:4], a[:, 2:3], 1.0 / D, EPS, ALU.mult, ALU.add).then_inc(ms_ready, 1)
                    v.wait_ge(r0_ready, 2 * t + 2)
                    newton(a[:, 3:4], a[:, 5:6], a[:, 6:7], a[:, 7:8], a[:, 4:5])
                    v.tensor_scalar(Pm[0:r, :], xb[0:r, :], a[:, 4:5], None, ALU.mult).then_inc(xs_ready, 1)
                if s == 19 and first:
                    modulate(r)
                if 23 <= s < 31:
                    choose(t, s - 23, r)
                if s == 31:
                    own.do(v.tensor_copy(gs[0:r, 0, :], top[0:r, :, 0]))
                    own.do(v.tensor_tensor(top[0:r, :, :], top[0:r, :, :],
                                           gs[0:r, 0, :].unsqueeze(2).to_broadcast([r, H, TOP]), ALU.subtract))
                    v.sem_inc(sh_ready, 1)
                    v.wait_ge(eg_ready, t + 1)
                    own.do(v.tensor_reduce(gs[0:r, 0, :], gn[0:r, :, :], X, ALU.add))
                    own.do(v.reciprocal(gs[0:r, 1, :], gs[0:r, 0, :]))
                    own.do(v.tensor_tensor(gn[0:r, :, :], gn[0:r, :, :],
                                           gs[0:r, 1, :].unsqueeze(2).to_broadcast([r, H, TOP]), ALU.mult))
                    assert own.n == (OV0 if first else OVT), own.n

            def begin(e, r):
                v.wait_ge(h2_ready, e + 1)
                v.tensor_copy(gc[0:r, :], gn[0:r, :, :].rearrange("p h k -> p (h k)"))
                v.tensor_copy(h2c[0:r, :], h2n[0:r, :]).then_inc(cur_ready, 1)
                v.wait_ge(cur_ready, e + 1)

            def diag(e, k, r):
                v.wait_ge(gelu_done, NG * e + k + 1)
                if not isinstance(e, int) or NG * e + k >= DG // GRP:
                    v.wait_ge(v_done, NG * e + k - DG // GRP + 1)
                for j in range(GRP):
                    s = GRP * k + j
                    a = v.tensor_scalar(dg[0:r, s % DG, 0:r], ident[0:r, 0:r], ga[0:r, s % RING:s % RING + 1],
                                        gc[0:r, s:s + 1], ALU.mult, ALU.mult)
                a.then_inc(diag_done, 1)

            def group(e, k, r):
                for j in range(GRP):
                    s = GRP * k + j
                    u = ring[0:r, s % RING, 0:D]
                    v.wait_ge(g_in[s % RING], 16 * (SLOTS // RING * e + s // RING + 1))
                    v.tensor_tensor_reduce(out=u, in0=u, in1=h2c[0:r, :], scale=1.0, scalar=0.0, op0=ALU.mult,
                                           op1=ALU.add, accum_out=act8[0:r, s % RING:s % RING + 1]).then_inc(dot_done, 1)
                if k:
                    diag(e, k - 1, r)

            def end(e, r):
                diag(e, NG - 1, r)
                v.wait_ge(v_done, NG * (e + 1))
                v.wait_ge(x1_in, 16 * (e + 1))
                if not isinstance(e, int) or e > 0:
                    v.wait_ge(gate_in[1], 16)
                v.tensor_tensor(Pm[0:r, :], YY[0:r, :], gate[1][0:r, :], ALU.mult).then_inc(yg_done, 1)
                v.wait_ge(yg_done, e + 1)
                v.tensor_tensor(Pm[0:r, :], Pm[0:r, :], PTs[0:r, :], ALU.add).then_inc(y_ready, 1)

            iterate(v, step, group, begin, end, prologue=lambda: v.wait_ge(once_in, ONCE))

        @block.tensor
        def _(pe):
            def weigh(h, t, nk):
                n = H * (t - 1) + h + 1
                pe.wait_ge(pts_ready, n)
                for b in range(nk // P):
                    mm = pe.matmul(V0[:, h * HD:(h + 1) * HD], PTs[:, b * P:(b + 1) * P], V[:, b, h * HD:(h + 1) * HD],
                                   start=(b == 0), stop=(b == nk // P - 1))
                mm.then_inc(pv_done, 1)

            def step(s, t, nk):
                r = rows(t)
                first = isinstance(t, int) and t == 0
                if s == 0 and first:
                    for g in range(2):
                        for c in range(CC):
                            mm = pe.transpose((SS, TT)[g][:, c * 120:(c + 1) * 120], state[:, g, c * P:(c + 1) * P],
                                              ident[0:120, 0:120])
                    mm.then_inc(stT_done, 1)
                if s < 2 * H and not first:
                    h = s // 2
                    n = H * (t - 1) + h + 1
                    if s % 2 == 0:
                        if h:
                            weigh(h - 1, t, nk)
                            pe.wait_ge(m_ready, n - 1)
                        else:
                            pe.wait_ge(q_in, 16 * t)
                            pe.wait_ge(fT_ready, t)
                            pe.wait_ge(sc_ready, H * t)
                        pe.wait_ge(k_in[h % 2], 64 * (t - 1) + 16 * (h // 2 + 1))
                        for b in range(nk // 512):
                            mm = pe.matmul(SS[:, b * 512:(b + 1) * 512], qTb[:, h, :], kh[h % 2][:, b * 512:(b + 1) * 512],
                                           start=True, stop=True)
                        mm.then_inc(s_done, 1)
                    else:
                        pe.wait_ge(e_done, n)
                        if h == 0:
                            pe.wait_ge(h2_ready, t)
                        for b in range(nk // P):
                            mm = pe.transpose(TT[:, b * P:(b + 1) * P], Pm[:, b * P:(b + 1) * P], ident[:, :])
                        mm.then_inc(pt_done, 1)
                if s == 16:
                    if not first:
                        weigh(H - 1, t, nk)
                    pe.wait_ge(conv_done, t + 1)
                    if not first:
                        pe.wait_ge(qh_ready, H * t)
                    for c in range(CC):
                        mm = pe.transpose(M0[0:r, c * P:(c + 1) * P], yac[:, c, 0:r], ident[:, :])
                    mm.then_inc(yT_done, 1)
                if s == 17:
                    if not first:
                        pe.wait_ge(att_ready, t)
                        for c in range(CC):
                            mm = pe.transpose(SS[:, c * P:(c + 1) * P], Pm[:, c * P:(c + 1) * P], ident[:, :])
                        mm.then_inc(attT_done, 1)
                    pe.wait_ge(yn_ready, t + 1)
                    for c in range(CC):
                        mm = pe.transpose(M0[:, c * P:c * P + r], Pm[0:r, 512 + c * P:512 + (c + 1) * P], ident[0:r, 0:r])
                    mm.then_inc(ynT_done, 1)
                if s == 18:
                    if not first:
                        pe.wait_ge(attT_ready, t)
                    pe.wait_ge(catc_ready, t + 1)
                    for g in range(2):
                        for k in range(DC):
                            mm = pe.matmul(TT[0:r, g * 512:(g + 1) * 512], fT[:, k, 0:r], w_o[:, k, g * 512:(g + 1) * 512],
                                           start=(k == 0), stop=(k == DC - 1))
                    mm.then_inc(wo_done, 1)
                if s == 19:
                    pe.wait_ge(xs_ready, t + 1)
                    for c in range(DC):
                        mm = pe.transpose(SS[:, c * P:c * P + r], Pm[0:r, c * P:(c + 1) * P], ident[0:r, 0:r])
                    mm.then_inc(x1T_done, 1)
                if s == 20:
                    pe.wait_ge(fT_ready, t + 1)
                    for c in range(DC):
                        mm = pe.transpose(TT[0:r, c * P:(c + 1) * P], fT[:, c, 0:r], ident[:, :])
                    mm.then_inc(h2_done, 1)
                if 22 <= s < 30:
                    n = H * t + s - 21
                    pe.wait_ge(qh_ready, n)
                    if not first or s > 22:
                        pe.wait_ge(sc_ready, n - 1)
                    for g in range(2):
                        mm = pe.matmul(V0[0:r, g * NK:(g + 1) * NK], qh[:, g, 0:r], subk[:, s - 22, g, :],
                                       start=True, stop=True)
                    mm.then_inc(sc_done, 1)
                if 21 <= s < 29:
                    h = s - 21
                    pe.wait_ge(wq_in[h % 2], 64 * t + 16 * (h // 2 + 1))
                    for g in range(2):
                        for k in range(DC):
                            mm = pe.matmul(M0[:, g * P:g * P + r], wq[h % 2][:, k, g * NK:(g + 1) * NK], fT[:, k, 0:r],
                                           start=(k == 0), stop=(k == DC - 1))
                    mm.then_inc(qd_done, 1)

            def sums(e, k, r):
                pe.wait_ge(diag_done, NG * e + k + 1)
                if k == 0 and (not isinstance(e, int) or e > 0):
                    pe.wait_ge(y_ready, e)
                for j in range(GRP):
                    s = GRP * k + j
                    for g in range(2):
                        mm = pe.matmul(YY[0:r, g * 512:(g + 1) * 512], dg[0:r, s % DG, 0:r],
                                       ring[0:r, s % RING, D + g * 512:D + (g + 1) * 512],
                                       start=(s == 0), stop=(s == SLOTS - 1), skip_group_check=True)
                mm.then_inc(v_done, 1)

            def group(e, k, r):
                if k:
                    sums(e, k - 1, r)

            iterate(pe, step, group, lambda e, r: None, lambda e, r: sums(e, NG - 1, r),
                    prologue=lambda: pe.wait_ge(once_in, ONCE))


def keys_of(t):
    return SEQ // 2 if t <= NB // 2 else SEQ


def iterate(eng, step, group, begin, end, prologue):
    def both(t, nk, r):
        begin(t - 1, r)
        for s in range(STEPS):
            step(s, t, nk)
            for k in range(sum(PLAN[:s]), sum(PLAN[:s + 1])):
                group(t - 1, k, r)
        end(t - 1, r)

    prologue()
    for s in range(STEPS):
        step(s, 0, 0)
    both(1, SEQ // 2, TS)
    with eng.Fori(2, NB // 2 + 1) as t:
        both(t, SEQ // 2, P)
    with eng.Fori(NB // 2 + 1, NB + 1) as t:
        both(t, SEQ, P)
    begin(NB, P)
    for k in range(NG):
        group(NB, k, P)
    end(NB, P)


def build(nc, I, O, S):
    with ExitStack() as ctx:
        K = {}
        for name, shape in (("ident", [P, P]), ("tri", [P, P]), ("ones", [P, P]), ("modT", [P, 48, M]),
                            ("sgT", [P, 2, DC, M])):
            K[name] = ctx.enter_context(nc.sbuf_tensor(name, shape, F32))
        condition(nc, I, S, K)
        project(nc, I, O, S, K)
        sampled(nc, I, O, S, K)
        tail(nc, I, O, S, K)


_OUTS = [("y_prompt", (SEQ, D)), ("y_sample", (TS, D)), ("k_prompt", (SEQ, DA)), ("v_prompt", (SEQ, DA)),
         ("logf_prompt", (SEQ, H)), ("conv_prompt", (W - 1, DA)), ("k_sample", (TS, DA)), ("v_sample", (TS, DA)),
         ("logf_sample", (TS, H)), ("conv_sample", (NS, W - 1, DA))]
_SHAPES = [(1, SEQ, D), (NS, QS, D), (1, 1, SEQ, H, HD), (1, 1, SEQ, H, HD), (1, 1, SEQ, H), (1, 1, W - 1, DA),
           (1, NS, QS, H, HD), (1, NS, QS, H, HD), (1, NS, QS, H), (1, NS, W - 1, DA)]
_SCRATCH = {"uT": (P, CC, W - 1 + SEQ), "uTs": (P, CC, TS), "qT": (AUG, H, SEQ), "kT": (AUG, H, SEQ),
            "qTs": (P, CC, TS), "kTs": (P, CC, TS), "attTs": (P, CC, TS), "x1": (NB + 1, P, D),
            "gate": (2, P, D), "gate_s": (2, TS, D)}


def kernel(**inputs):
    import numpy as np
    import concourse.bacc as _bacc
    from concourse.bass_utils import run_bass_kernel_spmd as _run

    g = {n: np.asarray(a) for n, a in inputs.items()}
    col = lambda a: np.ascontiguousarray(a.reshape(-1, P).T)
    arrays = {
        "x_prompt": g["x_prompt"].reshape(SEQ, D), "x_sample": g["x_sample"].reshape(TS, D),
        "cT": np.concatenate([g["c_prompt"], g["c_sample"]]).reshape(M, DC, P).transpose(2, 1, 0),
        "w_ada": g["w_ada"][0], "b_adaT": col(g["b_ada"][0]),
        "norm_gT": np.stack([g["norm1_g"][0].reshape(DC, P).T, g["norm2_g"][0].reshape(DC, P).T], axis=1),
        "w_in": g["w_in"][0], "q_g": g["q_norm_g"], "k_g": g["k_norm_g"], "b_f": g["b_f"],
        "b_gluT": g["b_glu"][0].reshape(2, CC, P).transpose(2, 0, 1),
        "state_conv": g["state_conv"][0],
        "w_o": g["w_o"][0], "w_query": g["peer_w_query"][0],
        "subkT": g["peer_sub_keys"][0].transpose(3, 0, 1, 2), "conv_wT": g["conv_w"][0].reshape(W, CC, P).transpose(2, 1, 0),
        "conv_v": np.stack([g[n][0].reshape(CC, P).T for n in ("conv_b", "conv_ln_g", "conv_ln_b")], axis=1),
        "experts": np.concatenate([g["peer_u"][0], g["peer_v"][0]], axis=1),
        "cache_k": g["cache_k"][0].reshape(-1, DA), "cache_v": g["cache_v"][0].reshape(-1, DA),
        "cache_logf": g["cache_logf"][0].reshape(-1, H), "page_table": g["page_table"].reshape(1, -1),
    }
    nc = _bacc.Bacc("TRN2", target_bir_lowering=False, num_devices=1)
    feed, I = {}, {}
    for n, a in arrays.items():
        feed[f"{n}_dram"] = a = np.ascontiguousarray(a)
        I[n] = nc.dram_tensor(f"{n}_dram", a.shape, mybir.dt.from_np(a.dtype), kind="ExternalInput").ap()
    O = {n: nc.dram_tensor(f"{n}_dram_out", s, F32, kind="ExternalOutput").ap() for n, s in _OUTS}
    S = {n: nc.dram_tensor(f"{n}_scratch", s, F32, kind="Internal").ap() for n, s in _SCRATCH.items()}
    S["mask"] = nc.dram_tensor("mask_scratch", (P, 2 * SEQ - P), BF16, kind="Internal").ap()
    build(nc, I, O, S)
    r = _run(nc, [feed], core_ids=[0])
    return tuple(r.results[0][f"{n}_dram_out"].reshape(s) for (n, _), s in zip(_OUTS, _SHAPES))
```

```python
from contextlib import ExitStack

import concourse.bass as bass
from concourse import mybir

F32 = mybir.dt.float32
BF16 = mybir.dt.bfloat16
I32 = mybir.dt.int32
U32 = mybir.dt.uint32
ALU = mybir.AluOpType
ACT = mybir.ActivationFunctionType
X = mybir.AxisListType.X

P = 128
D = 1024
DC = D // P
SEQ = 1024
NB = SEQ // P
NS = 8
QS = 4
TS = NS * QS
H = 8
HD = 64
DA = H * HD
CC = 4
W = 31
ZQ, ZK, ZV, ZF, ZG = 0, DA, 2 * DA, 3 * DA, 3 * DA + H
DIN = 3 * DA + H + 2 * CC * P
M = 1 + NS
EPS = 1e-6
AUG = HD + 2


def rows(t):
    return TS if isinstance(t, int) and t == 0 else P


class Own:

    def __init__(self, eng, sem):
        self.eng, self.sem, self.base, self.n = eng, sem, 0, 0

    def start(self, base):
        self.base, self.n = base, 0

    def step(self, ins):
        ins.then_inc(self.sem, 1)
        self.n += 1

    def settle(self):
        self.eng.wait_ge(self.sem, self.base + self.n)

    def carry(self):
        self.eng.sem_inc(self.carrier, 1)

    def do(self, ins):
        self.step(ins)
        self.settle()


def condition(nc, I, S, K):
    with ExitStack() as ctx:
        sb = lambda n, s, d=F32: ctx.enter_context(nc.sbuf_tensor(n, s, d))
        sem = lambda n: ctx.enter_context(nc.semaphore(n))
        wa = [sb(f"wa{i}", [P, DC, 512]) for i in range(3)]
        cT = sb("cT", [P, DC, M])
        bT = sb("bT", [P, 48])
        ng = sb("ng", [P, 2, DC])
        gS, gate, gate_s = sb("gS", [P, 2, DC, TS]), sb("gate", [P, 2, D]), sb("gate_s", [TS, 2, D])
        wide = sb("wide", [P, 2 * SEQ - P], BF16)
        mod_bank = ctx.enter_context(nc.psum_tensor("mod_bank", [P, 512], F32))
        mod_ps = mod_bank[:, 0:48 * M].rearrange("p (n m) -> p n m", m=M)
        gate_ps = [ctx.enter_context(nc.psum_tensor(f"gate_ps{i}", [P, 512], F32)) for i in range(4)]
        w_in = [sem(f"c_w{i}") for i in range(3)]
        small_in, w_used, id_step = sem("c_small"), sem("c_used"), sem("c_id")
        own_v, gates, gates_out = sem("c_own"), sem("c_gates"), sem("c_gout")
        stored = sem("c_stored")
        wv = I["w_ada"].rearrange("(k p) n -> p k n", p=P)
        modT, sgT, ident = K["modT"], K["sgT"], K["ident"]
        NCH = 12
        block = ctx.enter_context(nc.Block())

        @block.sync
        def _(sp):
            sp.dma_start(cT[:, :, :], I["cT"]).then_inc(small_in, 16)
            sp.dma_start(bT[:, :], I["b_adaT"]).then_inc(small_in, 16)
            sp.dma_start(ng[:, :, :], I["norm_gT"]).then_inc(small_in, 16)
            for n in range(NCH):
                if n >= 3:
                    sp.wait_ge(w_used, n - 2)
                sp.dma_start(wa[n % 3][:, :, :], wv[:, :, n * 512:(n + 1) * 512]).then_inc(w_in[n % 3], 16)
            sp.wait_ge(id_step, 7)
            sp.dma_start(S["mask"], wide[:, :]).then_inc(stored, 16)
            sp.wait_ge(gates_out, 2)
            for g in range(2):
                sp.dma_start(S["gate"][g], gate[:, g, :]).then_inc(stored, 16)
                sp.dma_start(S["gate_s"][g], gate_s[:, g, :]).then_inc(stored, 16)
            sp.wait_ge(stored, 16 * 5)

        @block.gpsimd
        def _(pool):
            pool.memset(ident[:, :], 0.0).then_inc(id_step, 1)
            pool.memset(K["tri"][:, :], 1.0).then_inc(id_step, 1)
            pool.memset(K["ones"][:, :], 1.0).then_inc(id_step, 1)
            pool.memset(wide[:, :], 0.0).then_inc(id_step, 1)
            pool.wait_ge(id_step, 4)
            pool.affine_select(out=ident[:, :], in_=ident[:, :], compare_op=ALU.not_equal, fill=1.0, base=0,
                               pattern=[[-1, P]], channel_multiplier=1).then_inc(id_step, 1)
            pool.affine_select(out=K["tri"][:, :], in_=K["tri"][:, :], compare_op=ALU.is_ge, fill=0.0, base=0,
                               pattern=[[1, P]], channel_multiplier=-1).then_inc(id_step, 1)
            pool.affine_select(out=wide[:, :], in_=wide[:, :], compare_op=ALU.is_ge, fill=-1e30, base=SEQ - P,
                               pattern=[[-1, 2 * SEQ - P]], channel_multiplier=1).then_inc(id_step, 1)

        @block.tensor
        def _(pe):
            pe.wait_ge(small_in, 48)
            for n in range(NCH):
                pe.wait_ge(w_in[n % 3], 16 * (n // 3 + 1))
                for j in range(4):
                    for k in range(DC):
                        mm = pe.matmul(mod_ps[:, 4 * n + j, :], wa[n % 3][:, k, j * P:(j + 1) * P], cT[:, k, :],
                                       start=(k == 0), stop=(k == DC - 1))
                mm.then_inc(w_used, 1)

            pe.wait_ge(own_v, 1)
            pe.wait_ge(id_step, 6)
            for g, first in ((0, 16), (1, 40)):
                for half in range(2):
                    for c in range(4):
                        mm = pe.matmul(gate_ps[2 * g + half][:, c * P:(c + 1) * P],
                                       modT[:, first + 4 * half + c, 0:1].to_broadcast([P, P]),
                                       ident[:, :], start=True, stop=True)
            mm.then_inc(gates, 1)
            pe.wait_ge(gates_out, 1)
            for g, first in ((0, 16), (1, 40)):
                for half in range(2):
                    for c in range(4):
                        mm = pe.matmul(gate_ps[2 * g + half][0:TS, c * P:(c + 1) * P],
                                       gS[:, g, 4 * half + c, :],
                                       ident[:, :], start=True, stop=True)
            mm.then_inc(gates, 1)

        @block.vector
        def _(v):
            own = Own(v, own_v)
            v.wait_ge(w_used, NCH)
            own.do(v.tensor_tensor(modT[:, :, :], mod_ps[:, :, :],
                                   bT[:, :].unsqueeze(2).to_broadcast([P, 48, M]), ALU.add))
            for i, first in ((0, 8), (1, 32)):
                own.do(v.tensor_scalar(sgT[:, i, :, :], modT[:, first:first + DC, :], 1.0, None, ALU.add))
                own.do(v.tensor_tensor(sgT[:, i, :, :], sgT[:, i, :, :],
                                       ng[:, i, :].unsqueeze(2).to_broadcast([P, DC, M]), ALU.mult))
                for c in range(DC):
                    fr = modT[:, (16, 40)[i] + c, 1:M].unsqueeze(2).to_broadcast([P, NS, QS])
                    own.do(v.tensor_copy(gS[:, i, c, :].rearrange("p (n q) -> p n q", n=NS), fr))
            v.wait_ge(gates, 1)
            for g in range(2):
                for half in range(2):
                    own.do(v.tensor_copy(gate[:, g, half * 512:(half + 1) * 512], gate_ps[2 * g + half][:, :]))
            v.sem_inc(gates_out, 1)
            v.wait_ge(gates, 2)
            for g in range(2):
                for half in range(2):
                    own.do(v.tensor_copy(gate_s[0:TS, g, half * 512:(half + 1) * 512],
                                         gate_ps[2 * g + half][0:TS, :]))
            v.sem_inc(gates_out, 1)


def project(nc, I, O, S, K):
    with ExitStack() as ctx:
        sb = lambda n, s, d=F32: ctx.enter_context(nc.sbuf_tensor(n, s, d))
        sem = lambda n: ctx.enter_context(nc.semaphore(n))
        w_in = sb("w_in", [P, DC, DIN])
        xb = sb("xb", [P, D])
        xs = sb("xs", [P, D])
        sqx = sb("sqx", [P, D])
        sqq = sb("sqq", [P, 2 * DA])
        hT = sb("hT", [P, DC, P])
        st = sb("st", [P, 8])
        sh = sb("sh", [P, 8, 2 * H])
        lf = sb("lf", [P, 8, H])
        lacc = sb("lacc", [P, H])
        qa = sb("qa", [P, H, AUG])
        ka = sb("ka", [P, H, AUG])
        vb = sb("vb", [P, DA])
        qTb = sb("qTb", [P, H, P])
        kTb = sb("kTb", [P, H, P])
        eg = sb("eg", [P, CC, P])
        uT = sb("uT", [P, CC, P])
        ub = sb("ub", [P, DA])
        gq = sb("gq", [P, HD])
        gk = sb("gk", [P, HD])
        bf = sb("bf", [P, H])
        bg = sb("bg", [P, 2, CC])
        nbg = sb("nbg", [P, CC])
        zero = sb("zero", [P, CC, W - 1])
        A = [ctx.enter_context(nc.psum_tensor(f"A{i}", [P, 512], F32)) for i in range(8)]

        w_sem, small_in, x_in = sem("p_w"), sem("p_small"), sem("p_x")
        ss_ready, ms_ready, r0_ready, xs_ready = sem("p_ss"), sem("p_ms"), sem("p_r0"), sem("p_xs")
        xT_done, hT_ready, qkv_done, fg_done, glu_done = sem("p_xT"), sem("p_hT"), sem("p_qkv"), sem("p_fg"), sem("p_glu")
        sqq_ready, hms_ready, hr0_ready, qk_ready = sem("p_sqq"), sem("p_hms"), sem("p_hr0"), sem("p_qk")
        v_ready, la_ready, lln_ready, logf_ready = sem("p_v"), sem("p_la"), sem("p_lln"), sem("p_logf")
        F_done, Fq_ready, qkT_done, qkT_ready = sem("p_F"), sem("p_Fq"), sem("p_qkT"), sem("p_qkTr")
        eg_ready, u_ready, uTT_done, ub_ready = sem("p_eg"), sem("p_u"), sem("p_uTT"), sem("p_ub")
        stored_k, stored_v, stored_l, stored_qk, stored_u = sem("p_ok"), sem("p_ov"), sem("p_ol"), sem("p_oqk"), sem("p_ou")
        once_out = sem("p_once")
        ubs_ready, ubs_out, cst2 = sem("p_ubs"), sem("p_ubso"), sem("p_cst2")
        own_v, own_a, own_p, cst = sem("p_ownv"), sem("p_owna"), sem("p_ownp"), sem("p_cst")
        OV, OA = 17, 1
        OVN, OAN = 4, 1
        ident = K["ident"]
        block = ctx.enter_context(nc.Block())

        @block.sync
        def _(sp):
            sp.dma_start(xb[0:TS, :], I["x_sample"]).then_inc(x_in, 16)
            sp.dma_start(w_in[:, :, :], I["w_in"].rearrange("(k p) n -> p k n", p=P)).then_inc(w_sem, 16)
            for dst, src in ((gq[:, :], I["q_g"].to_broadcast([P, HD])), (gk[:, :], I["k_g"].to_broadcast([P, HD])),
                             (bf[:, :], I["b_f"].to_broadcast([P, H])), (bg[:, :, :], I["b_gluT"])):
                sp.dma_start(dst, src).then_inc(small_in, 16)
            sp.dma_start(O["conv_sample"][:, 0:W - 1 - QS, :], I["state_conv"][:, QS:W - 1, :]).then_inc(once_out, 16)
            sp.wait_ge(cst, 1)
            sp.dma_start(S["uT"][:, :, 0:W - 1], zero[:, :, :]).then_inc(once_out, 16)

            def load_x(t, at):
                sp.wait_ge(xs_ready, t)
                sp.dma_start(xb[:, :], I["x_prompt"][bass.ds(at, P), :]).then_inc(x_in, 16)

            def store(t, n, at, u_at):
                r = rows(t)
                sp.wait_ge(v_ready, n)
                if r == TS:
                    sp.dma_start(O["v_sample"], vb[0:r, :]).then_inc(stored_v, 16)
                else:
                    sp.dma_start(O["v_prompt"][bass.ds(at, P), :], vb[:, :]).then_inc(stored_v, 16)
                sp.wait_ge(logf_ready, n)
                if r == TS:
                    sp.dma_start(O["logf_sample"], lf[0:r, 5, :]).then_inc(stored_l, 16)
                else:
                    sp.dma_start(O["logf_prompt"][bass.ds(at, P), :], lf[:, 5, :]).then_inc(stored_l, 16)
                sp.wait_ge(qk_ready, n)
                if r == TS:
                    sp.dma_start(O["k_sample"].rearrange("t (h d) -> t h d", h=H), ka[0:r, :, 0:HD]).then_inc(stored_k, 16)
                else:
                    sp.dma_start(O["k_prompt"][bass.ds(at, P), :].rearrange("t (h d) -> t h d", h=H),
                                 ka[:, :, 0:HD]).then_inc(stored_k, 16)
                sp.wait_ge(u_ready, n)
                if r == TS:
                    sp.dma_start(S["uTs"], uT[:, :, 0:TS]).then_inc(stored_u, 16)
                else:
                    sp.dma_start(S["uT"][:, :, bass.ds(u_at, P)], uT[:, :, :]).then_inc(stored_u, 16)
                sp.wait_ge(qkT_ready, n)
                if r == TS:
                    sp.dma_start(S["qTs"], qTb[:, 0:CC, 0:TS]).then_inc(stored_qk, 16)
                    sp.dma_start(S["kTs"], kTb[:, 0:CC, 0:TS]).then_inc(stored_qk, 16)
                else:
                    sp.dma_start(S["qT"][:, :, bass.ds(at, P)], qTb[0:AUG, :, :]).then_inc(stored_qk, 16)
                    sp.dma_start(S["kT"][:, :, bass.ds(at, P)], kTb[0:AUG, :, :]).then_inc(stored_qk, 16)

            load_x(1, 0)
            store(0, 1, None, None)
            sp.wait_ge(ubs_ready, 1)
            sp.dma_start(O["conv_sample"][:, W - 1 - QS:W - 1, :], ub[0:TS, :]).then_inc(ubs_out, 16)
            for t in range(1, NB):
                load_x(t + 1, t * P)
                store(t, t + 1, (t - 1) * P, (t - 1) * P + W - 1)
            store(NB, NB + 1, (NB - 1) * P, (NB - 1) * P + W - 1)
            sp.wait_ge(ub_ready, 1)
            sp.dma_start(O["conv_prompt"], ub[P - (W - 1):P, :]).then_inc(once_out, 16)
            sp.wait_ge(once_out, 16 * 3)
            for s, n in ((stored_k, 1), (stored_v, 1), (stored_l, 1), (stored_u, 1), (stored_qk, 2)):
                sp.wait_ge(s, 16 * n * (NB + 1))

        @block.gpsimd
        def _(pool):
            pool.memset(zero[:, :, :], 0.0).then_inc(cst, 1)
            pool.memset(lacc[:, :], 0.0).then_inc(own_p, 1)
            pool.memset(qa[:, :, HD + 1:AUG], 1.0).then_inc(own_p, 1)
            pool.memset(ka[:, :, HD:HD + 1], 1.0).then_inc(own_p, 1)
            pool.wait_ge(small_in, 64)
            pool.wait_ge(own_p, 3)
            pool.tensor_scalar(nbg[:, :], bg[:, 1, :], -1.0, None, ALU.mult).then_inc(own_p, 1)
            pool.tensor_scalar(gq[:, :], gq[:, :], HD ** -0.5, None, ALU.mult).then_inc(own_p, 1)

        @block.scalar
        def _(act):
            own = Own(act, own_a)

            def norm_x(t):
                r = rows(t)
                act.wait_ge(x_in, 16 * t + 16)
                act.activation(sqx[0:r, :], xb[0:r, :], ACT.Square, accum_out=st[0:r, 0:1]).then_inc(ss_ready, 1)
                act.wait_ge(ms_ready, t + 1)
                own.start(t)
                own.do(act.activation(st[0:r, 2:3], st[0:r, 1:2], ACT.Ln))
                act.activation(st[0:r, 3:4], st[0:r, 2:3], ACT.Exp, scale=-0.5).then_inc(r0_ready, 1)

            def body(t, more=True):
                r = rows(t)
                if r == P:
                    act.wait_ge(xT_done, t + 1)
                    for c in range(DC):
                        a = act.activation(hT[:, c, :], A[c // 4][:, (c % 4) * P:(c % 4 + 1) * P], ACT.Identity,
                                           scale=K["sgT"][:, 0, c, 0:1], bias=K["modT"][:, c, 0:1])
                    a.then_inc(hT_ready, 1)
                if more:
                    norm_x(t + 1)
                act.wait_ge(qkv_done, 3 * t + 3)
                act.activation(sqq[0:r, 0:DA], A[2][0:r, :], ACT.Square)
                act.activation(sqq[0:r, DA:2 * DA], A[3][0:r, :], ACT.Square).then_inc(sqq_ready, 1)
                if not isinstance(t, int) or t > 0:
                    act.wait_ge(stored_v, 16 * t)
                act.activation(vb[0:r, :], A[4][0:r, :], ACT.Copy).then_inc(v_ready, 1)
                act.wait_ge(hms_ready, t + 1)
                act.activation(sh[0:r, 2, :], sh[0:r, 1, :], ACT.Ln).then_inc(hr0_ready, 1)
                act.wait_ge(hr0_ready, 2 * t + 1)
                act.activation(sh[0:r, 3, :], sh[0:r, 2, :], ACT.Exp, scale=-0.5).then_inc(hr0_ready, 1)
                act.wait_ge(la_ready, t + 1)
                act.activation(lf[0:r, 2, :], lf[0:r, 1, :], ACT.Exp, scale=-1.0).then_inc(lln_ready, 1)
                act.wait_ge(lln_ready, 2 * t + 1)
                act.activation(lf[0:r, 3, :], lf[0:r, 2, :], ACT.Ln, bias=1.0).then_inc(lln_ready, 1)
                act.wait_ge(glu_done, t + 1)
                for c in range(CC):
                    a = act.activation(eg[:, c, 0:r], A[1][:, c * P:c * P + r], ACT.Exp, scale=-1.0,
                                       bias=nbg[:, c:c + 1])
                a.then_inc(eg_ready, 1)
                act.wait_ge(qkT_done, t + 1)
                if not isinstance(t, int) or t > 0:
                    act.wait_ge(stored_qk, 32 * t)
                if r == P:
                    for i, dst in enumerate((qTb, kTb)):
                        for g in range(2):
                            a = act.activation(dst[0:AUG, 4 * g:4 * g + 4, :].rearrange("p h t -> p (h t)"),
                                               A[2 + 2 * i + g][0:AUG, :], ACT.Copy)
                else:
                    for i, dst in enumerate((qTb, kTb)):
                        a = act.activation(dst[:, 0:CC, 0:TS],
                                           A[2 + 2 * i][:, 0:CC * TS].rearrange("p (c t) -> p c t", c=CC), ACT.Copy)
                a.then_inc(qkT_ready, 1)

            act.wait_ge(own_p, 5)
            norm_x(0)
            body(0)
            with act.Fori(1, NB) as t:
                body(t)
            body(NB, False)

        @block.vector
        def _(v):
            own = Own(v, own_v)

            def newton(m, r0, a, b, r):
                own.do(v.tensor_tensor(a, r0, r0, ALU.mult))
                own.do(v.tensor_tensor(b, a, m, ALU.mult))
                own.do(v.tensor_scalar(a, b, -0.5, 1.5, ALU.mult, ALU.add))
                return v.tensor_tensor(r, a, r0, ALU.mult)

            def norm_x(t):
                r = rows(t)
                v.wait_ge(ss_ready, t + 1)
                v.tensor_scalar(st[0:r, 1:2], st[0:r, 0:1], 1.0 / D, EPS, ALU.mult, ALU.add).then_inc(ms_ready, 1)
                v.wait_ge(r0_ready, t + 1)
                own.start(OVN * t + (0 if isinstance(t, int) and t == 0 else OV * (t - 1)))
                own.do(newton(st[0:r, 1:2], st[0:r, 3:4], st[0:r, 4:5], st[0:r, 5:6], st[0:r, 7:8]))
                if not isinstance(t, int) or t > 0:
                    v.wait_ge(xT_done, t)
                v.tensor_scalar(xs[0:r, :], xb[0:r, :], st[0:r, 7:8], None, ALU.mult).then_inc(xs_ready, 1)
                assert own.n == OVN

            def body(t, more=True):
                r = rows(t)
                if r == TS:
                    own.start(OVN)
                    v.wait_ge(xT_done, 1)
                    for g in range(2):
                        ps = A[g][:, :].rearrange("p (c n) -> p c n", c=4)
                        for c in range(4):
                            o = hT[:, 4 * g + c, 0:TS].rearrange("p (n q) -> p n q", n=NS)
                            i = ps[:, c, 0:TS].rearrange("p (n q) -> p n q", n=NS)
                            cc = 4 * g + c
                            v.tensor_tensor(o, i, K["sgT"][:, 0, cc, 1:M].unsqueeze(2).to_broadcast([P, NS, QS]),
                                            ALU.mult).then_inc(cst2, 1)
                            v.wait_ge(cst2, 2 * cc + 1)
                            v.tensor_tensor(o, o, K["modT"][:, cc, 1:M].unsqueeze(2).to_broadcast([P, NS, QS]),
                                            ALU.add).then_inc(cst2, 1)
                    v.wait_ge(cst2, 2 * DC)
                    v.sem_inc(hT_ready, 1)
                if more:
                    norm_x(t + 1)
                own.start(OVN * (t + 2) + OV * t if more else OVN * (t + 1) + OV * t)
                v.wait_ge(fg_done, t + 1)
                if not isinstance(t, int) or t > 0:
                    v.wait_ge(stored_l, 16 * t)
                own.do(v.tensor_tensor(lf[0:r, 0, :], A[5][0:r, 0:H], bf[0:r, :], ALU.add))
                own.do(v.tensor_scalar(lf[0:r, 4, :], lf[0:r, 0, :], -1.0, None, ALU.mult))
                v.tensor_tensor(lf[0:r, 1, :], lf[0:r, 0, :], lf[0:r, 4, :], ALU.max).then_inc(la_ready, 1)
                own.do(v.tensor_scalar(lf[0:r, 6, :], lf[0:r, 0, :], 0.0, None, ALU.min))
                v.wait_ge(sqq_ready, t + 1)
                own.do(v.tensor_reduce(sh[0:r, 0, :], sqq[0:r, :].rearrange("p (h d) -> p h d", d=HD), X, ALU.add))
                v.tensor_scalar(sh[0:r, 1, :], sh[0:r, 0, :], 1.0 / HD, EPS, ALU.mult, ALU.add).then_inc(hms_ready, 1)
                v.wait_ge(lln_ready, 2 * t + 2)
                own.settle()
                v.tensor_tensor(lf[0:r, 5, :], lf[0:r, 6, :], lf[0:r, 3, :], ALU.subtract).then_inc(logf_ready, 1)
                v.wait_ge(hr0_ready, 2 * t + 2)
                own.do(newton(sh[0:r, 1, :], sh[0:r, 3, :], sh[0:r, 4, :], sh[0:r, 5, :], sh[0:r, 7, :]))
                if not isinstance(t, int) or t > 0:
                    v.wait_ge(stored_k, 16 * t)
                    v.wait_ge(qkT_done, t)
                for i, (dst, g) in enumerate(((qa, gq), (ka, gk))):
                    o = dst[0:r, :, 0:HD]
                    own.do(v.tensor_tensor(o, A[2 + i][0:r, :].rearrange("p (h d) -> p h d", h=H),
                                           sh[0:r, 7, i * H:(i + 1) * H].unsqueeze(2).to_broadcast([r, H, HD]), ALU.mult))
                    own.step(v.tensor_tensor(o, o, g[0:r, :].unsqueeze(1).to_broadcast([r, H, HD]), ALU.mult))
                own.settle()
                if r == TS:
                    for i, src in enumerate((qa, ka)):
                        v.tensor_copy(sqq[0:r, i * DA:(i + 1) * DA].rearrange("p (h d) -> p h d", h=H),
                                      src[0:r, :, 0:HD]).then_inc(cst2, 1)
                    v.wait_ge(cst2, 2 * DC + 2)
                v.sem_inc(qk_ready, 1)
                v.wait_ge(F_done, t + 1)
                if r == P:
                    own.step(v.tensor_copy(qa[:, :, HD], A[5][:, 16:16 + H]))
                    own.step(v.tensor_scalar(ka[:, :, HD + 1], A[5][:, 16:16 + H], -1.0, None, ALU.mult))
                    own.step(v.tensor_tensor(lacc[:, :], lacc[:, :], lf[:, 5, :], ALU.add))
                    own.settle()
                else:
                    for _ in range(3):
                        own.step(v.nop())
                    own.settle()
                v.sem_inc(Fq_ready, 1)
                v.wait_ge(eg_ready, t + 1)
                own.do(v.tensor_scalar(eg[:, :, 0:r], eg[:, :, 0:r], 1.0, None, ALU.add))
                own.do(v.reciprocal(eg[:, :, 0:r], eg[:, :, 0:r]))
                if not isinstance(t, int) or t > 0:
                    v.wait_ge(stored_u, 16 * t)
                for c in range(CC):
                    a = v.scalar_tensor_tensor(uT[:, c, 0:r], A[0][:, c * P:c * P + r], bg[:, 0, c:c + 1],
                                               eg[:, c, 0:r], ALU.add, ALU.mult)
                a.then_inc(u_ready, 1)
                assert own.n == OV, own.n

            v.wait_ge(own_p, 5)
            norm_x(0)
            body(0)
            v.wait_ge(uTT_done, 1)
            v.tensor_copy(ub[0:TS, :], A[6][0:TS, :]).then_inc(ubs_ready, 1)
            with v.Fori(1, NB) as t:
                body(t)
            body(NB, False)
            v.wait_ge(uTT_done, 2)
            v.wait_ge(ubs_out, 16)
            v.tensor_copy(ub[:, :], A[6][:, :]).then_inc(ub_ready, 1)

        @block.tensor
        def _(pe):
            def body(t):
                r = rows(t)
                pe.wait_ge(xs_ready, t + 1)
                if not isinstance(t, int) or t > 0:
                    pe.wait_ge(u_ready, t)
                    pe.wait_ge(qkT_ready, t)
                for c in range(DC):
                    mm = pe.transpose(A[c // 4][:, (c % 4) * P:(c % 4) * P + r], xs[0:r, c * P:(c + 1) * P],
                                      ident[0:r, 0:r])
                mm.then_inc(xT_done, 1)
                pe.wait_ge(hT_ready, t + 1)
                for k in range(DC):
                    mm = pe.matmul(A[5][0:r, 0:H], hT[:, k, 0:r], w_in[:, k, ZF:ZF + H], start=(k == 0), stop=(k == DC - 1))
                mm.then_inc(fg_done, 1)
                for j in range(3):
                    for k in range(DC):
                        mm = pe.matmul(A[2 + j][0:r, :], hT[:, k, 0:r], w_in[:, k, j * DA:(j + 1) * DA],
                                       start=(k == 0), stop=(k == DC - 1))
                    mm.then_inc(qkv_done, 1)
                for j in range(2 * CC):
                    for k in range(DC):
                        mm = pe.matmul(A[j // CC][:, (j % CC) * P:(j % CC) * P + r],
                                       w_in[:, k, ZG + j * P:ZG + (j + 1) * P], hT[:, k, 0:r],
                                       start=(k == 0), stop=(k == DC - 1))
                mm.then_inc(glu_done, 1)
                pe.wait_ge(logf_ready, t + 1)
                if r == P:
                    pe.matmul(A[5][:, 16:16 + H], K["tri"][:, :], lf[:, 5, :], start=True, stop=False)
                    pe.matmul(A[5][:, 16:16 + H], K["ones"][:, :], lacc[:, :], start=False, stop=True).then_inc(F_done, 1)
                else:
                    pe.nop().then_inc(F_done, 1)
                pe.wait_ge(qk_ready, t + 1)
                pe.wait_ge(Fq_ready, t + 1)
                pe.wait_ge(v_ready, t + 1)
                if r == P:
                    for i, src in enumerate((qa, ka)):
                        for h in range(H):
                            mm = pe.transpose(A[2 + 2 * i + h // 4][0:AUG, (h % 4) * P:(h % 4 + 1) * P],
                                              src[:, h, :], ident[:, :])
                else:
                    for i, src in enumerate((qa, ka)):
                        for c in range(CC):
                            mm = pe.transpose(A[2 + 2 * i][:, c * TS:(c + 1) * TS],
                                              sqq[0:r, i * DA + c * P:i * DA + (c + 1) * P], ident[0:r, 0:r])
                mm.then_inc(qkT_done, 1)

            def u_rows(r):
                for c in range(CC):
                    mm = pe.transpose(A[6][0:r, c * P:(c + 1) * P], uT[:, c, 0:r], ident[:, :])
                mm.then_inc(uTT_done, 1)

            pe.wait_ge(w_sem, 16)
            body(0)
            pe.wait_ge(u_ready, 1)
            u_rows(TS)
            with pe.Fori(1, NB) as t:
                body(t)
            body(NB)
            pe.wait_ge(u_ready, NB + 1)
            pe.wait_ge(ubs_ready, 1)
            u_rows(P)


def sampled(nc, I, O, S, K):
    NP = 4
    with ExitStack() as ctx:
        sb = lambda n, s, d=F32: ctx.enter_context(nc.sbuf_tensor(n, s, d))
        sem = lambda n: ctx.enter_context(nc.semaphore(n))
        psum = lambda n: ctx.enter_context(nc.psum_tensor(n, [P, 512], F32))
        Kp = sb("Kp", [P, 2, NP, DA])
        Vp = sb("Vp", [P, NS, NP, DA])
        Lp = sb("Lp", [P, NS * NP, H])
        KT = sb("KT", [P, 2, CC, NP * P])
        idx = sb("idx", [P, NS * NP], I32)
        pt = sb("pt", [P, NS * NP], I32)
        lane = sb("lane", [P, 1], I32)
        lanef = sb("lanef", [P, 1])
        qT = sb("s_qT", [P, CC, TS])
        kT = sb("s_kT", [P, CC, TS])
        vs = sb("s_v", [TS, DA])
        ls = sb("s_l", [TS, H])
        Qbd = sb("Qbd", [P, CC, NS, H, QS])
        later = sb("later", [P, 896])
        later32 = sb("later32", [TS, TS])
        upto = sb("upto", [TS, NS, QS])
        uptoh = sb("uptoh", [TS, NS, H, QS])
        eqh = sb("eqh", [TS, NS, H, QS])
        L = sb("L", [TS, NS, H, QS])
        Lb = sb("Lb", [P, NS * NP, H, QS])
        hrow = sb("hrow", [H, P])
        hcol = sb("hcol", [H, DA])
        ones5 = sb("ones5", [TS, 512])
        hm = sb("hm", [P, DA])
        selS = sb("selS", [P, 2, TS])
        mown = sb("mown", [P, 2, TS])
        So = sb("So", [P, 2, TS])
        Pm = sb("Pm", [P, 2, 512 + TS])
        PT = sb("PT", [P, 2, NP, P])
        PTo = sb("PTo", [TS, 2, P])
        Om = sb("Om", [P, 2, DA])
        sm = sb("sm", [P, 2, 8])
        aT = sb("aT", [P, CC, TS])
        T = [psum(f"T{i}") for i in range(2)]
        SG = [psum(f"SG{i}") for i in range(2)]
        SO, MI, OG, AT = psum("SO"), psum("MI"), psum("OG"), psum("AT")
        OWN = [SO, MI]
        small_in, idx_ready, cst, own_v = sem("s_small"), sem("s_idx"), sem("s_cst"), sem("s_own")
        k_in = [sem(f"s_k{i}") for i in range(2)]
        v_in, l_in = [sem(f"s_v{i}") for i in range(2)], [sem(f"s_l{i}") for i in range(2)]
        pt_in = sem("s_pt")
        kt_done, kt_act, kt_dve = sem("s_ktd"), sem("s_kta"), sem("s_ktv")
        q_ready, s_done, masks_done, m_ready, e_done = sem("s_q"), sem("s_s"), sem("s_mk"), sem("s_m"), sem("s_e")
        pt_done, pt_ready, o_done, om_ready, at_done, at_ready = (sem("s_ptd"), sem("s_ptr"), sem("s_od"), sem("s_om"),
                                                                  sem("s_atd"), sem("s_atr"))
        stored, masks_ready = sem("s_st"), sem("s_mkr")
        ident = K["ident"]
        i32 = ident[0:TS, 0:TS]
        cache = {"k": I["cache_k"], "v": I["cache_v"], "l": I["cache_logf"]}
        block = ctx.enter_context(nc.Block())

        @block.sync
        def _(sp):
            sp.dma_start(pt[:, :], I["page_table"].to_broadcast([P, NS * NP])).then_inc(pt_in, 16)
            for dst, src in ((qT, S["qTs"]), (kT, S["kTs"]), (vs, O["v_sample"]), (ls, O["logf_sample"])):
                sp.dma_start(dst[:], src).then_inc(small_in, 16)
            sp.wait_ge(at_ready, 1)
            sp.dma_start(S["attTs"], aT[:, :, :]).then_inc(stored, 16)
            sp.wait_ge(stored, 16)

        @block.gpsimd
        def _(pool):
            pool.iota(lane[:, :], [[0, 1]], base=0, channel_multiplier=1).then_inc(cst, 1)
            pool.memset(later[:, :], 1.0).then_inc(cst, 1)
            pool.memset(later32[:, :], 1.0).then_inc(cst, 1)
            pool.memset(upto[:, :, :], 1.0).then_inc(cst, 1)
            pool.memset(hrow[:, :], 1.0).then_inc(cst, 1)
            pool.memset(hcol[:, :], 1.0).then_inc(cst, 1)
            pool.memset(ones5[:, :], 1.0).then_inc(cst, 1)
            pool.memset(Qbd[:, :, :, :, :], 0.0).then_inc(cst, 1)
            pool.wait_ge(cst, 8)
            pool.affine_select(out=later[:, :], in_=later[:, :], compare_op=ALU.is_gt, fill=0.0, base=384,
                               pattern=[[-1, 896]], channel_multiplier=1).then_inc(cst, 1)
            pool.affine_select(out=later32[:, :], in_=later32[:, :], compare_op=ALU.is_gt, fill=0.0, base=0,
                               pattern=[[-1, TS]], channel_multiplier=1).then_inc(cst, 1)
            pool.affine_select(out=upto[:, :, :], in_=upto[:, :, :], compare_op=ALU.is_ge, fill=0.0, base=0,
                               pattern=[[-QS, NS], [0, QS]], channel_multiplier=1).then_inc(cst, 1)
            pool.affine_select(out=hrow[:, :], in_=hrow[:, :], compare_op=ALU.is_equal, fill=0.0, base=0,
                               pattern=[[0, 4], [-1, H], [0, QS]], channel_multiplier=1).then_inc(cst, 1)
            pool.affine_select(out=hcol[:, :], in_=hcol[:, :], compare_op=ALU.is_equal, fill=0.0, base=0,
                               pattern=[[-1, H], [0, HD]], channel_multiplier=1).then_inc(cst, 1)
            pool.wait_ge(cst, 13)
            pool.affine_select(out=upto[:, :, :], in_=upto[:, :, :], compare_op=ALU.is_ge, fill=0.0, base=0,
                               pattern=[[QS, NS], [1, QS]], channel_multiplier=-1).then_inc(cst, 1)
            pool.wait_ge(idx_ready, 1)
            at = lambda n: bass.IndirectOffsetOnAxis(idx[:, n:n + 1], 0)
            for n in range(NS):
                if n >= 2:
                    pool.wait_ge(s_done, n - 1)
                for j in range(NP):
                    pool.indirect_dma_start(Kp[:, n % 2, j, :], None, cache["k"], at(NP * n + j)).then_inc(k_in[n % 2], 16)
                    pool.indirect_dma_start(Lp[:, NP * n + j, :], None, cache["l"], at(NP * n + j)).then_inc(l_in[n % 2], 16)
                for j in range(NP):
                    pool.indirect_dma_start(Vp[:, n, j, :], None, cache["v"], at(NP * n + j)).then_inc(v_in[n // 4], 16)

        @block.scalar
        def _(act):
            def keys(n):
                for c in range(1, CC, 2):
                    act.wait_ge(kt_done, CC * n + c + 1)
                    if n >= 2:
                        act.wait_ge(s_done, n - 1)
                    act.activation(KT[:, n % 2, c, :], T[c % 2][:, :], ACT.Copy).then_inc(kt_act, 1)

            def soft(g):
                act.wait_ge(m_ready, g + 1)
                act.activation(Pm[:, g, 0:512], SG[g][:, :], ACT.Exp, bias=sm[:, g, 2:3], accum_out=sm[:, g, 3:4])
                act.activation(Pm[:, g, 512:], So[:, g, :], ACT.Exp, bias=sm[:, g, 2:3],
                               accum_out=sm[:, g, 4:5]).then_inc(e_done, 1)

            for n in range(NS):
                keys(n)
                if n == 4:
                    soft(0)
            soft(1)

        @block.vector
        def _(v):
            own = Own(v, own_v)
            v.wait_ge(pt_in, 16)
            v.wait_ge(cst, 8)
            own.do(v.tensor_copy(lanef[:, :], lane[:, :]))
            v.tensor_scalar(idx[:, :], pt[:, :], float(P), lanef[:, 0:1], ALU.mult, ALU.add).then_inc(idx_ready, 1)
            v.wait_ge(small_in, 64)
            for c in range(CC):
                for half in range(2):
                    r = slice(half * HD, (half + 1) * HD)
                    own.step(v.tensor_copy(Qbd[r, c, :, 2 * c + half, :],
                                           qT[r, c, :].rearrange("p (n q) -> p n q", n=NS)))
            v.wait_ge(cst, 14)
            own.step(v.tensor_copy(uptoh[:, :, :, :], upto[:, :, :].unsqueeze(2).to_broadcast([TS, NS, H, QS])))
            own.step(v.tensor_copy(eqh[:, :, :, :], i32.rearrange("p (n q) -> p n q", n=NS).unsqueeze(2)
                                   .to_broadcast([TS, NS, H, QS])))
            own.settle()
            own.do(v.tensor_tensor(L[:, :, :, :].rearrange("p n h q -> p n (h q)").rearrange("p n (h q) -> p n h q", h=H),
                                   uptoh[:, :, :, :],
                                   ls[:, :].unsqueeze(1).unsqueeze(3).to_broadcast([TS, NS, H, QS]), ALU.mult))
            v.sem_inc(q_ready, 1)

            def keys(n):
                v.wait_ge(l_in[n % 2], 16 * NP * (n // 2 + 1))
                for j in range(NP):
                    own.step(v.tensor_copy(Lb[:, NP * n + j, :, :],
                                           Lp[:, NP * n + j, :].unsqueeze(2).to_broadcast([P, H, QS])))
                own.settle()
                for c in range(0, CC, 2):
                    v.wait_ge(kt_done, CC * n + c + 1)
                    if n >= 2:
                        v.wait_ge(s_done, n - 1)
                    v.tensor_copy(KT[:, n % 2, c, :], T[c % 2][:, :]).then_inc(kt_dve, 1)

            def soft(g):
                v.wait_ge(s_done, 4 * g + 4)
                own.do(v.tensor_tensor(So[:, g, :], OWN[g][:, 0:TS], mown[:, g, :], ALU.add))
                own.step(v.tensor_reduce(sm[:, g, 0:1], SG[g][:, :], X, ALU.max))
                own.step(v.tensor_reduce(sm[:, g, 1:2], So[:, g, :], X, ALU.max))
                own.settle()
                own.do(v.tensor_tensor(sm[:, g, 5:6], sm[:, g, 0:1], sm[:, g, 1:2], ALU.max))
                v.tensor_scalar(sm[:, g, 2:3], sm[:, g, 5:6], -1.0, None, ALU.mult).then_inc(m_ready, 1)
                v.wait_ge(e_done, g + 1)
                own.do(v.tensor_tensor(sm[:, g, 6:7], sm[:, g, 3:4], sm[:, g, 4:5], ALU.add))
                own.do(v.reciprocal(sm[:, g, 7:8], sm[:, g, 6:7]))

            def weigh(g):
                v.wait_ge(pt_done, g + 1)
                own.step(v.tensor_copy(PT[:, g, :, :].rearrange("p j r -> p (j r)"), AT[:, :]))
                own.step(v.tensor_copy(PTo[:, g, :], SO[0:TS, 0:P]))
                own.settle()
                v.sem_inc(pt_ready, 1)
                v.wait_ge(o_done, g + 1)
                v.scalar_tensor_tensor(Om[:, g, :], OG[:, :], sm[:, g, 7:8], hm[:, :], ALU.mult, ALU.mult)\
                    .then_inc(om_ready, 1)

            v.wait_ge(masks_done, 1)
            own.step(v.tensor_scalar(mown[:, :, :].rearrange("p g t -> p (g t)"), MI[:, 0:2 * TS], -1.0, 1e30,
                                     ALU.add, ALU.mult))
            own.step(v.tensor_copy(selS[:, :, :].rearrange("p g t -> p (g t)"), MI[:, 2 * TS:4 * TS]))
            own.step(v.tensor_copy(hm[:, :], OG[:, :]))
            own.settle()
            v.sem_inc(masks_ready, 1)
            for n in range(NS):
                keys(n)
                if n == 4:
                    soft(0)
                if n == 5:
                    weigh(0)
            soft(1)
            weigh(1)
            v.wait_ge(at_done, 1)
            v.tensor_copy(aT[:, :, :].rearrange("p c t -> p (c t)"), AT[:, 0:CC * TS]).then_inc(at_ready, 1)

        @block.tensor
        def _(pe):
            pe.wait_ge(q_ready, 1)
            for n in range(NS):
                o = slice(32 * (n % 4), 32 * (n % 4) + 32)
                hq = lambda a: a[:, n, :, :].rearrange("p h q -> p (h q)")
                pe.matmul(MI[o, (n // 4) * TS:(n // 4 + 1) * TS], hq(uptoh), i32, start=True, stop=True)
            for n in range(NS):
                o = slice(32 * (n % 4), 32 * (n % 4) + 32)
                hq = lambda a: a[:, n, :, :].rearrange("p h q -> p (h q)")
                pe.matmul(MI[o, (2 + n // 4) * TS:(3 + n // 4) * TS], hq(eqh), i32, start=True, stop=True)
            pe.matmul(OG[:, :], hrow[:, :], hcol[:, :], start=True, stop=True).then_inc(masks_done, 1)

            def score(n):
                g, o = n // 4, slice(32 * (n % 4), 32 * (n % 4) + 32)
                hq = lambda a, m: a[:, m, :, :].rearrange("p h q -> p (h q)")
                pe.wait_ge(k_in[n % 2], 16 * NP * (n // 2 + 1))
                for c in range(CC):
                    if c >= 2 or n >= 1:
                        last = 2 * n + c // 2
                        pe.wait_ge(kt_dve if c % 2 == 0 else kt_act, last)
                    for j in range(NP):
                        mm = pe.transpose(T[c % 2][:, j * P:(j + 1) * P], Kp[:, n % 2, j, c * P:(c + 1) * P], ident[:, :])
                    mm.then_inc(kt_done, 1)
                pe.wait_ge(kt_dve, 2 * n + 2)
                pe.wait_ge(kt_act, 2 * n + 2)
                for c in range(CC):
                    pe.matmul(SG[g][o, :], hq(Qbd[:, c], n), KT[:, n % 2, c, :], start=(c == 0), stop=False)
                for j in range(NP):
                    pe.matmul(SG[g][o, :], hq(Lb, NP * n + j), later[:, 384 - P * j:896 - P * j], start=False, stop=False)
                pe.matmul(SG[g][o, :], hq(L, n), ones5[:, :], start=False, stop=True)
                so = OWN[g][o, 0:TS]
                for c in range(CC):
                    pe.matmul(so, hq(Qbd[:, c], n), kT[:, c, :], start=(c == 0), stop=False)
                pe.matmul(so, hq(L, n), later32[:, :], start=False, stop=True).then_inc(s_done, 1)

            def values(g):
                pe.wait_ge(e_done, g + 1)
                for j in range(NP):
                    pe.transpose(AT[:, j * P:(j + 1) * P], Pm[:, g, j * P:(j + 1) * P], ident[:, :])
                pe.transpose(SO[0:TS, 0:P], Pm[:, g, 512:], ident[:, :]).then_inc(pt_done, 1)
                pe.wait_ge(pt_ready, g + 1)
                pe.wait_ge(v_in[g], 16 * NP * 4)
                if g:
                    pe.wait_ge(om_ready, 1)
                for n in range(4 * g, 4 * g + 4):
                    o = slice(32 * (n % 4), 32 * (n % 4) + 32)
                    for j in range(NP):
                        pe.matmul(OG[o, :], PT[:, g, j, o], Vp[:, n, j, :], start=(j == 0), stop=False)
                    mm = pe.matmul(OG[o, :], PTo[:, g, o], vs[:, :], start=False, stop=True)
                mm.then_inc(o_done, 1)

            pe.wait_ge(masks_ready, 1)
            for n in range(NS):
                score(n)
                if n == 5:
                    values(0)
            values(1)
            pe.wait_ge(om_ready, 2)
            for c in range(CC):
                for g in range(2):
                    mm = pe.matmul(AT[:, c * TS:(c + 1) * TS], Om[:, g, c * P:(c + 1) * P], selS[:, g, :],
                                   start=(g == 0), stop=(g == 1))
            mm.then_inc(at_done, 1)


NK = 128
TOP = 16
SLOTS = H * TOP
RING = 8
DG = 4
NG = SLOTS
NG_S = NG * TS // P
S_CONV = 2 * H
S_X1 = S_CONV + 12
S_ROUTE = S_X1 + 7
S_GATE = S_ROUTE + H + 2
STEPS = S_GATE + 3
PLAN = [3] * 14 + [4] * 2 + [2, 1, 1, 1, 2, 2, 1, 1, 2, 2, 2, 2] + [2, 1, 1, 1, 1, 2, 2] + [2, 2] + [5] * 7 + [6] + [2, 2, 0]
LOWEST = -3.0e38
ONCE = 16 * 8
OA = 6
OVT = 341


def some(n):
    return not isinstance(n, int) or n > 0


def height(t):
    return TS if isinstance(t, int) and t == NB else P


def groups_of(e):
    return NG_S if isinstance(e, int) and e == NB else NG


def tail(nc, I, O, S, K):
    with ExitStack() as ctx:
        sb = lambda n, s, d=F32: ctx.enter_context(nc.sbuf_tensor(n, s, d))
        sem = lambda n: ctx.enter_context(nc.semaphore("t_" + n))
        psum = lambda n, w: ctx.enter_context(nc.psum_tensor(n, [P, w], F32))
        ring = sb("ring", [P, RING, 2 * D])
        w_o = sb("w_o", [P, DC, D])
        wq = [sb(f"wq{i}", [P, DC, 2 * NK]) for i in range(2)]
        subk = sb("subk", [P, H, 2, NK])
        V = sb("V", [P, NB, DA])
        kh = [sb(f"kh{i}", [AUG, SEQ]) for i in range(2)]
        qTb = sb("t_qT", [AUG, H, P])
        gate = [sb(f"gate{i}", [P, D]) for i in range(2)]
        h2n = sb("h2n", [P, D])
        h2c = sb("h2c", [P, D])
        xb = sb("t_xb", [P, D])
        Pm = sb("t_Pm", [P, SEQ])
        PTs = sb("t_PT", [P, SEQ])
        fT = sb("fT", [P, DC, P])
        win = sb("win", [P, CC, P + W - 1])
        yac = sb("yac", [P, CC, P])
        mask = sb("mask", [P, SEQ], BF16)
        cw = sb("cw", [P, CC, W])
        cv = sb("cv", [P, 3, CC])
        ez = sb("ez", [P, CC, P])
        stt = sb("stt", [P, 2, 8])
        mx = sb("mx", [P, 3, H])
        rl = sb("rl", [P, H])
        act8 = sb("act8", [P, RING])
        ga = sb("ga", [P, RING])
        dg = sb("dg", [P, DG, P])
        idxn = sb("idxn", [P, SLOTS], I32)
        idxc = sb("idxc", [P, SLOTS], I32)
        gn = sb("gn", [P, H, TOP])
        gc = sb("gc", [P, SLOTS])
        gs = sb("gs", [P, 2, H])
        qh = sb("qh", [P, 2, P])
        sc = sb("sc", [P, 2, NK])
        sc2 = sb("sc2", [P, 2, NK])
        best = sb("best", [P, 2, TOP])
        bix = sb("bix", [P, 2, TOP], U32)
        cand = sb("cand", [P, 2, TOP, TOP])
        px = sb("px", [P, 3, TOP], U32)
        eq = sb("eq", [P, 2, TOP, TOP])
        ss = sb("sel2", [P, 2, TOP])
        fold = sb("fold", [P, TS])
        io16 = sb("io16", [P, TOP])
        io16i = sb("io16i", [P, TOP], I32)
        top = sb("top", [P, H, TOP])
        SS, TT, YY = psum("SS", SEQ), psum("TT", SEQ), psum("YY", D)
        V0, M0 = psum("V0", 512), psum("M0", 512)

        once_in, cst, own_v, own_a = sem("once"), sem("cst"), sem("own_v"), sem("own_a")
        g_in = [sem(f"g{i}") for i in range(RING)]
        quarter_copied = sem("quarter")
        idx_copied, dot_done, gelu_done, diag_done, v_done = (sem("idxc"), sem("dot"), sem("gelu"), sem("diag"), sem("v"))
        carrier_v, carrier, yg_done = sem("carrier_v"), sem("carrier"), sem("yg")
        q_in, win_in, mask_in, x_in = sem("q_in"), sem("win_in"), sem("mask_in"), sem("x_in")
        k_in = [sem(f"k{i}") for i in range(2)]
        wq_in = [sem(f"wq{i}") for i in range(2)]
        smp_in, gate_in = sem("smp"), sem("gate")
        x1_out, x1_in, y_out, m_out = sem("x1_out"), sem("x1_in"), sem("y_out"), sem("m_out")
        s_done, m_ready, e_done, pt_done, pts_ready, pv_done = (sem("s"), sem("m"), sem("e"), sem("pt"), sem("pts"), sem("pv"))
        conv_done, yT_done, y_sum, nmu_ready, ssq_ready = sem("conv"), sem("yT"), sem("ysum"), sem("nmu"), sem("ssq")
        ms_ready, r0_ready, att_ready, yn_ready = sem("ms"), sem("r0"), sem("att"), sem("yn")
        attT_done, ynT_done, attT_ready, z_ready, catc_ready = sem("attT"), sem("ynT"), sem("attTr"), sem("z"), sem("catc")
        wo_done, x1_ready, ss_ready, xs_ready, x1T_done = sem("wo"), sem("x1"), sem("ss"), sem("xs"), sem("x1T")
        fT_ready, h2_done, h2_ready = sem("fTr"), sem("h2d"), sem("h2")
        qd_done, qh_ready, sc_done, sc_ready = sem("qd"), sem("qh"), sem("scd"), sem("scr")
        idx_ready, sh_ready, eg_ready, route_ready, cur_ready = sem("idx"), sem("shr"), sem("eg"), sem("route"), sem("cur")
        sc_free, y_ready, st_in, stT_done, ue_ready = sem("scf"), sem("y"), sem("st_in"), sem("stT"), sem("ue")
        ident = K["ident"]
        state = V[0:120, 0:2, :]
        ue = V[:, 2:, :].rearrange("p b n -> p (b n)")[:, 0:CC * NS * (W - 1 + QS)]\
            .rearrange("p (c n w) -> p c n w", c=CC, n=NS)
        modT, sgT = K["modT"], K["sgT"]
        block = ctx.enter_context(nc.Block())

        @block.sync
        def _(sp):
            for dst, src in ((V[:, :, :], O["v_prompt"].rearrange("(b p) n -> p b n", p=P)),
                             (cw[:, :, :], I["conv_wT"]), (cv[:, :, :], I["conv_v"]), (xb[:, :], I["x_prompt"][0:P, :]),
                             (gate[0][:, :], S["gate"][0]), (gate[1][:, :], S["gate"][1]),
                             (w_o[:, :, :], I["w_o"].rearrange("(k p) n -> p k n", p=P)), (subk[:, :, :, :], I["subkT"])):
                sp.dma_start(dst, src).then_inc(once_in, 16)
            wqv = I["w_query"].rearrange("(k p) n -> p k n", p=P)

            def load_wq(t, h):
                n = H * t + h
                if n >= 2:
                    sp.wait_ge(qd_done, n - 1)
                sp.dma_start(wq[n % 2][:, :, :], wqv[:, :, h * 2 * NK:(h + 1) * 2 * NK]).then_inc(wq_in[n % 2], 16)

            def load_k(t, h):
                n, nk = H * t + h, keys_of(t)
                if n >= 2:
                    sp.wait_ge(s_done, n - 1)
                sp.dma_start(kh[n % 2][:, 0:nk], S["kT"][:, h, 0:nk]).then_inc(k_in[n % 2], 16)

            def prefetch(t):
                nk = keys_of(t)
                if t:
                    sp.wait_ge(s_done, H * t)
                    sp.wait_ge(m_ready, H * t)
                    sp.wait_ge(conv_done, t)
                sp.dma_start(qTb[:, :, :], S["qT"][:, :, t * P:(t + 1) * P]).then_inc(q_in, 16)
                sp.dma_start(mask[:, 0:nk], S["mask"][:, SEQ - P - t * P:SEQ - P - t * P + nk]).then_inc(mask_in, 16)
                sp.dma_start(win[:, :, :], S["uT"][:, :, t * P:t * P + P + W - 1]).then_inc(win_in, 16)
                load_k(t, 0)
                load_k(t, 1)

            def load_sampled():
                sp.wait_ge(pv_done, H * NB)
                sp.dma_start(state, I["state_conv"].rearrange("n w c -> (n w) c").rearrange("(g p) c -> p g c", g=2))\
                    .then_inc(smp_in, 16)
                sp.dma_start(ue[:, :, :, W - 1:], S["uTs"].rearrange("p c (n q) -> p c n q", n=NS)).then_inc(smp_in, 16)
                sp.wait_ge(qd_done, H * NB)
                sp.dma_start(fT[:, 0:CC, 0:TS], S["attTs"]).then_inc(smp_in, 16)
                sp.wait_ge(x1_ready, NB)
                sp.dma_start(gate[0][0:TS, :], S["gate_s"][0]).then_inc(smp_in, 16)

            def tail_io(t):
                r = height(t)
                if t < NB:
                    for h in range(2, H):
                        load_k(t, h)
                else:
                    load_sampled()
                if t:
                    sp.wait_ge(xs_ready, t)
                    sp.wait_ge(x1_out, 16 * t)
                    sp.dma_start(xb[0:r, :], I["x_prompt"][t * P:(t + 1) * P, :] if t < NB else I["x_sample"])\
                        .then_inc(x_in, 16)
                load_wq(t, 0)
                load_wq(t, 1)
                sp.wait_ge(x1_ready, t + 1)
                sp.dma_start(S["x1"][t, 0:r, :], xb[0:r, :]).then_inc(x1_out, 16)
                if t:
                    sp.wait_ge(x1_out, 16 * (t + 1))
                    sp.dma_start(PTs[:, :], S["x1"][t - 1, :, :]).then_inc(x1_in, 16)
                for h in range(2, H):
                    load_wq(t, h)
                if t < NB - 1:
                    prefetch(t + 1)

            def store_y(e):
                sp.wait_ge(y_ready, e + 1)
                dst = O["y_sample"] if e == NB else O["y_prompt"][e * P:(e + 1) * P, :]
                sp.dma_start(dst, Pm[0:height(e), :]).then_inc(y_out, 16)

            prefetch(0)
            tail_io(0)
            for i in range(1, NB + 1):
                tail_io(i)
                store_y(i - 1)
            sp.dma_start(PTs[0:TS, :], S["x1"][NB, 0:TS, :]).then_inc(x1_in, 16)
            sp.dma_start(gate[1][0:TS, :], S["gate_s"][1]).then_inc(gate_in, 16)
            store_y(NB)
            sp.wait_ge(y_out, 16 * (NB + 1))

        @block.gpsimd
        def _(pool):
            pool.iota(io16i[:, :], [[1, TOP]], base=0, channel_multiplier=0).then_inc(cst, 1)

            def experts(e):
                sampled_rows = isinstance(e, int) and e == NB
                half = SLOTS // 2
                if sampled_rows:
                    pool.wait_ge(quarter_copied, P // TS)
                else:
                    pool.wait_ge(idx_ready, 8 * e + 8)
                pool.sem_inc(carrier, 1)
                for k in range(groups_of(e)):
                    move = not sampled_rows and k in (0, NG // 2)
                    if move:
                        o = slice(0, half) if k == 0 else slice(half, SLOTS)
                        pool.tensor_copy(idxc[:, o], idxn[:, o]).then_inc(idx_copied, 1)
                        pool.wait_ge(idx_copied, 2 * e + (1 if k == 0 else 2))
                    n = NG * e + k
                    if some(n - RING + 1):
                        pool.wait_ge(v_done, n - RING + 1)
                    if move or some(n - RING + 1):
                        pool.sem_inc(carrier, 1)
                    pool.indirect_dma_start(ring[:, k % RING, :], None, I["experts"],
                                            bass.IndirectOffsetOnAxis(idxc[:, k:k + 1], 0)).then_inc(g_in[k % RING], 16)

            experts(0)
            with pool.Fori(1, NB) as e:
                experts(e)
            experts(NB)

        @block.scalar
        def _(act):
            own = Own(act, own_a)

            def rsqrt(count, r, src, ln, out):
                act.wait_ge(ms_ready, count)
                own.do(act.activation(ln, src, ACT.Ln))
                act.activation(out, ln, ACT.Exp, scale=-0.5).then_inc(r0_ready, 1)

            def step(s, t, nk):
                r = height(t)
                smp = r == TS
                if s == 0:
                    own.start(OA * t)
                if s < 2 * H and not smp:
                    n = H * t + s // 2 + 1
                    if s % 2 == 0:
                        act.wait_ge(m_ready, n)
                        act.activation(Pm[:, 0:nk], Pm[:, 0:nk], ACT.Exp, bias=mx[:, 1, s // 2:s // 2 + 1],
                                       accum_out=mx[:, 2, s // 2:s // 2 + 1]).then_inc(e_done, 1)
                    else:
                        act.wait_ge(pt_done, n)
                        act.activation(PTs[:, 0:nk], TT[:, 0:nk], ACT.Copy).then_inc(pts_ready, 1)
                yl = PTs[0:r, 512:1024]
                if s == S_CONV + 1:
                    act.wait_ge(yT_done, t + 1)
                    act.activation(yl, M0[0:r, :], ACT.Identity, accum_out=stt[0:r, 0, 0:1]).then_inc(y_sum, 1)
                if s == S_CONV + 3:
                    act.wait_ge(nmu_ready, t + 1)
                    act.activation(PTs[0:r, 0:512], yl, ACT.Square, bias=stt[0:r, 0, 1:2],
                                   accum_out=stt[0:r, 0, 2:3]).then_inc(ssq_ready, 1)
                    if not smp:
                        act.wait_ge(attT_done, t + 1)
                        act.activation(fT[:, 0:CC, :], SS[:, 0:512].rearrange("p (c t) -> p c t", c=CC),
                                       ACT.Copy).then_inc(attT_ready, 1)
                if s == S_CONV + 5:
                    rsqrt(2 * t + 1, r, stt[0:r, 0, 3:4], stt[0:r, 0, 4:5], stt[0:r, 0, 5:6])
                if s == S_CONV + 8:
                    act.wait_ge(ynT_done, t + 1)
                    for c in range(CC):
                        own.step(act.activation(ez[:, c, 0:r], M0[:, c * P:c * P + r], ACT.Identity,
                                                scale=cv[:, 1, c:c + 1], bias=cv[:, 2, c:c + 1]))
                    own.settle()
                    act.activation(yac[:, :, 0:r], ez[:, :, 0:r], ACT.Exp, scale=-1.0).then_inc(z_ready, 1)
                if s == S_X1 + 1:
                    act.wait_ge(x1_ready, t + 1)
                    act.activation(Pm[0:r, :], xb[0:r, :], ACT.Square, accum_out=stt[0:r, 1, 2:3]).then_inc(ss_ready, 1)
                if s == S_X1 + 3:
                    rsqrt(2 * t + 2, r, stt[0:r, 1, 3:4], stt[0:r, 1, 4:5], stt[0:r, 1, 5:6])
                if s == S_X1 + 6 and not smp:
                    act.wait_ge(x1T_done, t + 1)
                    for c in range(DC):
                        a = act.activation(fT[:, c, :], SS[:, c * P:(c + 1) * P], ACT.Identity,
                                           scale=sgT[:, 1, c, 0:1], bias=modT[:, 24 + c, 0:1])
                    a.then_inc(fT_ready, 1)
                if s == S_ROUTE + 1:
                    act.wait_ge(h2_done, t + 1)
                    if some(t):
                        act.wait_ge(cur_ready, t)
                    act.activation(h2n[:, :], TT[:, :], ACT.Copy).then_inc(h2_ready, 1)
                if S_ROUTE <= s < S_ROUTE + H:
                    h = s - S_ROUTE
                    act.wait_ge(qd_done, H * t + h + 1)
                    made = M0[:, 0:2 * P].rearrange("p (g t) -> p g t", g=2)
                    if smp:
                        act.activation(qh[:, :, :].rearrange("p g (q t) -> p g q t", t=TS),
                                       made[:, :, 0:TS].unsqueeze(2).to_broadcast([P, 2, P // TS, TS]),
                                       ACT.Copy).then_inc(qh_ready, 1)
                    else:
                        act.activation(qh[:, :, :], made, ACT.Copy).then_inc(qh_ready, 1)
                if S_ROUTE + 1 <= s < S_ROUTE + 1 + H:
                    h = s - S_ROUTE - 1
                    act.wait_ge(sc_done, H * t + h + 1)
                    if some(t) or h:
                        act.wait_ge(sc_free, H * t + h)
                    act.activation(sc[:, :, :].rearrange("p g k -> p (g k)"), V0[:, 0:2 * NK],
                                   ACT.Copy).then_inc(sc_ready, 1)
                if s == S_GATE + 1:
                    act.wait_ge(sh_ready, t + 1)
                    act.activation(gn[:, :, :], top[:, :, :], ACT.Exp).then_inc(eg_ready, 1)
                    assert own.n == OA, own.n

            def gelu(e, k):
                act.wait_ge(dot_done, NG * e + k + 1)
                a = k % RING
                act.activation(ga[:, a:a + 1], act8[:, a:a + 1], ACT.Gelu).then_inc(gelu_done, 1)

            iterate(act, step, gelu, lambda e: None, lambda e: None, prologue=lambda: act.wait_ge(once_in, ONCE))

        @block.vector
        def _(v):
            own = Own(v, own_v)
            own.carrier = carrier_v

            def newton(m, r0, a, b, out):
                own.do(v.tensor_tensor(a, r0, r0, ALU.mult))
                own.do(v.tensor_tensor(b, a, m, ALU.mult))
                own.do(v.tensor_scalar(a, b, -0.5, 1.5, ALU.mult, ALU.add))
                own.do(v.tensor_tensor(out, a, r0, ALU.mult))

            def taps(ks, r, rows_of, out_of):
                for k in ks:
                    for c in range(CC):
                        if k:
                            v.wait_ge(own.sem, own.base + own.n - CC + 1)
                            own.step(v.scalar_tensor_tensor(out_of(c), rows_of(c, k), cw[:, c, k:k + 1], out_of(c),
                                                            ALU.mult, ALU.add))
                        else:
                            own.step(v.tensor_scalar(out_of(c), rows_of(c, k), cw[:, c, 0:1], cv[:, 0, c:c + 1],
                                                     ALU.mult, ALU.add))

            def modulate(r):
                v.wait_ge(x1T_done, NB + 1)
                for c in range(DC):
                    o = fT[:, c, 0:r].rearrange("p (n q) -> p n q", n=NS)
                    i = SS[:, c * P:c * P + r].rearrange("p (n q) -> p n q", n=NS)
                    own.do(v.tensor_tensor(o, i, sgT[:, 1, c, 1:M].unsqueeze(2).to_broadcast([P, NS, QS]), ALU.mult))
                    own.do(v.tensor_tensor(o, o, modT[:, 24 + c, 1:M].unsqueeze(2).to_broadcast([P, NS, QS]), ALU.add))
                own.do(v.tensor_copy(fT[:, :, r:P].rearrange("p c (q t) -> p c q t", t=r),
                                     fT[:, :, 0:r].unsqueeze(2).to_broadcast([P, DC, P // r - 1, r])))
                v.sem_inc(fT_ready, 1)

            def choose(t, h):
                v.wait_ge(sc_ready, H * t + h + 1)
                own.carry()
                for g in range(2):
                    own.step(v.max(best[:, g, 0:8], sc[:, g, :]))
                own.settle()
                own.carry()
                for g in range(2):
                    own.step(v.max_index(bix[:, g, 0:8], best[:, g, 0:8], sc[:, g, :]))
                    own.step(v.match_replace(sc2[:, g, :], best[:, g, 0:8], sc[:, g, :], LOWEST))
                own.settle()
                v.sem_inc(sc_free, 1)
                for g in range(2):
                    own.step(v.max(best[:, g, 8:16], sc2[:, g, :]))
                own.settle()
                own.carry()
                for g in range(2):
                    own.step(v.max_index(bix[:, g, 8:16], best[:, g, 8:16], sc2[:, g, :]))
                own.do(v.tensor_tensor(cand[:, 0, :, :], best[:, 0, :].unsqueeze(2).to_broadcast([P, TOP, TOP]),
                                       best[:, 1, :].unsqueeze(1).to_broadcast([P, TOP, TOP]), ALU.add))
                c0 = cand[:, 0, :, :].rearrange("p i j -> p (i j)")
                c1 = cand[:, 1, :, :].rearrange("p i j -> p (i j)")
                own.carry()
                own.do(v.max(top[:, h, 0:8], c0))
                own.carry()
                own.step(v.max_index(px[:, 0, 0:8], top[:, h, 0:8], c0))
                own.do(v.match_replace(c1, top[:, h, 0:8], c0, LOWEST))
                own.carry()
                own.do(v.max(top[:, h, 8:16], c1))
                own.carry()
                own.do(v.max_index(px[:, 0, 8:16], top[:, h, 8:16], c1))
                own.step(v.tensor_scalar(px[:, 1, :], px[:, 0, :], 4, None, ALU.logical_shift_right))
                own.do(v.tensor_scalar(px[:, 2, :], px[:, 0, :], 15, None, ALU.bitwise_and))
                for g in range(2):
                    own.step(v.tensor_tensor(eq[:, g, :, :], px[:, 1 + g, :].unsqueeze(2).to_broadcast([P, TOP, TOP]),
                                             io16[:, :].unsqueeze(1).to_broadcast([P, TOP, TOP]), ALU.is_equal))
                own.settle()
                for g in range(2):
                    own.step(v.tensor_tensor(eq[:, g, :, :], eq[:, g, :, :],
                                             bix[:, g, :].unsqueeze(1).to_broadcast([P, TOP, TOP]), ALU.mult))
                own.settle()
                for g in range(2):
                    own.step(v.tensor_reduce(ss[:, g, :], eq[:, g, :, :], X, ALU.add))
                own.settle()
                if h == 0 and some(t):
                    v.wait_ge(idx_copied, 2 * t)
                v.scalar_tensor_tensor(idxn[:, h * TOP:(h + 1) * TOP], ss[:, 0, :], float(NK), ss[:, 1, :],
                                       ALU.mult, ALU.add).then_inc(idx_ready, 1)

            def step(s, t, nk):
                r = height(t)
                smp = r == TS
                if s == 0:
                    own.start(OVT * t)
                    if some(t - 1):
                        v.wait_ge(y_out, 16 * (t - 1))
                if smp and s == 1:
                    v.wait_ge(stT_done, 1)
                    for g in range(2):
                        src = (SS, TT)[g][:, 0:CC * 120].rearrange("p (c n w) -> p c n w", c=CC, n=4)
                        for c in range(CC):
                            own.step(v.tensor_copy(ue[:, c, 4 * g:4 * g + 4, 0:W - 1], src[:, c, :, :]))
                    own.settle()
                if smp and 2 <= s < S_CONV:
                    taps(range(W * (s - 2) // (S_CONV - 2), W * (s - 1) // (S_CONV - 2)), r,
                         lambda c, k: ue[:, c, :, k:k + QS],
                         lambda c: yac[:, c, 0:TS].rearrange("p (n q) -> p n q", n=NS))
                if s < 2 * H and not smp:
                    h = s // 2
                    if s == 0:
                        v.wait_ge(win_in, 16 * (t + 1))
                    if s % 2 == 0:
                        n = H * t + h + 1
                        if s == 0:
                            v.wait_ge(mask_in, 16 * (t + 1))
                        else:
                            v.wait_ge(pt_done, n - 1)
                        v.wait_ge(s_done, n)
                        own.carry()
                        own.do(v.tensor_tensor_reduce(out=Pm[:, 0:nk], in0=SS[:, 0:nk], in1=mask[:, 0:nk], scale=1.0,
                                                      scalar=LOWEST, op0=ALU.add, op1=ALU.max,
                                                      accum_out=mx[:, 0, h:h + 1]))
                        v.tensor_scalar(mx[:, 1, h:h + 1], mx[:, 0, h:h + 1], -1.0, None, ALU.mult).then_inc(m_ready, 1)
                    if s == 0 and some(t):
                        v.wait_ge(z_ready, t)
                    taps([k for k in (2 * s, 2 * s + 1) if k < W], r, lambda c, k: win[:, c, k:k + P],
                         lambda c: yac[:, c, :])
                if s == S_CONV - 1:
                    own.settle()
                    v.sem_inc(conv_done, 1)
                a = stt[0:r, 0, :]
                if s == S_CONV + 1 and not smp:
                    v.wait_ge(e_done, H * t + H)
                    own.do(v.reciprocal(rl[:, :], mx[:, 2, :]))
                    v.wait_ge(pv_done, H * t + H)
                    v.tensor_tensor(Pm[:, 0:DA].rearrange("p (h d) -> p h d", h=H),
                                    V0[:, :].rearrange("p (h d) -> p h d", h=H),
                                    rl[:, :].unsqueeze(2).to_broadcast([P, H, HD]), ALU.mult).then_inc(att_ready, 1)
                if s == S_CONV + 2:
                    v.wait_ge(y_sum, t + 1)
                    v.tensor_scalar(a[:, 1:2], a[:, 0:1], -1.0 / DA, None, ALU.mult).then_inc(nmu_ready, 1)
                if s == S_CONV + 4:
                    v.wait_ge(ssq_ready, t + 1)
                    v.tensor_scalar(a[:, 3:4], a[:, 2:3], 1.0 / DA, EPS, ALU.mult, ALU.add).then_inc(ms_ready, 1)
                if s == S_CONV + 6:
                    v.wait_ge(r0_ready, 2 * t + 1)
                    newton(a[:, 3:4], a[:, 5:6], a[:, 6:7], a[:, 7:8], a[:, 4:5])
                    v.tensor_scalar(Pm[0:r, 512:1024], PTs[0:r, 512:1024], a[:, 1:2], a[:, 4:5], ALU.add, ALU.mult)\
                        .then_inc(yn_ready, 1)
                if s == S_CONV + 9:
                    v.wait_ge(z_ready, t + 1)
                    own.do(v.tensor_scalar(yac[:, :, 0:r], yac[:, :, 0:r], 1.0, None, ALU.add))
                    own.do(v.reciprocal(yac[:, :, 0:r], yac[:, :, 0:r]))
                    v.tensor_tensor(fT[:, CC:DC, 0:r], ez[:, :, 0:r], yac[:, :, 0:r], ALU.mult).then_inc(catc_ready, 1)
                a = stt[0:r, 1, :]
                if s == S_X1:
                    v.wait_ge(wo_done, t + 1)
                    if some(t):
                        v.wait_ge(x_in, 16 * t)
                    if smp:
                        v.wait_ge(smp_in, 64)
                    own.do(v.tensor_tensor(PTs[0:r, :], TT[0:r, :], gate[0][0:r, :], ALU.mult))
                    v.tensor_tensor(xb[0:r, :], xb[0:r, :], PTs[0:r, :], ALU.add).then_inc(x1_ready, 1)
                if s == S_X1 + 2:
                    v.wait_ge(ss_ready, t + 1)
                    v.tensor_scalar(a[:, 3:4], a[:, 2:3], 1.0 / D, EPS, ALU.mult, ALU.add).then_inc(ms_ready, 1)
                if s == S_X1 + 4:
                    v.wait_ge(r0_ready, 2 * t + 2)
                    newton(a[:, 3:4], a[:, 5:6], a[:, 6:7], a[:, 7:8], a[:, 4:5])
                    v.tensor_scalar(Pm[0:r, :], xb[0:r, :], a[:, 4:5], None, ALU.mult).then_inc(xs_ready, 1)
                if s == S_X1 + 6 and smp:
                    modulate(r)
                if S_ROUTE + 2 <= s < S_ROUTE + 2 + H:
                    choose(t, s - S_ROUTE - 2)
                if s == S_GATE and smp:
                    v.wait_ge(idx_ready, 8 * t + 8)
                    v.wait_ge(v_done, NG * (t - 1) + NG // 2)
                    for q in range(P // TS):
                        o = slice(q * TS, (q + 1) * TS)
                        v.tensor_copy(idxc[o, 0:NG_S], idxn[o, q * NG_S:(q + 1) * NG_S]).then_inc(quarter_copied, 1)
                if s == S_GATE:
                    own.do(v.tensor_copy(gs[:, 0, :], top[:, :, 0]))
                    own.do(v.tensor_tensor(top[:, :, :], top[:, :, :],
                                           gs[:, 0, :].unsqueeze(2).to_broadcast([P, H, TOP]), ALU.subtract))
                    v.sem_inc(sh_ready, 1)
                if s == S_GATE + 2:
                    v.wait_ge(eg_ready, t + 1)
                    own.do(v.tensor_reduce(gs[:, 0, :], gn[:, :, :], X, ALU.add))
                    own.do(v.reciprocal(gs[:, 1, :], gs[:, 0, :]))
                    own.do(v.tensor_tensor(gn[:, :, :], gn[:, :, :],
                                           gs[:, 1, :].unsqueeze(2).to_broadcast([P, H, TOP]), ALU.mult))
                    assert smp or own.n == OVT, own.n

            def begin(e):
                v.wait_ge(h2_ready, e + 1)
                flat = gn[:, :, :].rearrange("p h k -> p (h k)")
                if isinstance(e, int) and e == NB:
                    for q in range(P // TS):
                        o = slice(q * TS, (q + 1) * TS)
                        v.tensor_copy(gc[o, 0:NG_S], flat[o, q * NG_S:(q + 1) * NG_S])
                else:
                    v.tensor_copy(gc[:, :], flat)
                v.tensor_copy(h2c[:, :], h2n[:, :]).then_inc(cur_ready, 1)
                v.wait_ge(cur_ready, e + 1)

            def diag(e, k):
                n = NG * e + k
                folded = isinstance(e, int) and e == NB
                v.wait_ge(gelu_done, n + 1)
                if some(n - DG + 1):
                    v.wait_ge(v_done, n - DG + 1)
                v.tensor_scalar(dg[:, k % DG, 0:TS] if folded else dg[:, k % DG, :], fold[:, :] if folded else ident[:, :],
                                ga[:, k % RING:k % RING + 1], gc[:, k:k + 1], ALU.mult, ALU.mult).then_inc(diag_done, 1)

            def group(e, k):
                u = ring[:, k % RING, 0:D]
                v.wait_ge(g_in[k % RING], 16 * (NG // RING * e + k // RING + 1))
                v.tensor_tensor_reduce(out=u, in0=u, in1=h2c[:, :], scale=1.0, scalar=0.0, op0=ALU.mult,
                                       op1=ALU.add, accum_out=act8[:, k % RING:k % RING + 1]).then_inc(dot_done, 1)
                if k:
                    diag(e, k - 1)

            def end(e):
                r = height(e)
                diag(e, groups_of(e) - 1)
                v.wait_ge(v_done, NG * e + groups_of(e))
                v.wait_ge(x1_in, 16 * (e + 1))
                if r == TS:
                    v.wait_ge(gate_in, 16)
                v.tensor_tensor(Pm[0:r, :], YY[0:r, :], gate[1][0:r, :], ALU.mult).then_inc(yg_done, 1)
                v.wait_ge(yg_done, e + 1)
                v.tensor_tensor(Pm[0:r, :], Pm[0:r, :], PTs[0:r, :], ALU.add).then_inc(y_ready, 1)

            def prologue():
                v.wait_ge(once_in, ONCE)
                v.wait_ge(cst, 1)
                v.tensor_copy(io16[:, :], io16i[:, :]).then_inc(cst, 1)
                v.tensor_reduce(fold[:, :], ident[:, :].rearrange("p (q t) -> p t q", t=TS), X, ALU.add).then_inc(cst, 1)
                v.wait_ge(cst, 3)

            iterate(v, step, group, begin, end, prologue)

        @block.tensor
        def _(pe):
            def weigh(h, t, nk):
                n = H * t + h + 1
                pe.wait_ge(pts_ready, n)
                for b in range(nk // P):
                    mm = pe.matmul(V0[:, h * HD:(h + 1) * HD], PTs[:, b * P:(b + 1) * P], V[:, b, h * HD:(h + 1) * HD],
                                   start=(b == 0), stop=(b == nk // P - 1))
                mm.then_inc(pv_done, 1)

            def step(s, t, nk):
                r = height(t)
                smp = r == TS
                if s == 0 and smp:
                    pe.wait_ge(smp_in, 64)
                    pe.wait_ge(fT_ready, t)
                    pe.wait_ge(h2_ready, t)
                    for g in range(2):
                        for c in range(CC):
                            mm = pe.transpose((SS, TT)[g][:, c * 120:(c + 1) * 120], state[:, g, c * P:(c + 1) * P],
                                              ident[0:120, 0:120])
                    mm.then_inc(stT_done, 1)
                if s < 2 * H and not smp:
                    h = s // 2
                    n = H * t + h + 1
                    if s % 2 == 0:
                        if h:
                            weigh(h - 1, t, nk)
                            pe.wait_ge(m_ready, n - 1)
                        else:
                            pe.wait_ge(q_in, 16 * (t + 1))
                            if some(t):
                                pe.wait_ge(fT_ready, t)
                                pe.wait_ge(sc_ready, H * t)
                        pe.wait_ge(k_in[h % 2], 64 * t + 16 * (h // 2 + 1))
                        for b in range(0, nk, 512):
                            o = slice(b, min(b + 512, nk))
                            mm = pe.matmul(SS[:, o], qTb[:, h, :], kh[h % 2][:, o],
                                           start=True, stop=True)
                        mm.then_inc(s_done, 1)
                    else:
                        pe.wait_ge(e_done, n)
                        if h == 0 and some(t):
                            pe.wait_ge(h2_ready, t)
                        for b in range(nk // P):
                            mm = pe.transpose(TT[:, b * P:(b + 1) * P], Pm[:, b * P:(b + 1) * P], ident[:, :])
                        mm.then_inc(pt_done, 1)
                if s == S_CONV:
                    if not smp:
                        weigh(H - 1, t, nk)
                    pe.wait_ge(conv_done, t + 1)
                    if some(t):
                        pe.wait_ge(qh_ready, H * t)
                    for c in range(CC):
                        mm = pe.transpose(M0[0:r, c * P:(c + 1) * P], yac[:, c, 0:r], ident[:, :])
                    mm.then_inc(yT_done, 1)
                if s == S_CONV + 2 and not smp:
                    pe.wait_ge(att_ready, t + 1)
                    for c in range(CC):
                        mm = pe.transpose(SS[:, c * P:(c + 1) * P], Pm[:, c * P:(c + 1) * P], ident[:, :])
                    mm.then_inc(attT_done, 1)
                if s in (S_CONV + 4, S_CONV + 5):
                    if not smp:
                        pe.wait_ge(attT_ready, t + 1)
                    project_out(s - S_CONV - 4, range(CC), r)
                if s == S_CONV + 7:
                    pe.wait_ge(yn_ready, t + 1)
                    for c in range(CC):
                        mm = pe.transpose(M0[:, c * P:c * P + r], Pm[0:r, 512 + c * P:512 + (c + 1) * P], ident[0:r, 0:r])
                    mm.then_inc(ynT_done, 1)
                if s in (S_CONV + 10, S_CONV + 11):
                    pe.wait_ge(catc_ready, t + 1)
                    mm = project_out(s - S_CONV - 10, range(CC, DC), r)
                    if s == S_CONV + 11:
                        mm.then_inc(wo_done, 1)
                if s == S_X1 + 5:
                    pe.wait_ge(xs_ready, t + 1)
                    for c in range(DC):
                        mm = pe.transpose(SS[:, c * P:c * P + r], Pm[0:r, c * P:(c + 1) * P], ident[0:r, 0:r])
                    mm.then_inc(x1T_done, 1)
                if s == S_ROUTE:
                    pe.wait_ge(fT_ready, t + 1)
                    for c in range(DC):
                        mm = pe.transpose(TT[:, c * P:(c + 1) * P], fT[:, c, :], ident[:, :])
                    mm.then_inc(h2_done, 1)
                if S_ROUTE + 1 <= s < S_ROUTE + 1 + H:
                    h = s - S_ROUTE - 1
                    pe.wait_ge(qh_ready, H * t + h + 1)
                    if some(t) or h:
                        pe.wait_ge(sc_ready, H * t + h)
                    for g in range(2):
                        mm = pe.matmul(V0[:, g * NK:(g + 1) * NK], qh[:, g, :], subk[:, h, g, :], start=True, stop=True)
                    mm.then_inc(sc_done, 1)
                if S_ROUTE <= s < S_ROUTE + H:
                    h = s - S_ROUTE
                    pe.wait_ge(wq_in[h % 2], 64 * t + 16 * (h // 2 + 1))
                    for g in range(2):
                        for k in range(DC):
                            mm = pe.matmul(M0[:, g * P:g * P + r], wq[h % 2][:, k, g * NK:(g + 1) * NK], fT[:, k, 0:r],
                                           start=(k == 0), stop=(k == DC - 1))
                    mm.then_inc(qd_done, 1)

            def project_out(g, chunks, r):
                for k in chunks:
                    mm = pe.matmul(TT[0:r, g * 512:(g + 1) * 512], fT[:, k, 0:r], w_o[:, k, g * 512:(g + 1) * 512],
                                   start=(k == 0), stop=(k == DC - 1), skip_group_check=True)
                return mm

            def sums(e, k):
                w = height(e)
                pe.wait_ge(diag_done, NG * e + k + 1)
                if k == 0 and some(e):
                    pe.wait_ge(y_ready, e)
                for g in range(2):
                    mm = pe.matmul(YY[0:w, g * 512:(g + 1) * 512], dg[:, k % DG, 0:w],
                                   ring[:, k % RING, D + g * 512:D + (g + 1) * 512],
                                   start=(k == 0), stop=(k == groups_of(e) - 1), skip_group_check=True)
                mm.then_inc(v_done, 1)

            def group(e, k):
                if k:
                    sums(e, k - 1)

            iterate(pe, step, group, lambda e: None, lambda e: sums(e, groups_of(e) - 1),
                    prologue=lambda: pe.wait_ge(once_in, ONCE))


def keys_of(t):
    return P if t == 0 else SEQ // 2 if t < NB // 2 else SEQ


def iterate(eng, step, group, begin, end, prologue):
    def both(t, nk):
        begin(t - 1)
        for s in range(STEPS):
            step(s, t, nk)
            for k in range(sum(PLAN[:s]), sum(PLAN[:s + 1])):
                group(t - 1, k)
        end(t - 1)

    assert sum(PLAN) == NG and len(PLAN) == STEPS
    prologue()
    for s in range(STEPS):
        step(s, 0, keys_of(0))
    both(1, keys_of(1))
    with eng.Fori(2, NB // 2) as t:
        both(t, SEQ // 2)
    with eng.Fori(NB // 2, NB) as t:
        both(t, SEQ)
    both(NB, 0)
    begin(NB)
    for k in range(NG_S):
        group(NB, k)
    end(NB)


def build(nc, I, O, S):
    with ExitStack() as ctx:
        K = {}
        for name, shape in (("ident", [P, P]), ("tri", [P, P]), ("ones", [P, P]), ("modT", [P, 48, M]),
                            ("sgT", [P, 2, DC, M])):
            K[name] = ctx.enter_context(nc.sbuf_tensor(name, shape, F32))
        condition(nc, I, S, K)
        project(nc, I, O, S, K)
        sampled(nc, I, O, S, K)
        tail(nc, I, O, S, K)


_OUTS = [("y_prompt", (SEQ, D)), ("y_sample", (TS, D)), ("k_prompt", (SEQ, DA)), ("v_prompt", (SEQ, DA)),
         ("logf_prompt", (SEQ, H)), ("conv_prompt", (W - 1, DA)), ("k_sample", (TS, DA)), ("v_sample", (TS, DA)),
         ("logf_sample", (TS, H)), ("conv_sample", (NS, W - 1, DA))]
_SHAPES = [(1, SEQ, D), (NS, QS, D), (1, 1, SEQ, H, HD), (1, 1, SEQ, H, HD), (1, 1, SEQ, H), (1, 1, W - 1, DA),
           (1, NS, QS, H, HD), (1, NS, QS, H, HD), (1, NS, QS, H), (1, NS, W - 1, DA)]
_SCRATCH = {"uT": (P, CC, W - 1 + SEQ), "uTs": (P, CC, TS), "qT": (AUG, H, SEQ), "kT": (AUG, H, SEQ),
            "qTs": (P, CC, TS), "kTs": (P, CC, TS), "attTs": (P, CC, TS), "x1": (NB + 1, P, D),
            "gate": (2, P, D), "gate_s": (2, TS, D)}


def kernel(**inputs):
    import numpy as np
    import concourse.bacc as _bacc
    from concourse.bass_utils import run_bass_kernel_spmd as _run

    g = {n: np.asarray(a) for n, a in inputs.items()}
    col = lambda a: np.ascontiguousarray(a.reshape(-1, P).T)
    arrays = {
        "x_prompt": g["x_prompt"].reshape(SEQ, D), "x_sample": g["x_sample"].reshape(TS, D),
        "cT": np.concatenate([g["c_prompt"], g["c_sample"]]).reshape(M, DC, P).transpose(2, 1, 0),
        "w_ada": g["w_ada"][0], "b_adaT": col(g["b_ada"][0]),
        "norm_gT": np.stack([g["norm1_g"][0].reshape(DC, P).T, g["norm2_g"][0].reshape(DC, P).T], axis=1),
        "w_in": g["w_in"][0], "q_g": g["q_norm_g"], "k_g": g["k_norm_g"], "b_f": g["b_f"],
        "b_gluT": g["b_glu"][0].reshape(2, CC, P).transpose(2, 0, 1),
        "state_conv": g["state_conv"][0],
        "w_o": g["w_o"][0], "w_query": g["peer_w_query"][0],
        "subkT": g["peer_sub_keys"][0].transpose(3, 0, 1, 2), "conv_wT": g["conv_w"][0].reshape(W, CC, P).transpose(2, 1, 0),
        "conv_v": np.stack([g[n][0].reshape(CC, P).T for n in ("conv_b", "conv_ln_g", "conv_ln_b")], axis=1),
        "experts": np.concatenate([g["peer_u"][0], g["peer_v"][0]], axis=1),
        "cache_k": g["cache_k"][0].reshape(-1, DA), "cache_v": g["cache_v"][0].reshape(-1, DA),
        "cache_logf": g["cache_logf"][0].reshape(-1, H), "page_table": g["page_table"].reshape(1, -1),
    }
    nc = _bacc.Bacc("TRN2", target_bir_lowering=False, num_devices=1)
    feed, I = {}, {}
    for n, a in arrays.items():
        feed[f"{n}_dram"] = a = np.ascontiguousarray(a)
        I[n] = nc.dram_tensor(f"{n}_dram", a.shape, mybir.dt.from_np(a.dtype), kind="ExternalInput").ap()
    O = {n: nc.dram_tensor(f"{n}_dram_out", s, F32, kind="ExternalOutput").ap() for n, s in _OUTS}
    S = {n: nc.dram_tensor(f"{n}_scratch", s, F32, kind="Internal").ap() for n, s in _SCRATCH.items()}
    S["mask"] = nc.dram_tensor("mask_scratch", (P, 2 * SEQ - P), BF16, kind="Internal").ap()
    build(nc, I, O, S)
    r = _run(nc, [feed], core_ids=[0])
    return tuple(r.results[0][f"{n}_dram_out"].reshape(s) for (n, _), s in zip(_OUTS, _SHAPES))
```

```python
from contextlib import ExitStack

import concourse.bass as bass
from concourse import mybir

F32 = mybir.dt.float32
BF16 = mybir.dt.bfloat16
I32 = mybir.dt.int32
U32 = mybir.dt.uint32
ALU = mybir.AluOpType
ACT = mybir.ActivationFunctionType
X = mybir.AxisListType.X

P = 128
D = 1024
DC = D // P
SEQ = 1024
NB = SEQ // P
NS = 8
QS = 4
TS = NS * QS
H = 8
HD = 64
DA = H * HD
CC = 4
W = 31
ZQ, ZK, ZV, ZF, ZG = 0, DA, 2 * DA, 3 * DA, 3 * DA + H
DIN = 3 * DA + H + 2 * CC * P
M = 1 + NS
EPS = 1e-6
AUG = HD + 2


def rows(t):
    return TS if isinstance(t, int) and t == 0 else P


def some(n):
    return not isinstance(n, int) or n > 0


class Own:

    def __init__(self, eng, sem):
        self.eng, self.sem, self.base, self.n = eng, sem, 0, 0

    def start(self, base):
        self.base, self.n = base, 0

    def step(self, ins):
        ins.then_inc(self.sem, 1)
        self.n += 1

    def settle(self):
        self.eng.wait_ge(self.sem, self.base + self.n)

    def carry(self):
        self.eng.sem_inc(self.carrier, 1)

    def do(self, ins):
        self.step(ins)
        self.settle()


def condition(nc, I, S, K, w_in_load):
    with ExitStack() as ctx:
        sb = lambda n, s, d=F32: ctx.enter_context(nc.sbuf_tensor(n, s, d))
        sem = lambda n: ctx.enter_context(nc.semaphore(n))
        wa = [sb(f"wa{i}", [P, DC, 512]) for i in range(3)]
        cT = sb("cT", [P, DC, M])
        bT = sb("bT", [P, 48])
        ng = sb("ng", [P, 2, DC])
        gS, gate, gate_s = sb("gS", [P, 2, DC, TS]), sb("gate", [P, 2, D]), sb("gate_s", [TS, 2, D])
        mod = sb("mod", [M, 6 * D])
        wide = sb("wide", [P, 2 * SEQ - P], BF16)
        mod_bank = ctx.enter_context(nc.psum_tensor("mod_bank", [P, 512], F32))
        mod_ps = mod_bank[:, 0:48 * M].rearrange("p (n m) -> p n m", m=M)
        row_ps = [ctx.enter_context(nc.psum_tensor(f"row_ps{i}", [P, 512], F32)) for i in range(3)]
        gate_ps = [ctx.enter_context(nc.psum_tensor(f"gate_ps{i}", [P, 512], F32)) for i in range(4)]
        ada_in = [sem(f"c_w{i}") for i in range(3)]
        rows_copied, modT_done = sem("c_rows"), sem("c_modT")
        small_in, w_used, id_step = sem("c_small"), sem("c_used"), sem("c_id")
        own_v, gates, gates_out = sem("c_own"), sem("c_gates"), sem("c_gout")
        stored = sem("c_stored")
        wv = I["w_ada"].rearrange("(k p) n -> p k n", p=P)
        modT, sgT, ident = K["modT"], K["sgT"], K["ident"]
        NCH = 12
        block = ctx.enter_context(nc.Block())

        @block.sync
        def _(sp):
            sp.dma_start(cT[:, :, :], I["cT"]).then_inc(small_in, 16)
            sp.dma_start(bT[:, :], I["b_adaT"]).then_inc(small_in, 16)
            sp.dma_start(ng[:, :, :], I["norm_gT"]).then_inc(small_in, 16)
            for n in range(NCH):
                if n >= 3:
                    sp.wait_ge(w_used, n - 2)
                sp.dma_start(wa[n % 3][:, :, :], wv[:, :, n * 512:(n + 1) * 512]).then_inc(ada_in[n % 3], 16)
            sp.dma_start(K["w_in"][:, :, :], I["w_in"].rearrange("(k p) n -> p k n", p=P)).then_inc(w_in_load, 16)
            sp.wait_ge(id_step, 7)
            sp.dma_start(S["mask"], wide[:, :]).then_inc(stored, 16)
            sp.wait_ge(gates_out, 2)
            for g in range(2):
                sp.dma_start(S["gate"][g], gate[:, g, :]).then_inc(stored, 16)
                sp.dma_start(S["gate_s"][g], gate_s[:, g, :]).then_inc(stored, 16)
            sp.wait_ge(stored, 16 * 5)

        @block.gpsimd
        def _(pool):
            pool.memset(ident[:, :], 0.0).then_inc(id_step, 1)
            pool.memset(K["tri"][:, :], 1.0).then_inc(id_step, 1)
            pool.memset(K["ones"][:, :], 1.0).then_inc(id_step, 1)
            pool.memset(wide[:, :], 0.0).then_inc(id_step, 1)
            pool.wait_ge(id_step, 4)
            pool.affine_select(out=ident[:, :], in_=ident[:, :], compare_op=ALU.not_equal, fill=1.0, base=0,
                               pattern=[[-1, P]], channel_multiplier=1).then_inc(id_step, 1)
            pool.affine_select(out=K["tri"][:, :], in_=K["tri"][:, :], compare_op=ALU.is_ge, fill=0.0, base=0,
                               pattern=[[1, P]], channel_multiplier=-1).then_inc(id_step, 1)
            pool.affine_select(out=wide[:, :], in_=wide[:, :], compare_op=ALU.is_ge, fill=-1e30, base=SEQ - P,
                               pattern=[[-1, 2 * SEQ - P]], channel_multiplier=1).then_inc(id_step, 1)

        @block.tensor
        def _(pe):
            pe.wait_ge(small_in, 48)

            def to_columns(n):
                pe.wait_ge(rows_copied, n + 1)
                for j in range(4):
                    mm = pe.transpose(mod_ps[:, 4 * n + j, :], mod[:, n * 512 + j * P:n * 512 + (j + 1) * P],
                                      ident[0:M, 0:M])
                mm.then_inc(modT_done, 1)

            pe.wait_ge(id_step, 5)
            for n in range(NCH):
                pe.wait_ge(ada_in[n % 3], 16 * (n // 3 + 1))
                if n >= 3:
                    pe.wait_ge(rows_copied, n - 2)
                for k in range(DC):
                    mm = pe.matmul(row_ps[n % 3][0:M, :], cT[:, k, :], wa[n % 3][:, k, :], start=(k == 0), stop=(k == DC - 1))
                mm.then_inc(w_used, 1)
                if n:
                    to_columns(n - 1)
            to_columns(NCH - 1)

            pe.wait_ge(own_v, 1)
            pe.wait_ge(id_step, 6)
            for g, first in ((0, 16), (1, 40)):
                for half in range(2):
                    for c in range(4):
                        mm = pe.matmul(gate_ps[2 * g + half][:, c * P:(c + 1) * P],
                                       modT[:, first + 4 * half + c, 0:1].to_broadcast([P, P]),
                                       ident[:, :], start=True, stop=True)
            mm.then_inc(gates, 1)
            pe.wait_ge(gates_out, 1)
            for g, first in ((0, 16), (1, 40)):
                for half in range(2):
                    for c in range(4):
                        mm = pe.matmul(gate_ps[2 * g + half][0:TS, c * P:(c + 1) * P],
                                       gS[:, g, 4 * half + c, :],
                                       ident[:, :], start=True, stop=True)
            mm.then_inc(gates, 1)

        @block.vector
        def _(v):
            own = Own(v, own_v)
            for n in range(NCH):
                v.wait_ge(w_used, n + 1)
                v.tensor_copy(mod[:, n * 512:(n + 1) * 512], row_ps[n % 3][0:M, :]).then_inc(rows_copied, 1)
            v.wait_ge(modT_done, NCH)
            v.wait_ge(small_in, 48)
            own.do(v.tensor_tensor(modT[:, :, :], mod_ps[:, :, :],
                                   bT[:, :].unsqueeze(2).to_broadcast([P, 48, M]), ALU.add))
            for i, first in ((0, 8), (1, 32)):
                own.do(v.tensor_scalar(sgT[:, i, :, :], modT[:, first:first + DC, :], 1.0, None, ALU.add))
                own.do(v.tensor_tensor(sgT[:, i, :, :], sgT[:, i, :, :],
                                       ng[:, i, :].unsqueeze(2).to_broadcast([P, DC, M]), ALU.mult))
                for c in range(DC):
                    fr = modT[:, (16, 40)[i] + c, 1:M].unsqueeze(2).to_broadcast([P, NS, QS])
                    own.do(v.tensor_copy(gS[:, i, c, :].rearrange("p (n q) -> p n q", n=NS), fr))
            v.wait_ge(gates, 1)
            for g in range(2):
                for half in range(2):
                    own.do(v.tensor_copy(gate[:, g, half * 512:(half + 1) * 512], gate_ps[2 * g + half][:, :]))
            v.sem_inc(gates_out, 1)
            v.wait_ge(gates, 2)
            for g in range(2):
                for half in range(2):
                    own.do(v.tensor_copy(gate_s[0:TS, g, half * 512:(half + 1) * 512],
                                         gate_ps[2 * g + half][0:TS, :]))
            v.sem_inc(gates_out, 1)


def project(nc, I, O, S, K, w_in_load):
    with ExitStack() as ctx:
        sb = lambda n, s, d=F32: ctx.enter_context(nc.sbuf_tensor(n, s, d))
        sem = lambda n: ctx.enter_context(nc.semaphore(n))
        w_in = K["w_in"]
        xb = sb("xb", [P, D])
        xs = sb("xs", [P, D])
        sqx = sb("sqx", [P, D])
        sqq = sb("sqq", [P, 2 * DA])
        hT = sb("hT", [P, DC, P])
        st = sb("st", [P, 8])
        sh = sb("sh", [P, 8, 2 * H])
        lf = sb("lf", [P, 8, H])
        lacc = sb("lacc", [P, H])
        qa = sb("qa", [P, H, AUG])
        ka = sb("ka", [P, H, AUG])
        vb = sb("vb", [P, DA])
        qTb = sb("qTb", [P, H, P])
        kTb = sb("kTb", [P, H, P])
        eg = sb("eg", [P, CC, P])
        uT = sb("uT", [P, CC, P])
        ub = sb("ub", [P, DA])
        gq = sb("gq", [P, HD])
        gk = sb("gk", [P, HD])
        bf = sb("bf", [P, H])
        bg = sb("bg", [P, 2, CC])
        nbg = sb("nbg", [P, CC])
        zero = sb("zero", [P, CC, W - 1])
        A = [ctx.enter_context(nc.psum_tensor(f"A{i}", [P, 512], F32)) for i in range(8)]

        small_in, x_in = sem("p_small"), sem("p_x")
        ss_ready, ms_ready, r0_ready, xs_ready = sem("p_ss"), sem("p_ms"), sem("p_r0"), sem("p_xs")
        xT_done, hT_ready, qkv_done, fg_done, glu_done = sem("p_xT"), sem("p_hT"), sem("p_qkv"), sem("p_fg"), sem("p_glu")
        sqq_ready, hms_ready, hr0_ready, qk_ready = sem("p_sqq"), sem("p_hms"), sem("p_hr0"), sem("p_qk")
        v_ready, la_ready, lln_ready, logf_ready = sem("p_v"), sem("p_la"), sem("p_lln"), sem("p_logf")
        F_done, Fq_ready, qkT_done, qkT_ready = sem("p_F"), sem("p_Fq"), sem("p_qkT"), sem("p_qkTr")
        eg_ready, u_ready, uTT_done, ub_ready = sem("p_eg"), sem("p_u"), sem("p_uTT"), sem("p_ub")
        stored_k, stored_v, stored_l, stored_qk, stored_u = sem("p_ok"), sem("p_ov"), sem("p_ol"), sem("p_oqk"), sem("p_ou")
        once_out = sem("p_once")
        ubs_ready, ubs_out, cst2 = sem("p_ubs"), sem("p_ubso"), sem("p_cst2")
        own_v, own_a, own_p, cst = sem("p_ownv"), sem("p_owna"), sem("p_ownp"), sem("p_cst")
        OV, OA = 17, 1
        OVN, OAN = 4, 1
        ident = K["ident"]
        block = ctx.enter_context(nc.Block())

        @block.sync
        def _(sp):
            sp.dma_start(xb[0:TS, :], I["x_sample"]).then_inc(x_in, 16)
            for dst, src in ((gq[:, :], I["q_g"].to_broadcast([P, HD])), (gk[:, :], I["k_g"].to_broadcast([P, HD])),
                             (bf[:, :], I["b_f"].to_broadcast([P, H])), (bg[:, :, :], I["b_gluT"])):
                sp.dma_start(dst, src).then_inc(small_in, 16)
            sp.dma_start(O["conv_sample"][:, 0:W - 1 - QS, :], I["state_conv"][:, QS:W - 1, :]).then_inc(once_out, 16)
            sp.wait_ge(cst, 1)
            sp.dma_start(S["uT"][:, :, 0:W - 1], zero[:, :, :]).then_inc(once_out, 16)

            def load_x(t, at):
                sp.wait_ge(xs_ready, t)
                sp.dma_start(xb[:, :], I["x_prompt"][bass.ds(at, P), :]).then_inc(x_in, 16)

            def store(t, n, at, u_at):
                r = rows(t)
                sp.wait_ge(v_ready, n)
                if r == TS:
                    sp.dma_start(O["v_sample"], vb[0:r, :]).then_inc(stored_v, 16)
                else:
                    sp.dma_start(O["v_prompt"][bass.ds(at, P), :], vb[:, :]).then_inc(stored_v, 16)
                sp.wait_ge(logf_ready, n)
                if r == TS:
                    sp.dma_start(O["logf_sample"], lf[0:r, 5, :]).then_inc(stored_l, 16)
                else:
                    sp.dma_start(O["logf_prompt"][bass.ds(at, P), :], lf[:, 5, :]).then_inc(stored_l, 16)
                sp.wait_ge(qk_ready, n)
                if r == TS:
                    sp.dma_start(O["k_sample"].rearrange("t (h d) -> t h d", h=H), ka[0:r, :, 0:HD]).then_inc(stored_k, 16)
                else:
                    sp.dma_start(O["k_prompt"][bass.ds(at, P), :].rearrange("t (h d) -> t h d", h=H),
                                 ka[:, :, 0:HD]).then_inc(stored_k, 16)
                sp.wait_ge(u_ready, n)
                if r == TS:
                    sp.dma_start(S["uTs"], uT[:, :, 0:TS]).then_inc(stored_u, 16)
                else:
                    sp.dma_start(S["uT"][:, :, bass.ds(u_at, P)], uT[:, :, :]).then_inc(stored_u, 16)
                sp.wait_ge(qkT_ready, n)
                if r == TS:
                    sp.dma_start(S["qTs"], qTb[:, 0:CC, 0:TS]).then_inc(stored_qk, 16)
                    sp.dma_start(S["kTs"], kTb[:, 0:CC, 0:TS]).then_inc(stored_qk, 16)
                else:
                    sp.dma_start(S["qT"][:, :, bass.ds(at, P)], qTb[0:AUG, :, :]).then_inc(stored_qk, 16)
                    sp.dma_start(S["kT"][:, :, bass.ds(at, P)], kTb[0:AUG, :, :]).then_inc(stored_qk, 16)

            load_x(1, 0)
            store(0, 1, None, None)
            sp.wait_ge(ubs_ready, 1)
            sp.dma_start(O["conv_sample"][:, W - 1 - QS:W - 1, :], ub[0:TS, :]).then_inc(ubs_out, 16)
            for t in range(1, NB):
                load_x(t + 1, t * P)
                store(t, t + 1, (t - 1) * P, (t - 1) * P + W - 1)
            store(NB, NB + 1, (NB - 1) * P, (NB - 1) * P + W - 1)
            sp.wait_ge(ub_ready, 1)
            sp.dma_start(O["conv_prompt"], ub[P - (W - 1):P, :]).then_inc(once_out, 16)
            sp.wait_ge(once_out, 16 * 3)
            for s, n in ((stored_k, 1), (stored_v, 1), (stored_l, 1), (stored_u, 1), (stored_qk, 2)):
                sp.wait_ge(s, 16 * n * (NB + 1))

        @block.gpsimd
        def _(pool):
            pool.memset(zero[:, :, :], 0.0).then_inc(cst, 1)
            pool.memset(lacc[:, :], 0.0).then_inc(own_p, 1)
            pool.memset(qa[:, :, HD + 1:AUG], 1.0).then_inc(own_p, 1)
            pool.memset(ka[:, :, HD:HD + 1], 1.0).then_inc(own_p, 1)
            pool.wait_ge(small_in, 64)
            pool.wait_ge(own_p, 3)
            pool.tensor_scalar(nbg[:, :], bg[:, 1, :], -1.0, None, ALU.mult).then_inc(own_p, 1)
            pool.tensor_scalar(gq[:, :], gq[:, :], HD ** -0.5, None, ALU.mult).then_inc(own_p, 1)

        @block.scalar
        def _(act):
            own = Own(act, own_a)

            def norm_x(t):
                r = rows(t)
                act.wait_ge(x_in, 16 * t + 16)
                act.activation(sqx[0:r, :], xb[0:r, :], ACT.Square, accum_out=st[0:r, 0:1]).then_inc(ss_ready, 1)
                act.wait_ge(ms_ready, t + 1)
                own.start(t)
                own.do(act.activation(st[0:r, 2:3], st[0:r, 1:2], ACT.Ln))
                act.activation(st[0:r, 3:4], st[0:r, 2:3], ACT.Exp, scale=-0.5).then_inc(r0_ready, 1)

            def body(t, more=True):
                r = rows(t)
                if more:
                    norm_x(t + 1)
                act.wait_ge(qkv_done, 3 * t + 3)
                act.activation(sqq[0:r, 0:DA], A[2][0:r, :], ACT.Square)
                act.activation(sqq[0:r, DA:2 * DA], A[3][0:r, :], ACT.Square).then_inc(sqq_ready, 1)
                if not isinstance(t, int) or t > 0:
                    act.wait_ge(stored_v, 16 * t)
                act.activation(vb[0:r, :], A[4][0:r, :], ACT.Copy).then_inc(v_ready, 1)
                act.wait_ge(hms_ready, t + 1)
                act.activation(sh[0:r, 2, :], sh[0:r, 1, :], ACT.Ln).then_inc(hr0_ready, 1)
                act.wait_ge(hr0_ready, 2 * t + 1)
                act.activation(sh[0:r, 3, :], sh[0:r, 2, :], ACT.Exp, scale=-0.5).then_inc(hr0_ready, 1)
                act.wait_ge(la_ready, t + 1)
                act.activation(lf[0:r, 2, :], lf[0:r, 1, :], ACT.Exp, scale=-1.0).then_inc(lln_ready, 1)
                act.wait_ge(lln_ready, 2 * t + 1)
                act.activation(lf[0:r, 3, :], lf[0:r, 2, :], ACT.Ln, bias=1.0).then_inc(lln_ready, 1)
                act.wait_ge(glu_done, t + 1)
                for c in range(CC):
                    a = act.activation(eg[:, c, 0:r], A[1][:, c * P:c * P + r], ACT.Exp, scale=-1.0,
                                       bias=nbg[:, c:c + 1])
                a.then_inc(eg_ready, 1)
                if more:
                    act.wait_ge(xT_done, t + 2)
                    for c in range(DC):
                        a = act.activation(hT[:, c, :], A[6 + c // 4][:, (c % 4) * P:(c % 4 + 1) * P], ACT.Identity,
                                           scale=K["sgT"][:, 0, c, 0:1], bias=K["modT"][:, c, 0:1])
                    a.then_inc(hT_ready, 1)
                act.wait_ge(qkT_done, t + 1)
                if not isinstance(t, int) or t > 0:
                    act.wait_ge(stored_qk, 32 * t)
                if r == P:
                    for i, dst in enumerate((qTb, kTb)):
                        for g in range(2):
                            a = act.activation(dst[0:AUG, 4 * g:4 * g + 4, :].rearrange("p h t -> p (h t)"),
                                               A[2 + 2 * i + g][0:AUG, :], ACT.Copy)
                else:
                    for i, dst in enumerate((qTb, kTb)):
                        a = act.activation(dst[:, 0:CC, 0:TS],
                                           A[2 + 2 * i][:, 0:CC * TS].rearrange("p (c t) -> p c t", c=CC), ACT.Copy)
                a.then_inc(qkT_ready, 1)

            act.wait_ge(own_p, 5)
            norm_x(0)
            body(0)
            with act.Fori(1, NB) as t:
                body(t)
            body(NB, False)

        @block.vector
        def _(v):
            own = Own(v, own_v)

            def newton(m, r0, a, b, r):
                own.do(v.tensor_tensor(a, r0, r0, ALU.mult))
                own.do(v.tensor_tensor(b, a, m, ALU.mult))
                own.do(v.tensor_scalar(a, b, -0.5, 1.5, ALU.mult, ALU.add))
                return v.tensor_tensor(r, a, r0, ALU.mult)

            def norm_x(t):
                r = rows(t)
                v.wait_ge(ss_ready, t + 1)
                v.tensor_scalar(st[0:r, 1:2], st[0:r, 0:1], 1.0 / D, EPS, ALU.mult, ALU.add).then_inc(ms_ready, 1)
                v.wait_ge(r0_ready, t + 1)
                own.start(OVN * t + (0 if isinstance(t, int) and t == 0 else OV * (t - 1)))
                own.do(newton(st[0:r, 1:2], st[0:r, 3:4], st[0:r, 4:5], st[0:r, 5:6], st[0:r, 7:8]))
                if not isinstance(t, int) or t > 0:
                    v.wait_ge(xT_done, t)
                v.tensor_scalar(xs[0:r, :], xb[0:r, :], st[0:r, 7:8], None, ALU.mult).then_inc(xs_ready, 1)
                assert own.n == OVN

            def body(t, more=True):
                r = rows(t)
                if r == TS:
                    own.start(OVN)
                    v.wait_ge(xT_done, 1)
                    for g in range(2):
                        ps = A[6 + g][:, :].rearrange("p (c n) -> p c n", c=4)
                        for c in range(4):
                            o = hT[:, 4 * g + c, 0:TS].rearrange("p (n q) -> p n q", n=NS)
                            i = ps[:, c, 0:TS].rearrange("p (n q) -> p n q", n=NS)
                            cc = 4 * g + c
                            v.tensor_tensor(o, i, K["sgT"][:, 0, cc, 1:M].unsqueeze(2).to_broadcast([P, NS, QS]),
                                            ALU.mult).then_inc(cst2, 1)
                            v.wait_ge(cst2, 2 * cc + 1)
                            v.tensor_tensor(o, o, K["modT"][:, cc, 1:M].unsqueeze(2).to_broadcast([P, NS, QS]),
                                            ALU.add).then_inc(cst2, 1)
                    v.wait_ge(cst2, 2 * DC)
                    v.sem_inc(hT_ready, 1)
                if more:
                    norm_x(t + 1)
                own.start(OVN * (t + 2) + OV * t if more else OVN * (t + 1) + OV * t)
                v.wait_ge(fg_done, t + 1)
                if not isinstance(t, int) or t > 0:
                    v.wait_ge(stored_l, 16 * t)
                own.do(v.tensor_tensor(lf[0:r, 0, :], A[5][0:r, 0:H], bf[0:r, :], ALU.add))
                own.do(v.tensor_scalar(lf[0:r, 4, :], lf[0:r, 0, :], -1.0, None, ALU.mult))
                v.tensor_tensor(lf[0:r, 1, :], lf[0:r, 0, :], lf[0:r, 4, :], ALU.max).then_inc(la_ready, 1)
                own.do(v.tensor_scalar(lf[0:r, 6, :], lf[0:r, 0, :], 0.0, None, ALU.min))
                v.wait_ge(sqq_ready, t + 1)
                own.do(v.tensor_reduce(sh[0:r, 0, :], sqq[0:r, :].rearrange("p (h d) -> p h d", d=HD), X, ALU.add))
                v.tensor_scalar(sh[0:r, 1, :], sh[0:r, 0, :], 1.0 / HD, EPS, ALU.mult, ALU.add).then_inc(hms_ready, 1)
                v.wait_ge(lln_ready, 2 * t + 2)
                own.settle()
                v.tensor_tensor(lf[0:r, 5, :], lf[0:r, 6, :], lf[0:r, 3, :], ALU.subtract).then_inc(logf_ready, 1)
                v.wait_ge(hr0_ready, 2 * t + 2)
                own.do(newton(sh[0:r, 1, :], sh[0:r, 3, :], sh[0:r, 4, :], sh[0:r, 5, :], sh[0:r, 7, :]))
                if not isinstance(t, int) or t > 0:
                    v.wait_ge(stored_k, 16 * t)
                    v.wait_ge(qkT_done, t)
                for i, (dst, g) in enumerate(((qa, gq), (ka, gk))):
                    o = dst[0:r, :, 0:HD]
                    own.do(v.tensor_tensor(o, A[2 + i][0:r, :].rearrange("p (h d) -> p h d", h=H),
                                           sh[0:r, 7, i * H:(i + 1) * H].unsqueeze(2).to_broadcast([r, H, HD]), ALU.mult))
                    own.step(v.tensor_tensor(o, o, g[0:r, :].unsqueeze(1).to_broadcast([r, H, HD]), ALU.mult))
                own.settle()
                if r == TS:
                    for i, src in enumerate((qa, ka)):
                        v.tensor_copy(sqq[0:r, i * DA:(i + 1) * DA].rearrange("p (h d) -> p h d", h=H),
                                      src[0:r, :, 0:HD]).then_inc(cst2, 1)
                    v.wait_ge(cst2, 2 * DC + 2)
                v.sem_inc(qk_ready, 1)
                v.wait_ge(F_done, t + 1)
                if r == P:
                    own.step(v.tensor_copy(qa[:, :, HD], A[5][:, 16:16 + H]))
                    own.step(v.tensor_scalar(ka[:, :, HD + 1], A[5][:, 16:16 + H], -1.0, None, ALU.mult))
                    own.step(v.tensor_tensor(lacc[:, :], lacc[:, :], lf[:, 5, :], ALU.add))
                    own.settle()
                else:
                    for _ in range(3):
                        own.step(v.nop())
                    own.settle()
                v.sem_inc(Fq_ready, 1)
                v.wait_ge(eg_ready, t + 1)
                own.do(v.tensor_scalar(eg[:, :, 0:r], eg[:, :, 0:r], 1.0, None, ALU.add))
                own.do(v.reciprocal(eg[:, :, 0:r], eg[:, :, 0:r]))
                if not isinstance(t, int) or t > 0:
                    v.wait_ge(stored_u, 16 * t)
                for c in range(CC):
                    a = v.scalar_tensor_tensor(uT[:, c, 0:r], A[0][:, c * P:c * P + r], bg[:, 0, c:c + 1],
                                               eg[:, c, 0:r], ALU.add, ALU.mult)
                a.then_inc(u_ready, 1)
                assert own.n == OV, own.n

            v.wait_ge(own_p, 5)
            norm_x(0)
            body(0)
            v.wait_ge(uTT_done, 1)
            v.tensor_copy(ub[0:TS, :], A[0][0:TS, :]).then_inc(ubs_ready, 1)
            with v.Fori(1, NB) as t:
                body(t)
            body(NB, False)
            v.wait_ge(uTT_done, 2)
            v.wait_ge(ubs_out, 16)
            v.tensor_copy(ub[:, :], A[0][:, :]).then_inc(ub_ready, 1)

        @block.tensor
        def _(pe):
            def rows_up(t):
                r = rows(t)
                pe.wait_ge(xs_ready, t + 1)
                if some(t):
                    pe.wait_ge(hT_ready, t)
                for c in range(DC):
                    mm = pe.transpose(A[6 + c // 4][:, (c % 4) * P:(c % 4) * P + r], xs[0:r, c * P:(c + 1) * P],
                                      ident[0:r, 0:r])
                mm.then_inc(xT_done, 1)

            def body(t, more=True):
                r = rows(t)
                pe.wait_ge(hT_ready, t + 1)
                if some(t):
                    pe.wait_ge(qkT_ready, t)
                for k in range(DC):
                    mm = pe.matmul(A[5][0:r, 0:H], hT[:, k, 0:r], w_in[:, k, ZF:ZF + H], start=(k == 0), stop=(k == DC - 1))
                mm.then_inc(fg_done, 1)
                for j in range(3):
                    for k in range(DC):
                        mm = pe.matmul(A[2 + j][0:r, :], hT[:, k, 0:r], w_in[:, k, j * DA:(j + 1) * DA],
                                       start=(k == 0), stop=(k == DC - 1))
                    mm.then_inc(qkv_done, 1)
                if some(t):
                    pe.wait_ge(u_ready, t)
                for j in range(2 * CC):
                    for k in range(DC):
                        mm = pe.matmul(A[j // CC][:, (j % CC) * P:(j % CC) * P + r],
                                       w_in[:, k, ZG + j * P:ZG + (j + 1) * P], hT[:, k, 0:r],
                                       start=(k == 0), stop=(k == DC - 1))
                mm.then_inc(glu_done, 1)
                pe.wait_ge(logf_ready, t + 1)
                if r == P:
                    pe.matmul(A[5][:, 16:16 + H], K["tri"][:, :], lf[:, 5, :], start=True, stop=False)
                    pe.matmul(A[5][:, 16:16 + H], K["ones"][:, :], lacc[:, :], start=False, stop=True).then_inc(F_done, 1)
                else:
                    pe.nop().then_inc(F_done, 1)
                if more:
                    rows_up(t + 1)
                pe.wait_ge(qk_ready, t + 1)
                pe.wait_ge(Fq_ready, t + 1)
                pe.wait_ge(v_ready, t + 1)
                if r == P:
                    for i, src in enumerate((qa, ka)):
                        for h in range(H):
                            mm = pe.transpose(A[2 + 2 * i + h // 4][0:AUG, (h % 4) * P:(h % 4 + 1) * P],
                                              src[:, h, :], ident[:, :])
                else:
                    for i, src in enumerate((qa, ka)):
                        for c in range(CC):
                            mm = pe.transpose(A[2 + 2 * i][:, c * TS:(c + 1) * TS],
                                              sqq[0:r, i * DA + c * P:i * DA + (c + 1) * P], ident[0:r, 0:r])
                mm.then_inc(qkT_done, 1)

            def u_rows(r):
                for c in range(CC):
                    mm = pe.transpose(A[0][0:r, c * P:(c + 1) * P], uT[:, c, 0:r], ident[:, :])
                mm.then_inc(uTT_done, 1)

            pe.wait_ge(w_in_load, 16)
            rows_up(0)
            body(0)
            pe.wait_ge(u_ready, 1)
            u_rows(TS)
            pe.wait_ge(ubs_ready, 1)
            with pe.Fori(1, NB) as t:
                body(t)
            body(NB, False)
            pe.wait_ge(u_ready, NB + 1)
            u_rows(P)


def sampled(nc, I, O, S, K):
    NP = 4
    with ExitStack() as ctx:
        sb = lambda n, s, d=F32: ctx.enter_context(nc.sbuf_tensor(n, s, d))
        sem = lambda n: ctx.enter_context(nc.semaphore(n))
        psum = lambda n: ctx.enter_context(nc.psum_tensor(n, [P, 512], F32))
        pages = sb("pages", [P, NS * NP, 2 * DA + H])
        KT = sb("KT", [P, 2, CC, NP * P])
        idx = sb("idx", [P, NS * NP], I32)
        pt = sb("pt", [P, NS * NP], I32)
        lane = sb("lane", [P, 1], I32)
        lanef = sb("lanef", [P, 1])
        qT = sb("s_qT", [P, CC, TS])
        kT = sb("s_kT", [P, CC, TS])
        vs = sb("s_v", [TS, DA])
        ls = sb("s_l", [TS, H])
        Qbd = sb("Qbd", [P, CC, NS, H, QS])
        later = sb("later", [P, 896])
        later32 = sb("later32", [TS, TS])
        upto = sb("upto", [TS, NS, QS])
        uptoh = sb("uptoh", [TS, NS, H, QS])
        eqh = sb("eqh", [TS, NS, H, QS])
        L = sb("L", [TS, NS, H, QS])
        Lb = sb("Lb", [P, NS * NP, H, QS])
        hrow = sb("hrow", [H, P])
        hcol = sb("hcol", [H, DA])
        ones5 = sb("ones5", [TS, 512])
        hm = sb("hm", [P, DA])
        selS = sb("selS", [P, 2, TS])
        mown = sb("mown", [P, 2, TS])
        So = sb("So", [P, 2, TS])
        Pm = sb("Pm", [P, 2, 512 + TS])
        PT = sb("PT", [P, 2, NP, P])
        PTo = sb("PTo", [TS, 2, P])
        Om = sb("Om", [P, 2, DA])
        sm = sb("sm", [P, 2, 8])
        aT = sb("aT", [P, CC, TS])
        T = [psum(f"T{i}") for i in range(2)]
        SG = [psum(f"SG{i}") for i in range(2)]
        SO, MI, OG, AT = psum("SO"), psum("MI"), psum("OG"), psum("AT")
        OWN = [SO, MI]
        small_in, idx_ready, cst, own_v = sem("s_small"), sem("s_idx"), sem("s_cst"), sem("s_own")
        page_in = [sem(f"s_page{i}") for i in range(NS)]
        pt_in = sem("s_pt")
        kt_done, kt_act, kt_dve = sem("s_ktd"), sem("s_kta"), sem("s_ktv")
        q_ready, s_done, masks_done, m_ready, e_done = sem("s_q"), sem("s_s"), sem("s_mk"), sem("s_m"), sem("s_e")
        pt_done, pt_ready, o_done, om_ready, at_done, at_ready = (sem("s_ptd"), sem("s_ptr"), sem("s_od"), sem("s_om"),
                                                                  sem("s_atd"), sem("s_atr"))
        stored, masks_ready = sem("s_st"), sem("s_mkr")
        ident = K["ident"]
        i32 = ident[0:TS, 0:TS]
        block = ctx.enter_context(nc.Block())

        @block.sync
        def _(sp):
            sp.dma_start(pt[:, :], I["page_table"].to_broadcast([P, NS * NP])).then_inc(pt_in, 16)
            for dst, src in ((qT, S["qTs"]), (kT, S["kTs"]), (vs, O["v_sample"]), (ls, O["logf_sample"])):
                sp.dma_start(dst[:], src).then_inc(small_in, 16)
            sp.wait_ge(at_ready, 1)
            sp.dma_start(S["attTs"], aT[:, :, :]).then_inc(stored, 16)
            sp.wait_ge(stored, 16)

        @block.gpsimd
        def _(pool):
            pool.iota(lane[:, :], [[0, 1]], base=0, channel_multiplier=1).then_inc(cst, 1)
            pool.memset(later[:, :], 1.0).then_inc(cst, 1)
            pool.memset(later32[:, :], 1.0).then_inc(cst, 1)
            pool.memset(upto[:, :, :], 1.0).then_inc(cst, 1)
            pool.memset(hrow[:, :], 1.0).then_inc(cst, 1)
            pool.memset(hcol[:, :], 1.0).then_inc(cst, 1)
            pool.memset(ones5[:, :], 1.0).then_inc(cst, 1)
            pool.memset(Qbd[:, :, :, :, :], 0.0).then_inc(cst, 1)
            pool.wait_ge(cst, 8)
            pool.affine_select(out=later[:, :], in_=later[:, :], compare_op=ALU.is_gt, fill=0.0, base=384,
                               pattern=[[-1, 896]], channel_multiplier=1).then_inc(cst, 1)
            pool.affine_select(out=later32[:, :], in_=later32[:, :], compare_op=ALU.is_gt, fill=0.0, base=0,
                               pattern=[[-1, TS]], channel_multiplier=1).then_inc(cst, 1)
            pool.affine_select(out=upto[:, :, :], in_=upto[:, :, :], compare_op=ALU.is_ge, fill=0.0, base=0,
                               pattern=[[-QS, NS], [0, QS]], channel_multiplier=1).then_inc(cst, 1)
            pool.affine_select(out=hrow[:, :], in_=hrow[:, :], compare_op=ALU.is_equal, fill=0.0, base=0,
                               pattern=[[0, 4], [-1, H], [0, QS]], channel_multiplier=1).then_inc(cst, 1)
            pool.affine_select(out=hcol[:, :], in_=hcol[:, :], compare_op=ALU.is_equal, fill=0.0, base=0,
                               pattern=[[-1, H], [0, HD]], channel_multiplier=1).then_inc(cst, 1)
            pool.wait_ge(cst, 13)
            pool.affine_select(out=upto[:, :, :], in_=upto[:, :, :], compare_op=ALU.is_ge, fill=0.0, base=0,
                               pattern=[[QS, NS], [1, QS]], channel_multiplier=-1).then_inc(cst, 1)
            pool.wait_ge(idx_ready, 1)
            for n in range(NS * NP):
                pool.indirect_dma_start(pages[:, n, :], None, I["cache"], bass.IndirectOffsetOnAxis(idx[:, n:n + 1], 0))\
                    .then_inc(page_in[n // NP], 16)

        @block.scalar
        def _(act):
            def keys(n):
                for c in range(1, CC, 2):
                    act.wait_ge(kt_done, CC * n + c + 1)
                    if n >= 2:
                        act.wait_ge(s_done, n - 1)
                    act.activation(KT[:, n % 2, c, :], T[c % 2][:, :], ACT.Copy).then_inc(kt_act, 1)

            def soft(g):
                act.wait_ge(m_ready, g + 1)
                act.activation(Pm[:, g, 0:512], SG[g][:, :], ACT.Exp, bias=sm[:, g, 2:3], accum_out=sm[:, g, 3:4])
                act.activation(Pm[:, g, 512:], So[:, g, :], ACT.Exp, bias=sm[:, g, 2:3],
                               accum_out=sm[:, g, 4:5]).then_inc(e_done, 1)

            for n in range(NS):
                keys(n)
                if n == 4:
                    soft(0)
            soft(1)

        @block.vector
        def _(v):
            own = Own(v, own_v)
            v.wait_ge(pt_in, 16)
            v.wait_ge(cst, 8)
            own.do(v.tensor_copy(lanef[:, :], lane[:, :]))
            v.tensor_scalar(idx[:, :], pt[:, :], float(P), lanef[:, 0:1], ALU.mult, ALU.add).then_inc(idx_ready, 1)
            v.wait_ge(small_in, 64)
            for c in range(CC):
                for half in range(2):
                    r = slice(half * HD, (half + 1) * HD)
                    own.step(v.tensor_copy(Qbd[r, c, :, 2 * c + half, :],
                                           qT[r, c, :].rearrange("p (n q) -> p n q", n=NS)))
            v.wait_ge(cst, 14)
            own.step(v.tensor_copy(uptoh[:, :, :, :], upto[:, :, :].unsqueeze(2).to_broadcast([TS, NS, H, QS])))
            own.step(v.tensor_copy(eqh[:, :, :, :], i32.rearrange("p (n q) -> p n q", n=NS).unsqueeze(2)
                                   .to_broadcast([TS, NS, H, QS])))
            own.settle()
            own.do(v.tensor_tensor(L[:, :, :, :].rearrange("p n h q -> p n (h q)").rearrange("p n (h q) -> p n h q", h=H),
                                   uptoh[:, :, :, :],
                                   ls[:, :].unsqueeze(1).unsqueeze(3).to_broadcast([TS, NS, H, QS]), ALU.mult))
            v.sem_inc(q_ready, 1)

            def keys(n):
                v.wait_ge(page_in[n], 16 * NP)
                for j in range(NP):
                    own.step(v.tensor_copy(Lb[:, NP * n + j, :, :],
                                           pages[:, NP * n + j, 2 * DA:].unsqueeze(2).to_broadcast([P, H, QS])))
                own.settle()
                for c in range(0, CC, 2):
                    v.wait_ge(kt_done, CC * n + c + 1)
                    if n >= 2:
                        v.wait_ge(s_done, n - 1)
                    v.tensor_copy(KT[:, n % 2, c, :], T[c % 2][:, :]).then_inc(kt_dve, 1)

            def soft(g):
                v.wait_ge(s_done, 4 * g + 4)
                own.do(v.tensor_tensor(So[:, g, :], OWN[g][:, 0:TS], mown[:, g, :], ALU.add))
                own.step(v.tensor_reduce(sm[:, g, 0:1], SG[g][:, :], X, ALU.max))
                own.step(v.tensor_reduce(sm[:, g, 1:2], So[:, g, :], X, ALU.max))
                own.settle()
                own.do(v.tensor_tensor(sm[:, g, 5:6], sm[:, g, 0:1], sm[:, g, 1:2], ALU.max))
                v.tensor_scalar(sm[:, g, 2:3], sm[:, g, 5:6], -1.0, None, ALU.mult).then_inc(m_ready, 1)
                v.wait_ge(e_done, g + 1)
                own.do(v.tensor_tensor(sm[:, g, 6:7], sm[:, g, 3:4], sm[:, g, 4:5], ALU.add))
                own.do(v.reciprocal(sm[:, g, 7:8], sm[:, g, 6:7]))

            def weigh(g):
                v.wait_ge(pt_done, g + 1)
                own.step(v.tensor_copy(PT[:, g, :, :].rearrange("p j r -> p (j r)"), AT[:, :]))
                own.step(v.tensor_copy(PTo[:, g, :], SO[0:TS, 0:P]))
                own.settle()
                v.sem_inc(pt_ready, 1)
                v.wait_ge(o_done, g + 1)
                v.scalar_tensor_tensor(Om[:, g, :], OG[:, :], sm[:, g, 7:8], hm[:, :], ALU.mult, ALU.mult)\
                    .then_inc(om_ready, 1)

            v.wait_ge(masks_done, 1)
            own.step(v.tensor_scalar(mown[:, :, :].rearrange("p g t -> p (g t)"), MI[:, 0:2 * TS], -1.0, 1e30,
                                     ALU.add, ALU.mult))
            own.step(v.tensor_copy(selS[:, :, :].rearrange("p g t -> p (g t)"), MI[:, 2 * TS:4 * TS]))
            own.step(v.tensor_copy(hm[:, :], OG[:, :]))
            own.settle()
            v.sem_inc(masks_ready, 1)
            for n in range(NS):
                keys(n)
                if n == 4:
                    soft(0)
                if n == 5:
                    weigh(0)
            soft(1)
            weigh(1)
            v.wait_ge(at_done, 1)
            v.tensor_copy(aT[:, :, :].rearrange("p c t -> p (c t)"), AT[:, 0:CC * TS]).then_inc(at_ready, 1)

        @block.tensor
        def _(pe):
            pe.wait_ge(q_ready, 1)
            for n in range(NS):
                o = slice(32 * (n % 4), 32 * (n % 4) + 32)
                hq = lambda a: a[:, n, :, :].rearrange("p h q -> p (h q)")
                pe.matmul(MI[o, (n // 4) * TS:(n // 4 + 1) * TS], hq(uptoh), i32, start=True, stop=True)
            for n in range(NS):
                o = slice(32 * (n % 4), 32 * (n % 4) + 32)
                hq = lambda a: a[:, n, :, :].rearrange("p h q -> p (h q)")
                pe.matmul(MI[o, (2 + n // 4) * TS:(3 + n // 4) * TS], hq(eqh), i32, start=True, stop=True)
            pe.matmul(OG[:, :], hrow[:, :], hcol[:, :], start=True, stop=True).then_inc(masks_done, 1)

            def score(n):
                g, o = n // 4, slice(32 * (n % 4), 32 * (n % 4) + 32)
                hq = lambda a, m: a[:, m, :, :].rearrange("p h q -> p (h q)")
                pe.wait_ge(page_in[n], 16 * NP)
                for c in range(CC):
                    if c >= 2 or n >= 1:
                        last = 2 * n + c // 2
                        pe.wait_ge(kt_dve if c % 2 == 0 else kt_act, last)
                    for j in range(NP):
                        mm = pe.transpose(T[c % 2][:, j * P:(j + 1) * P], pages[:, NP * n + j, c * P:(c + 1) * P], ident[:, :])
                    mm.then_inc(kt_done, 1)
                pe.wait_ge(kt_dve, 2 * n + 2)
                pe.wait_ge(kt_act, 2 * n + 2)
                for c in range(CC):
                    pe.matmul(SG[g][o, :], hq(Qbd[:, c], n), KT[:, n % 2, c, :], start=(c == 0), stop=False)
                for j in range(NP):
                    pe.matmul(SG[g][o, :], hq(Lb, NP * n + j), later[:, 384 - P * j:896 - P * j], start=False, stop=False)
                pe.matmul(SG[g][o, :], hq(L, n), ones5[:, :], start=False, stop=True)
                so = OWN[g][o, 0:TS]
                for c in range(CC):
                    pe.matmul(so, hq(Qbd[:, c], n), kT[:, c, :], start=(c == 0), stop=False)
                pe.matmul(so, hq(L, n), later32[:, :], start=False, stop=True).then_inc(s_done, 1)

            def values(g):
                pe.wait_ge(e_done, g + 1)
                for j in range(NP):
                    pe.transpose(AT[:, j * P:(j + 1) * P], Pm[:, g, j * P:(j + 1) * P], ident[:, :])
                pe.transpose(SO[0:TS, 0:P], Pm[:, g, 512:], ident[:, :]).then_inc(pt_done, 1)
                pe.wait_ge(pt_ready, g + 1)
                if g:
                    pe.wait_ge(om_ready, 1)
                for n in range(4 * g, 4 * g + 4):
                    o = slice(32 * (n % 4), 32 * (n % 4) + 32)
                    for j in range(NP):
                        pe.matmul(OG[o, :], PT[:, g, j, o], pages[:, NP * n + j, DA:2 * DA], start=(j == 0), stop=False)
                    mm = pe.matmul(OG[o, :], PTo[:, g, o], vs[:, :], start=False, stop=True)
                mm.then_inc(o_done, 1)

            pe.wait_ge(masks_ready, 1)
            for n in range(NS):
                score(n)
                if n == 5:
                    values(0)
            values(1)
            pe.wait_ge(om_ready, 2)
            for c in range(CC):
                for g in range(2):
                    mm = pe.matmul(AT[:, c * TS:(c + 1) * TS], Om[:, g, c * P:(c + 1) * P], selS[:, g, :],
                                   start=(g == 0), stop=(g == 1))
            mm.then_inc(at_done, 1)


NK = 128
TOP = 16
SLOTS = H * TOP
RING = 8
DG = 4
NG = SLOTS
NG_S = NG * TS // P
S_CONV = 2 * H
S_X1 = S_CONV + 12
S_ROUTE = S_X1 + 7
S_GATE = S_ROUTE + 3
STEPS = S_GATE + H + 1
S_STATE = 4
S_KEEP = 6
PLAN = [3] * 14 + [4] * 2 + [2, 1, 1, 1, 2, 2, 1, 1, 2, 2, 2, 2] + [2, 1, 1, 1, 1, 2, 2] + [2, 2] + [5] * 7 + [6] + [2, 2]
PLAN_0 = [0] * (S_GATE + 1) + [4] + [5] * 5 + [2, 2]
LOWEST = -3.0e38
OA = 6
REST = 2 * (H - 2)
OVT = 352


def height(t):
    return TS if isinstance(t, int) and t == NB else P


def groups_of(e):
    return NG_S if isinstance(e, int) and e == NB else NG


def tail(nc, I, O, S, K):
    with ExitStack() as ctx:
        sb = lambda n, s, d=F32: ctx.enter_context(nc.sbuf_tensor(n, s, d))
        sem = lambda n: ctx.enter_context(nc.semaphore("t_" + n))
        psum = lambda n, w: ctx.enter_context(nc.psum_tensor(n, [P, w], F32))
        ring = sb("ring", [P, RING, 2 * D])
        w_o = sb("w_o", [P, DC, D])
        wq = [sb(f"wq{i}", [P, DC, 2 * NK]) for i in range(2)]
        subk = sb("subk", [P, H, 2, NK])
        V = sb("V", [P, NB, DA])
        kh = [sb(f"kh{i}", [AUG, SEQ]) for i in range(2)]
        qTb = sb("t_qT", [AUG, H, P])
        gate = [sb(f"gate{i}", [P, D]) for i in range(2)]
        h2n = sb("h2n", [P, D])
        h2c = sb("h2c", [P, D])
        xb = sb("t_xb", [P, D])
        Pm = sb("t_Pm", [P, SEQ])
        PTs = sb("t_PT", [P, SEQ])
        fT = sb("fT", [P, DC, P])
        win = sb("win", [P, CC, P + W - 1])
        yac = sb("yac", [P, CC, P])
        mask = sb("mask", [P, SEQ], BF16)
        cw = sb("cw", [P, CC, W])
        cv = sb("cv", [P, 3, CC])
        ez = sb("ez", [P, CC, P])
        stt = sb("stt", [P, 2, 8])
        mx = sb("mx", [P, 3, H])
        rl = sb("rl", [P, H])
        act8 = sb("act8", [P, RING])
        ga = sb("ga", [P, RING])
        dg = sb("dg", [P, DG, P])
        idxn = sb("idxn", [P, SLOTS], I32)
        idxc = sb("idxc", [P, SLOTS], I32)
        gn = sb("gn", [P, H, TOP])
        gc = sb("gc", [P, SLOTS])
        gs = sb("gs", [P, 2, H])
        qh = sb("qh", [P, 2, P])
        sc = sb("sc", [P, 2, NK])
        best = sb("best", [P, 2, TOP])
        bix = sb("bix", [P, 2, TOP], U32)
        cand = sb("cand", [P, 2, TOP, TOP])
        px = sb("px", [P, 3, TOP], U32)
        eq = sb("eq", [P, 2, TOP, TOP])
        sc2 = eq[:, 0, :, :].rearrange("p i j -> p (i j)").rearrange("p (g k) -> p g k", g=2)
        ss = sb("sel2", [P, 2, TOP])
        yb = sb("yb", [P, D])
        fold = sb("fold", [P, TS])
        io16 = sb("io16", [P, TOP])
        io16i = sb("io16i", [P, TOP], I32)
        top = sb("top", [P, H, TOP])
        SS, TT, YY = psum("SS", SEQ), psum("TT", SEQ), psum("YY", D)
        V0, M0 = psum("V0", 512), psum("M0", 512)

        conv_in, V_in, rest_in = sem("conv_in"), sem("V_in"), sem("rest_in")
        cst, own_v, own_a = sem("cst"), sem("own_v"), sem("own_a")
        g_in = [sem(f"g{i}") for i in range(RING)]
        quarter_copied, head_copied = sem("quarter"), sem("head")
        idx_copied, dot_done, gelu_done, diag_done, v_done = (sem("idxc"), sem("dot"), sem("gelu"), sem("diag"), sem("v"))
        carrier_v, carrier, yg_done = sem("carrier_v"), sem("carrier"), sem("yg")
        q_in, win_in, mask_in, x_in = sem("q_in"), sem("win_in"), sem("mask_in"), sem("x_in")
        k_in = [sem(f"k{i}") for i in range(2)]
        wq_in = [sem(f"wq{i}") for i in range(2)]
        smp_in, gate_in = sem("smp"), sem("gate")
        x1_kept, y_out = sem("x1_kept"), sem("y_out")
        s_done, m_ready, e_done, pt_done, pts_ready, pv_done = (sem("s"), sem("m"), sem("e"), sem("pt"), sem("pts"), sem("pv"))
        conv_done, yT_done, y_sum, nmu_ready, ssq_ready = sem("conv"), sem("yT"), sem("ysum"), sem("nmu"), sem("ssq")
        ms_ready, r0_ready, att_ready, yn_ready = sem("ms"), sem("r0"), sem("att"), sem("yn")
        attT_done, ynT_done, attT_ready, z_ready, catc_ready = sem("attT"), sem("ynT"), sem("attTr"), sem("z"), sem("catc")
        wo_done, x1_ready, ss_ready, xs_ready, x1T_done = sem("wo"), sem("x1"), sem("ss"), sem("xs"), sem("x1T")
        fT_ready, h2_done, h2_ready = sem("fTr"), sem("h2d"), sem("h2")
        qd_done, qh_ready, sc_done, sc_ready = sem("qd"), sem("qh"), sem("scd"), sem("scr")
        idx_ready, sh_ready, eg_ready, cur_ready = sem("idx"), sem("shr"), sem("eg"), sem("cur")
        sc_free, y_ready, stT_done = sem("scf"), sem("y"), sem("stT")
        ident = K["ident"]
        state = V[0:120, 0:2, :]
        ue = V[:, 2:, :].rearrange("p b n -> p (b n)")[:, 0:CC * NS * (W - 1 + QS)]\
            .rearrange("p (c n w) -> p c n w", c=CC, n=NS)
        modT, sgT = K["modT"], K["sgT"]
        block = ctx.enter_context(nc.Block())

        @block.sync
        def _(sp):
            wqv = I["w_query"].rearrange("(k p) n -> p k n", p=P)

            def load_wq(t, h):
                n = H * t + h
                if n >= 2:
                    sp.wait_ge(qd_done, n - 1)
                sp.dma_start(wq[n % 2][:, :, :], wqv[:, :, h * 2 * NK:(h + 1) * 2 * NK]).then_inc(wq_in[n % 2], 16)

            def load_k(t, h):
                n, nk = H * t + h, keys_of(t)
                if n >= 2:
                    sp.wait_ge(s_done, n - 1)
                sp.dma_start(kh[n % 2][:, 0:nk], S["kT"][:, h, 0:nk]).then_inc(k_in[n % 2], 16)

            def prefetch(t):
                nk = keys_of(t)
                if t:
                    sp.wait_ge(s_done, H * t)
                    sp.wait_ge(m_ready, H * t)
                    sp.wait_ge(conv_done, t)
                sp.dma_start(qTb[:, :, :], S["qT"][:, :, t * P:(t + 1) * P]).then_inc(q_in, 16)
                sp.dma_start(mask[:, 0:nk], S["mask"][:, SEQ - P - t * P:SEQ - P - t * P + nk]).then_inc(mask_in, 16)
                sp.dma_start(win[:, :, :], S["uT"][:, :, t * P:t * P + P + W - 1]).then_inc(win_in, 16)
                load_k(t, 0)
                load_k(t, 1)

            def load_sampled():
                sp.wait_ge(pv_done, H * NB)
                sp.dma_start(state, I["state_conv"].rearrange("n w c -> (n w) c").rearrange("(g p) c -> p g c", g=2))\
                    .then_inc(smp_in, 16)
                sp.dma_start(ue[:, :, :, W - 1:], S["uTs"].rearrange("p c (n q) -> p c n q", n=NS)).then_inc(smp_in, 16)
                sp.wait_ge(qd_done, H * NB)
                sp.dma_start(fT[:, 0:CC, 0:TS], S["attTs"]).then_inc(smp_in, 16)
                sp.wait_ge(x1_ready, NB)
                sp.dma_start(gate[0][0:TS, :], S["gate_s"][0]).then_inc(smp_in, 16)

            rest = [(xb[:, :], I["x_prompt"][0:P, :]), (gate[0][:, :], S["gate"][0])]
            rest += [(w_o[:, k, :], I["w_o"][k * P:(k + 1) * P, :]) for k in range(DC)]
            rest += [(subk[:, :, :, :], I["subkT"]), (gate[1][:, :], S["gate"][1])]
            assert len(rest) == REST

            def tail_io(t):
                r = height(t)
                if t < NB:
                    for h in range(2, H):
                        load_k(t, h)
                        if t == 0:
                            for dst, src in rest[2 * (h - 2):2 * (h - 1)]:
                                sp.dma_start(dst, src).then_inc(rest_in, 16)
                else:
                    load_sampled()
                if t:
                    sp.wait_ge(x1_kept, t)
                    sp.dma_start(xb[0:r, :], I["x_prompt"][t * P:(t + 1) * P, :] if t < NB else I["x_sample"])\
                        .then_inc(x_in, 16)
                load_wq(t, 0)
                load_wq(t, 1)
                for h in range(2, H):
                    load_wq(t, h)
                if t < NB - 1:
                    prefetch(t + 1)

            def store_y(e):
                sp.wait_ge(y_ready, e + 1)
                dst = O["y_sample"] if e == NB else O["y_prompt"][e * P:(e + 1) * P, :]
                sp.dma_start(dst, yb[0:height(e), :]).then_inc(y_out, 16)

            for dst, src in ((cw[:, :, :], I["conv_wT"]), (cv[:, :, :], I["conv_v"])):
                sp.dma_start(dst, src).then_inc(conv_in, 16)
            prefetch(0)
            sp.dma_start(V[:, :, :], O["v_prompt"].rearrange("(b p) n -> p b n", p=P)).then_inc(V_in, 16)
            tail_io(0)
            for i in range(1, NB + 1):
                tail_io(i)
                store_y(i - 1)
            sp.dma_start(gate[1][0:TS, :], S["gate_s"][1]).then_inc(gate_in, 16)
            store_y(NB)
            sp.wait_ge(y_out, 16 * (NB + 1))

        @block.gpsimd
        def _(pool):
            pool.iota(io16i[:, :], [[1, TOP]], base=0, channel_multiplier=0).then_inc(cst, 1)

            def experts(e):
                sampled_rows = isinstance(e, int) and e == NB
                half = SLOTS // 2
                if sampled_rows:
                    pool.wait_ge(quarter_copied, P // TS)
                elif some(e):
                    pool.wait_ge(idx_ready, 8 * e + 8)
                pool.sem_inc(carrier, 1)
                for k in range(groups_of(e)):
                    move = not sampled_rows and k in (0, NG // 2)
                    if not some(e) and k < NG // 2:
                        move = k % TOP == 0
                        if move:
                            pool.wait_ge(idx_ready, k // TOP + 1)
                            pool.sem_inc(carrier, 1)
                            pool.tensor_copy(idxc[:, k:k + TOP], idxn[:, k:k + TOP]).then_inc(head_copied, 1)
                            pool.wait_ge(head_copied, k // TOP + 1)
                        if k == half - TOP:
                            pool.sem_inc(idx_copied, 1)
                    elif move:
                        if not some(e):
                            pool.wait_ge(idx_ready, 8)
                            pool.sem_inc(carrier, 1)
                        o = slice(0, half) if k == 0 else slice(half, SLOTS)
                        pool.tensor_copy(idxc[:, o], idxn[:, o]).then_inc(idx_copied, 1)
                        pool.wait_ge(idx_copied, 2 * e + (1 if k == 0 else 2))
                    n = NG * e + k
                    if some(n - RING + 1):
                        pool.wait_ge(v_done, n - RING + 1)
                    if move or some(n - RING + 1):
                        pool.sem_inc(carrier, 1)
                    pool.indirect_dma_start(ring[:, k % RING, :], None, I["experts"],
                                            bass.IndirectOffsetOnAxis(idxc[:, k:k + 1], 0)).then_inc(g_in[k % RING], 16)

            experts(0)
            with pool.Fori(1, NB) as e:
                experts(e)
            experts(NB)

        @block.scalar
        def _(act):
            own = Own(act, own_a)

            def rsqrt(count, r, src, ln, out):
                act.wait_ge(ms_ready, count)
                own.do(act.activation(ln, src, ACT.Ln))
                act.activation(out, ln, ACT.Exp, scale=-0.5).then_inc(r0_ready, 1)

            def step(s, t, nk):
                r = height(t)
                smp = r == TS
                if s == 0:
                    own.start(OA * t)
                if s < 2 * H and not smp:
                    n = H * t + s // 2 + 1
                    if s % 2 == 0:
                        act.wait_ge(m_ready, n)
                        act.activation(Pm[:, 0:nk], Pm[:, 0:nk], ACT.Exp, bias=mx[:, 1, s // 2:s // 2 + 1],
                                       accum_out=mx[:, 2, s // 2:s // 2 + 1]).then_inc(e_done, 1)
                    else:
                        act.wait_ge(pt_done, n)
                        act.activation(PTs[:, 0:nk], TT[:, 0:nk], ACT.Copy).then_inc(pts_ready, 1)
                yl = PTs[0:r, 512:1024]
                if s == S_CONV + 1:
                    act.wait_ge(yT_done, t + 1)
                    act.activation(yl, M0[0:r, :], ACT.Identity, accum_out=stt[0:r, 0, 0:1]).then_inc(y_sum, 1)
                if s == S_CONV + 3:
                    act.wait_ge(nmu_ready, t + 1)
                    act.activation(PTs[0:r, 0:512], yl, ACT.Square, bias=stt[0:r, 0, 1:2],
                                   accum_out=stt[0:r, 0, 2:3]).then_inc(ssq_ready, 1)
                    if not smp:
                        act.wait_ge(attT_done, t + 1)
                        act.activation(fT[:, 0:CC, :], SS[:, 0:512].rearrange("p (c t) -> p c t", c=CC),
                                       ACT.Copy).then_inc(attT_ready, 1)
                if s == S_CONV + 5:
                    rsqrt(2 * t + 1, r, stt[0:r, 0, 3:4], stt[0:r, 0, 4:5], stt[0:r, 0, 5:6])
                if s == S_CONV + 8:
                    act.wait_ge(ynT_done, t + 1)
                    for c in range(CC):
                        own.step(act.activation(ez[:, c, 0:r], M0[:, c * P:c * P + r], ACT.Identity,
                                                scale=cv[:, 1, c:c + 1], bias=cv[:, 2, c:c + 1]))
                    own.settle()
                    act.activation(yac[:, :, 0:r], ez[:, :, 0:r], ACT.Exp, scale=-1.0).then_inc(z_ready, 1)
                if s == S_X1 + 1:
                    act.wait_ge(x1_ready, t + 1)
                    act.activation(Pm[0:r, :], xb[0:r, :], ACT.Square, accum_out=stt[0:r, 1, 2:3]).then_inc(ss_ready, 1)
                if s == S_X1 + 3:
                    rsqrt(2 * t + 2, r, stt[0:r, 1, 3:4], stt[0:r, 1, 4:5], stt[0:r, 1, 5:6])
                if s == S_X1 + 6 and not smp:
                    act.wait_ge(x1T_done, t + 1)
                    for c in range(DC):
                        a = act.activation(fT[:, c, :], SS[:, c * P:(c + 1) * P], ACT.Identity,
                                           scale=sgT[:, 1, c, 0:1], bias=modT[:, 24 + c, 0:1])
                    a.then_inc(fT_ready, 1)
                if s == S_ROUTE + 1:
                    act.wait_ge(h2_done, t + 1)
                    if some(t):
                        act.wait_ge(cur_ready, t)
                    act.activation(h2n[:, :], TT[:, :], ACT.Copy).then_inc(h2_ready, 1)
                if S_ROUTE <= s < S_ROUTE + H:
                    h = s - S_ROUTE
                    act.wait_ge(qd_done, H * t + h + 1)
                    made = M0[:, 0:2 * P].rearrange("p (g t) -> p g t", g=2)
                    if smp:
                        act.activation(qh[:, :, :].rearrange("p g (q t) -> p g q t", t=TS),
                                       made[:, :, 0:TS].unsqueeze(2).to_broadcast([P, 2, P // TS, TS]),
                                       ACT.Copy).then_inc(qh_ready, 1)
                    else:
                        act.activation(qh[:, :, :], made, ACT.Copy).then_inc(qh_ready, 1)
                if S_ROUTE + 1 <= s < S_ROUTE + 1 + H:
                    h = s - S_ROUTE - 1
                    act.wait_ge(sc_done, H * t + h + 1)
                    if some(t) or h:
                        act.wait_ge(sc_free, H * t + h)
                    act.activation(sc[:, :, :].rearrange("p g k -> p (g k)"), V0[:, 0:2 * NK],
                                   ACT.Copy).then_inc(sc_ready, 1)
                if S_GATE <= s < S_GATE + H:
                    h = s - S_GATE
                    act.wait_ge(sh_ready, H * t + h + 1)
                    act.activation(gn[:, h, :], top[:, h, :], ACT.Exp, bias=gs[:, 0, h:h + 1],
                                   accum_out=gs[:, 1, h:h + 1]).then_inc(eg_ready, 1)
                if s == STEPS - 1:
                    assert own.n == OA, own.n

            def gelu(e, k):
                act.wait_ge(dot_done, NG * e + k + 1)
                a = k % RING
                act.activation(ga[:, a:a + 1], act8[:, a:a + 1], ACT.Gelu).then_inc(gelu_done, 1)

            iterate(act, step, gelu, lambda e: None, lambda e: None, prologue=lambda: act.wait_ge(conv_in, 32))

        @block.vector
        def _(v):
            own = Own(v, own_v)
            own.carrier = carrier_v

            def newton(m, r0, a, b, out):
                own.do(v.tensor_tensor(a, r0, r0, ALU.mult))
                own.do(v.tensor_tensor(b, a, m, ALU.mult))
                own.do(v.tensor_scalar(a, b, -0.5, 1.5, ALU.mult, ALU.add))
                own.do(v.tensor_tensor(out, a, r0, ALU.mult))

            def taps(ks, r, rows_of, out_of):
                for k in ks:
                    for c in range(CC):
                        if k:
                            v.wait_ge(own.sem, own.base + own.n - CC + 1)
                            own.step(v.scalar_tensor_tensor(out_of(c), rows_of(c, k), cw[:, c, k:k + 1], out_of(c),
                                                            ALU.mult, ALU.add))
                        else:
                            own.step(v.tensor_scalar(out_of(c), rows_of(c, k), cw[:, c, 0:1], cv[:, 0, c:c + 1],
                                                     ALU.mult, ALU.add))

            def modulate(r):
                v.wait_ge(x1T_done, NB + 1)
                for c in range(DC):
                    o = fT[:, c, 0:r].rearrange("p (n q) -> p n q", n=NS)
                    i = SS[:, c * P:c * P + r].rearrange("p (n q) -> p n q", n=NS)
                    own.do(v.tensor_tensor(o, i, sgT[:, 1, c, 1:M].unsqueeze(2).to_broadcast([P, NS, QS]), ALU.mult))
                    own.do(v.tensor_tensor(o, o, modT[:, 24 + c, 1:M].unsqueeze(2).to_broadcast([P, NS, QS]), ALU.add))
                own.do(v.tensor_copy(fT[:, :, r:P].rearrange("p c (q t) -> p c q t", t=r),
                                     fT[:, :, 0:r].unsqueeze(2).to_broadcast([P, DC, P // r - 1, r])))
                v.sem_inc(fT_ready, 1)

            def choose(t, h):
                v.wait_ge(sc_ready, H * t + h + 1)
                own.carry()
                for g in range(2):
                    own.step(v.max(best[:, g, 0:8], sc[:, g, :]))
                own.settle()
                own.carry()
                for g in range(2):
                    own.step(v.max_index(bix[:, g, 0:8], best[:, g, 0:8], sc[:, g, :]))
                    own.step(v.match_replace(sc2[:, g, :], best[:, g, 0:8], sc[:, g, :], LOWEST))
                own.settle()
                v.sem_inc(sc_free, 1)
                for g in range(2):
                    own.step(v.max(best[:, g, 8:16], sc2[:, g, :]))
                own.settle()
                own.carry()
                for g in range(2):
                    own.step(v.max_index(bix[:, g, 8:16], best[:, g, 8:16], sc2[:, g, :]))
                own.do(v.tensor_tensor(cand[:, 0, :, :], best[:, 0, :].unsqueeze(2).to_broadcast([P, TOP, TOP]),
                                       best[:, 1, :].unsqueeze(1).to_broadcast([P, TOP, TOP]), ALU.add))
                c0 = cand[:, 0, :, :].rearrange("p i j -> p (i j)")
                c1 = cand[:, 1, :, :].rearrange("p i j -> p (i j)")
                own.carry()
                own.do(v.max(top[:, h, 0:8], c0))
                own.carry()
                own.step(v.max_index(px[:, 0, 0:8], top[:, h, 0:8], c0))
                own.do(v.match_replace(c1, top[:, h, 0:8], c0, LOWEST))
                own.carry()
                own.do(v.max(top[:, h, 8:16], c1))
                own.carry()
                own.do(v.max_index(px[:, 0, 8:16], top[:, h, 8:16], c1))
                own.step(v.tensor_scalar(px[:, 1, :], px[:, 0, :], 4, None, ALU.logical_shift_right))
                own.do(v.tensor_scalar(px[:, 2, :], px[:, 0, :], 15, None, ALU.bitwise_and))
                for g in range(2):
                    own.step(v.tensor_tensor(eq[:, g, :, :], px[:, 1 + g, :].unsqueeze(2).to_broadcast([P, TOP, TOP]),
                                             io16[:, :].unsqueeze(1).to_broadcast([P, TOP, TOP]), ALU.is_equal))
                own.settle()
                for g in range(2):
                    own.step(v.tensor_tensor(eq[:, g, :, :], eq[:, g, :, :],
                                             bix[:, g, :].unsqueeze(1).to_broadcast([P, TOP, TOP]), ALU.mult))
                own.settle()
                for g in range(2):
                    own.step(v.tensor_reduce(ss[:, g, :], eq[:, g, :, :], X, ALU.add))
                own.settle()
                if h == 0 and some(t):
                    v.wait_ge(idx_copied, 2 * t)
                v.tensor_scalar(gs[:, 0, h:h + 1], top[:, h, 0:1], -1.0, None, ALU.mult).then_inc(sh_ready, 1)
                v.scalar_tensor_tensor(idxn[:, h * TOP:(h + 1) * TOP], ss[:, 0, :], float(NK), ss[:, 1, :],
                                       ALU.mult, ALU.add).then_inc(idx_ready, 1)

            def step(s, t, nk):
                r = height(t)
                smp = r == TS
                if s == 0:
                    own.start(OVT * t)
                if s == S_KEEP and some(t):
                    keep_x1(t - 1)
                if smp and s == S_STATE + 1:
                    v.wait_ge(stT_done, 1)
                    for g in range(2):
                        src = (SS, TT)[g][:, 0:CC * 120].rearrange("p (c n w) -> p c n w", c=CC, n=4)
                        for c in range(CC):
                            own.step(v.tensor_copy(ue[:, c, 4 * g:4 * g + 4, 0:W - 1], src[:, c, :, :]))
                    own.settle()
                if smp and S_STATE + 2 <= s < S_CONV:
                    i, n = s - S_STATE - 2, S_CONV - S_STATE - 2
                    taps(range(W * i // n, W * (i + 1) // n), r,
                         lambda c, k: ue[:, c, :, k:k + QS],
                         lambda c: yac[:, c, 0:TS].rearrange("p (n q) -> p n q", n=NS))
                if s < 2 * H and not smp:
                    h = s // 2
                    if s == 0:
                        v.wait_ge(win_in, 16 * (t + 1))
                    if s % 2 == 0:
                        n = H * t + h + 1
                        if s == 0:
                            v.wait_ge(mask_in, 16 * (t + 1))
                        else:
                            v.wait_ge(pt_done, n - 1)
                        v.wait_ge(s_done, n)
                        own.carry()
                        own.do(v.tensor_tensor_reduce(out=Pm[:, 0:nk], in0=SS[:, 0:nk], in1=mask[:, 0:nk], scale=1.0,
                                                      scalar=LOWEST, op0=ALU.add, op1=ALU.max,
                                                      accum_out=mx[:, 0, h:h + 1]))
                        v.tensor_scalar(mx[:, 1, h:h + 1], mx[:, 0, h:h + 1], -1.0, None, ALU.mult).then_inc(m_ready, 1)
                    if s == 0 and some(t):
                        v.wait_ge(z_ready, t)
                    taps([k for k in (2 * s, 2 * s + 1) if k < W], r, lambda c, k: win[:, c, k:k + P],
                         lambda c: yac[:, c, :])
                if s == S_CONV - 1:
                    own.settle()
                    v.sem_inc(conv_done, 1)
                a = stt[0:r, 0, :]
                if s == S_CONV + 1 and not smp:
                    v.wait_ge(e_done, H * t + H)
                    own.do(v.reciprocal(rl[:, :], mx[:, 2, :]))
                    v.wait_ge(pv_done, H * t + H)
                    v.tensor_tensor(Pm[:, 0:DA].rearrange("p (h d) -> p h d", h=H),
                                    V0[:, :].rearrange("p (h d) -> p h d", h=H),
                                    rl[:, :].unsqueeze(2).to_broadcast([P, H, HD]), ALU.mult).then_inc(att_ready, 1)
                if s == S_CONV + 2:
                    v.wait_ge(y_sum, t + 1)
                    v.tensor_scalar(a[:, 1:2], a[:, 0:1], -1.0 / DA, None, ALU.mult).then_inc(nmu_ready, 1)
                if s == S_CONV + 4:
                    v.wait_ge(ssq_ready, t + 1)
                    v.tensor_scalar(a[:, 3:4], a[:, 2:3], 1.0 / DA, EPS, ALU.mult, ALU.add).then_inc(ms_ready, 1)
                if s == S_CONV + 6:
                    v.wait_ge(r0_ready, 2 * t + 1)
                    newton(a[:, 3:4], a[:, 5:6], a[:, 6:7], a[:, 7:8], a[:, 4:5])
                    v.tensor_scalar(Pm[0:r, 512:1024], PTs[0:r, 512:1024], a[:, 1:2], a[:, 4:5], ALU.add, ALU.mult)\
                        .then_inc(yn_ready, 1)
                if s == S_CONV + 9:
                    v.wait_ge(z_ready, t + 1)
                    own.do(v.tensor_scalar(yac[:, :, 0:r], yac[:, :, 0:r], 1.0, None, ALU.add))
                    own.do(v.reciprocal(yac[:, :, 0:r], yac[:, :, 0:r]))
                    v.tensor_tensor(fT[:, CC:DC, 0:r], ez[:, :, 0:r], yac[:, :, 0:r], ALU.mult).then_inc(catc_ready, 1)
                a = stt[0:r, 1, :]
                if s == S_X1:
                    v.wait_ge(wo_done, t + 1)
                    if some(t):
                        v.wait_ge(x_in, 16 * t)
                    else:
                        v.wait_ge(rest_in, 16 * REST)
                    if smp:
                        v.wait_ge(smp_in, 64)
                    own.do(v.tensor_tensor(PTs[0:r, :], TT[0:r, :], gate[0][0:r, :], ALU.mult))
                    v.tensor_tensor(xb[0:r, :], xb[0:r, :], PTs[0:r, :], ALU.add).then_inc(x1_ready, 1)
                if s == S_X1 + 2:
                    v.wait_ge(ss_ready, t + 1)
                    v.tensor_scalar(a[:, 3:4], a[:, 2:3], 1.0 / D, EPS, ALU.mult, ALU.add).then_inc(ms_ready, 1)
                if s == S_X1 + 4:
                    v.wait_ge(r0_ready, 2 * t + 2)
                    newton(a[:, 3:4], a[:, 5:6], a[:, 6:7], a[:, 7:8], a[:, 4:5])
                    v.tensor_scalar(Pm[0:r, :], xb[0:r, :], a[:, 4:5], None, ALU.mult).then_inc(xs_ready, 1)
                if s == S_X1 + 6 and smp:
                    modulate(r)
                if S_ROUTE + 2 <= s < S_ROUTE + 2 + H:
                    choose(t, s - S_ROUTE - 2)
                if S_GATE < s <= S_GATE + H:
                    h = s - S_GATE - 1
                    v.wait_ge(eg_ready, H * t + h + 1)
                    own.do(v.reciprocal(gs[:, 0, h:h + 1], gs[:, 1, h:h + 1]))
                    own.do(v.tensor_scalar(gn[:, h, :] if some(t) else gc[:, h * TOP:(h + 1) * TOP], gn[:, h, :],
                                           gs[:, 0, h:h + 1], None, ALU.mult))
                if s == S_ROUTE + 2 and not some(t):
                    v.wait_ge(h2_ready, 1)
                    v.tensor_copy(h2c[:, :], h2n[:, :]).then_inc(cur_ready, 1)
                    v.wait_ge(cur_ready, 1)
                if s == S_ROUTE + H + 2 and smp:
                    v.wait_ge(idx_ready, 8 * t + 8)
                    v.wait_ge(v_done, NG * (t - 1) + NG // 2)
                    for q in range(P // TS):
                        o = slice(q * TS, (q + 1) * TS)
                        v.tensor_copy(idxc[o, 0:NG_S], idxn[o, q * NG_S:(q + 1) * NG_S]).then_inc(quarter_copied, 1)
                if s == STEPS - 1:
                    assert smp or own.n == OVT, own.n

            def keep_x1(e):
                if some(e):
                    v.wait_ge(y_out, 16 * e)
                r = height(e)
                v.tensor_copy(yb[0:r, :], xb[0:r, :]).then_inc(x1_kept, 1)

            def begin(e):
                if not some(e):
                    return
                v.wait_ge(h2_ready, e + 1)
                flat = gn[:, :, :].rearrange("p h k -> p (h k)")
                if isinstance(e, int) and e == NB:
                    for q in range(P // TS):
                        o = slice(q * TS, (q + 1) * TS)
                        v.tensor_copy(gc[o, 0:NG_S], flat[o, q * NG_S:(q + 1) * NG_S])
                else:
                    v.tensor_copy(gc[:, :], flat)
                v.tensor_copy(h2c[:, :], h2n[:, :]).then_inc(cur_ready, 1)
                v.wait_ge(cur_ready, e + 1)

            def diag(e, k):
                n = NG * e + k
                folded = isinstance(e, int) and e == NB
                v.wait_ge(gelu_done, n + 1)
                if some(n - DG + 1):
                    v.wait_ge(v_done, n - DG + 1)
                v.tensor_scalar(dg[:, k % DG, 0:TS] if folded else dg[:, k % DG, :], fold[:, :] if folded else ident[:, :],
                                ga[:, k % RING:k % RING + 1], gc[:, k:k + 1], ALU.mult, ALU.mult).then_inc(diag_done, 1)

            def group(e, k):
                u = ring[:, k % RING, 0:D]
                v.wait_ge(g_in[k % RING], 16 * (NG // RING * e + k // RING + 1))
                v.tensor_tensor_reduce(out=u, in0=u, in1=h2c[:, :], scale=1.0, scalar=0.0, op0=ALU.mult,
                                       op1=ALU.add, accum_out=act8[:, k % RING:k % RING + 1]).then_inc(dot_done, 1)
                if k:
                    diag(e, k - 1)

            def end(e):
                r = height(e)
                diag(e, groups_of(e) - 1)
                v.wait_ge(v_done, NG * e + groups_of(e))
                if r == TS:
                    keep_x1(e)
                    v.wait_ge(gate_in, 16)
                v.tensor_tensor(PTs[0:r, :], YY[0:r, :], gate[1][0:r, :], ALU.mult).then_inc(yg_done, 1)
                v.wait_ge(x1_kept, e + 1)
                v.wait_ge(yg_done, e + 1)
                v.tensor_tensor(yb[0:r, :], PTs[0:r, :], yb[0:r, :], ALU.add).then_inc(y_ready, 1)

            def prologue():
                v.wait_ge(conv_in, 32)
                v.wait_ge(cst, 1)
                v.tensor_copy(io16[:, :], io16i[:, :]).then_inc(cst, 1)
                v.tensor_reduce(fold[:, :], ident[:, :].rearrange("p (q t) -> p t q", t=TS), X, ALU.add).then_inc(cst, 1)
                v.wait_ge(cst, 3)

            iterate(v, step, group, begin, end, prologue)

        @block.tensor
        def _(pe):
            def scores(h, t, nk):
                pe.wait_ge(k_in[h % 2], 64 * t + 16 * (h // 2 + 1))
                for b in range(0, nk, 512):
                    o = slice(b, min(b + 512, nk))
                    mm = pe.matmul(SS[:, o], qTb[:, h, :], kh[h % 2][:, o], start=True, stop=True)
                mm.then_inc(s_done, 1)

            def weigh(h, t, nk):
                n = H * t + h + 1
                if not some(t) and h == 0:
                    pe.wait_ge(V_in, 16)
                pe.wait_ge(pts_ready, n)
                for b in range(nk // P):
                    mm = pe.matmul(V0[:, h * HD:(h + 1) * HD], PTs[:, b * P:(b + 1) * P], V[:, b, h * HD:(h + 1) * HD],
                                   start=(b == 0), stop=(b == nk // P - 1))
                mm.then_inc(pv_done, 1)

            def step(s, t, nk):
                r = height(t)
                smp = r == TS
                if s == S_STATE and smp:
                    pe.wait_ge(smp_in, 64)
                    pe.wait_ge(fT_ready, t)
                    pe.wait_ge(h2_ready, t)
                    for g in range(2):
                        for c in range(CC):
                            mm = pe.transpose((SS, TT)[g][:, c * 120:(c + 1) * 120], state[:, g, c * P:(c + 1) * P],
                                              ident[0:120, 0:120])
                    mm.then_inc(stT_done, 1)
                if s < 2 * H and not smp:
                    h = s // 2
                    n = H * t + h + 1
                    if s == 0:
                        pe.wait_ge(q_in, 16 * (t + 1))
                        if some(t):
                            pe.wait_ge(fT_ready, t)
                            pe.wait_ge(sc_ready, H * t)
                        scores(0, t, nk)
                    elif s % 2 == 0:
                        weigh(h - 1, t, nk)
                    else:
                        pe.wait_ge(e_done, n)
                        if h == 0 and some(t):
                            pe.wait_ge(h2_ready, t)
                        for b in range(nk // P):
                            mm = pe.transpose(TT[:, b * P:(b + 1) * P], Pm[:, b * P:(b + 1) * P], ident[:, :])
                        mm.then_inc(pt_done, 1)
                        if h < H - 1:
                            pe.wait_ge(m_ready, n)
                            scores(h + 1, t, nk)
                if s == S_CONV:
                    if not smp:
                        weigh(H - 1, t, nk)
                    pe.wait_ge(conv_done, t + 1)
                    if some(t):
                        pe.wait_ge(qh_ready, H * t)
                    for c in range(CC):
                        mm = pe.transpose(M0[0:r, c * P:(c + 1) * P], yac[:, c, 0:r], ident[:, :])
                    mm.then_inc(yT_done, 1)
                if s == S_CONV + 2 and not smp:
                    pe.wait_ge(att_ready, t + 1)
                    for c in range(CC):
                        mm = pe.transpose(SS[:, c * P:(c + 1) * P], Pm[:, c * P:(c + 1) * P], ident[:, :])
                    mm.then_inc(attT_done, 1)
                if s in (S_CONV + 4, S_CONV + 5):
                    if not some(t):
                        pe.wait_ge(rest_in, 16 * REST)
                    if not smp:
                        pe.wait_ge(attT_ready, t + 1)
                    project_out(s - S_CONV - 4, range(CC), r)
                if s == S_CONV + 7:
                    pe.wait_ge(yn_ready, t + 1)
                    for c in range(CC):
                        mm = pe.transpose(M0[:, c * P:c * P + r], Pm[0:r, 512 + c * P:512 + (c + 1) * P], ident[0:r, 0:r])
                    mm.then_inc(ynT_done, 1)
                if s in (S_CONV + 10, S_CONV + 11):
                    pe.wait_ge(catc_ready, t + 1)
                    mm = project_out(s - S_CONV - 10, range(CC, DC), r)
                    if s == S_CONV + 11:
                        mm.then_inc(wo_done, 1)
                if s == S_X1 + 5:
                    pe.wait_ge(xs_ready, t + 1)
                    for c in range(DC):
                        mm = pe.transpose(SS[:, c * P:c * P + r], Pm[0:r, c * P:(c + 1) * P], ident[0:r, 0:r])
                    mm.then_inc(x1T_done, 1)
                if s == S_ROUTE:
                    pe.wait_ge(fT_ready, t + 1)
                    for c in range(DC):
                        mm = pe.transpose(TT[:, c * P:(c + 1) * P], fT[:, c, :], ident[:, :])
                    mm.then_inc(h2_done, 1)
                if S_ROUTE + 1 <= s < S_ROUTE + 1 + H:
                    h = s - S_ROUTE - 1
                    pe.wait_ge(qh_ready, H * t + h + 1)
                    if some(t) or h:
                        pe.wait_ge(sc_ready, H * t + h)
                    for g in range(2):
                        mm = pe.matmul(V0[:, g * NK:(g + 1) * NK], qh[:, g, :], subk[:, h, g, :], start=True, stop=True)
                    mm.then_inc(sc_done, 1)
                if S_ROUTE <= s < S_ROUTE + H:
                    h = s - S_ROUTE
                    pe.wait_ge(wq_in[h % 2], 64 * t + 16 * (h // 2 + 1))
                    for g in range(2):
                        for k in range(DC):
                            mm = pe.matmul(M0[:, g * P:g * P + r], wq[h % 2][:, k, g * NK:(g + 1) * NK], fT[:, k, 0:r],
                                           start=(k == 0), stop=(k == DC - 1))
                    mm.then_inc(qd_done, 1)

            def project_out(g, chunks, r):
                for k in chunks:
                    mm = pe.matmul(TT[0:r, g * 512:(g + 1) * 512], fT[:, k, 0:r], w_o[:, k, g * 512:(g + 1) * 512],
                                   start=(k == 0), stop=(k == DC - 1), skip_group_check=True)
                return mm

            def sums(e, k):
                w = height(e)
                pe.wait_ge(diag_done, NG * e + k + 1)
                if k == 0 and some(e):
                    pe.wait_ge(y_ready, e)
                for g in range(2):
                    mm = pe.matmul(YY[0:w, g * 512:(g + 1) * 512], dg[:, k % DG, 0:w],
                                   ring[:, k % RING, D + g * 512:D + (g + 1) * 512],
                                   start=(k == 0), stop=(k == groups_of(e) - 1), skip_group_check=True)
                mm.then_inc(v_done, 1)

            def group(e, k):
                if k:
                    sums(e, k - 1)

            iterate(pe, step, group, lambda e: None, lambda e: sums(e, groups_of(e) - 1),
                    prologue=lambda: None)


def keys_of(t):
    return P if t == 0 else SEQ // 2 if t < NB // 2 else 3 * SEQ // 4 if t < 3 * NB // 4 else SEQ


def iterate(eng, step, group, begin, end, prologue):
    def both(t, nk, done=0):
        upto = [sum(PLAN[:s]) * (NG - done) // NG for s in range(STEPS + 1)]
        begin(t - 1)
        for s in range(STEPS):
            step(s, t, nk)
            for k in range(upto[s], upto[s + 1]):
                group(t - 1, done + k)
        end(t - 1)

    assert sum(PLAN) == NG and len(PLAN) == len(PLAN_0) == STEPS
    prologue()
    for s in range(STEPS):
        step(s, 0, keys_of(0))
        for k in range(sum(PLAN_0[:s]), sum(PLAN_0[:s + 1])):
            group(0, k)
    both(1, keys_of(1), sum(PLAN_0))
    for first, end_of in ((2, NB // 2), (NB // 2, 3 * NB // 4), (3 * NB // 4, NB)):
        with eng.Fori(first, end_of) as t:
            both(t, keys_of(first))
    both(NB, 0)
    begin(NB)
    for k in range(NG_S):
        group(NB, k)
    end(NB)


def build(nc, I, O, S):
    with ExitStack() as ctx:
        K = {}
        w_in_load = ctx.enter_context(nc.semaphore("w_in_load"))
        for name, shape in (("ident", [P, P]), ("modT", [P, 48, M]), ("sgT", [P, 2, DC, M])):
            K[name] = ctx.enter_context(nc.sbuf_tensor(name, shape, F32))
        with ExitStack() as early:
            for name, shape in (("tri", [P, P]), ("ones", [P, P]), ("w_in", [P, DC, DIN])):
                K[name] = early.enter_context(nc.sbuf_tensor(name, shape, F32))
            condition(nc, I, S, K, w_in_load)
            project(nc, I, O, S, K, w_in_load)
        sampled(nc, I, O, S, K)
        tail(nc, I, O, S, K)


_OUTS = [("y_prompt", (SEQ, D)), ("y_sample", (TS, D)), ("k_prompt", (SEQ, DA)), ("v_prompt", (SEQ, DA)),
         ("logf_prompt", (SEQ, H)), ("conv_prompt", (W - 1, DA)), ("k_sample", (TS, DA)), ("v_sample", (TS, DA)),
         ("logf_sample", (TS, H)), ("conv_sample", (NS, W - 1, DA))]
_SHAPES = [(1, SEQ, D), (NS, QS, D), (1, 1, SEQ, H, HD), (1, 1, SEQ, H, HD), (1, 1, SEQ, H), (1, 1, W - 1, DA),
           (1, NS, QS, H, HD), (1, NS, QS, H, HD), (1, NS, QS, H), (1, NS, W - 1, DA)]
_SCRATCH = {"uT": (P, CC, W - 1 + SEQ), "uTs": (P, CC, TS), "qT": (AUG, H, SEQ), "kT": (AUG, H, SEQ),
            "qTs": (P, CC, TS), "kTs": (P, CC, TS), "attTs": (P, CC, TS),
            "gate": (2, P, D), "gate_s": (2, TS, D)}


def kernel(**inputs):
    import numpy as np
    import concourse.bacc as _bacc
    from concourse.bass_utils import run_bass_kernel_spmd as _run

    g = {n: np.asarray(a) for n, a in inputs.items()}
    col = lambda a: np.ascontiguousarray(a.reshape(-1, P).T)
    arrays = {
        "x_prompt": g["x_prompt"].reshape(SEQ, D), "x_sample": g["x_sample"].reshape(TS, D),
        "cT": np.concatenate([g["c_prompt"], g["c_sample"]]).reshape(M, DC, P).transpose(2, 1, 0),
        "w_ada": g["w_ada"][0], "b_adaT": col(g["b_ada"][0]),
        "norm_gT": np.stack([g["norm1_g"][0].reshape(DC, P).T, g["norm2_g"][0].reshape(DC, P).T], axis=1),
        "w_in": g["w_in"][0], "q_g": g["q_norm_g"], "k_g": g["k_norm_g"], "b_f": g["b_f"],
        "b_gluT": g["b_glu"][0].reshape(2, CC, P).transpose(2, 0, 1),
        "state_conv": g["state_conv"][0],
        "w_o": g["w_o"][0], "w_query": g["peer_w_query"][0],
        "subkT": g["peer_sub_keys"][0].transpose(3, 0, 1, 2), "conv_wT": g["conv_w"][0].reshape(W, CC, P).transpose(2, 1, 0),
        "conv_v": np.stack([g[n][0].reshape(CC, P).T for n in ("conv_b", "conv_ln_g", "conv_ln_b")], axis=1),
        "experts": np.concatenate([g["peer_u"][0], g["peer_v"][0]], axis=1),
        "cache": np.concatenate([g["cache_k"][0].reshape(-1, DA), g["cache_v"][0].reshape(-1, DA),
                                 g["cache_logf"][0].reshape(-1, H)], axis=1), "page_table": g["page_table"].reshape(1, -1),
    }
    nc = _bacc.Bacc("TRN2", target_bir_lowering=False, num_devices=1)
    feed, I = {}, {}
    for n, a in arrays.items():
        feed[f"{n}_dram"] = a = np.ascontiguousarray(a)
        I[n] = nc.dram_tensor(f"{n}_dram", a.shape, mybir.dt.from_np(a.dtype), kind="ExternalInput").ap()
    O = {n: nc.dram_tensor(f"{n}_dram_out", s, F32, kind="ExternalOutput").ap() for n, s in _OUTS}
    S = {n: nc.dram_tensor(f"{n}_scratch", s, F32, kind="Internal").ap() for n, s in _SCRATCH.items()}
    S["mask"] = nc.dram_tensor("mask_scratch", (P, 2 * SEQ - P), BF16, kind="Internal").ap()
    build(nc, I, O, S)
    r = _run(nc, [feed], core_ids=[0])
    return tuple(r.results[0][f"{n}_dram_out"].reshape(s) for (n, _), s in zip(_OUTS, _SHAPES))
```
